# Optimizing a Trainium2 kernel written in Bass

```python
import jax, jax.numpy as jnp
from jax import lax
import numpy as np

D_MODEL = 1024
BATCH = 1
SEQ = 512
DEPTH = 1

CHUNK = 64
N_META = 16
Q_BLOCK = 128
EPS = 1e-6
NEG_INF = -1e30
ROPE_BASE = 10000.0

FOX_HEADS = 8
FOX_HEAD_DIM = D_MODEL // (2 * FOX_HEADS)
FOX_WIDTH = FOX_HEADS * FOX_HEAD_DIM
MLA_HEADS = 8
MLA_NOPE_DIM = 64
MLA_ROPE_DIM = 32
MLA_V_DIM = D_MODEL // (2 * MLA_HEADS)
MLA_Q_RANK = D_MODEL // 4
MLA_KV_RANK = D_MODEL // 8
MLA_QK_DIM = MLA_NOPE_DIM + MLA_ROPE_DIM
MLA_WIDTH = MLA_HEADS * MLA_V_DIM
D_MIX = FOX_WIDTH + MLA_WIDTH

IN_SPLITS = (FOX_WIDTH, FOX_WIDTH, FOX_WIDTH, FOX_HEADS, FOX_WIDTH,
             MLA_Q_RANK, MLA_KV_RANK, MLA_ROPE_DIM, MLA_WIDTH)
D_IN = sum(IN_SPLITS)


def _rmsnorm(x, g):
    xf = x.astype(jnp.float32)
    r = lax.rsqrt(jnp.mean(xf * xf, axis=-1, keepdims=True) + EPS)
    return (xf * r * g.astype(jnp.float32)).astype(x.dtype)

def _rope(x, cos, sin):
    half = x.shape[-1] // 2
    x1, x2 = x[..., :half], x[..., half:]
    c, s = cos[None, :, None, :], sin[None, :, None, :]
    return jnp.concatenate([x1 * c - x2 * s, x1 * s + x2 * c], axis=-1)

def _chunk_id(p):
    return jnp.where(p < N_META, 0, 1 + (p - N_META) // CHUNK)

def _chunk_end(p):
    if p < N_META:
        return N_META
    return N_META + ((p - N_META) // CHUNK + 1) * CHUNK

def _block_sweep(q, k, v, scale, key_end, mask_and_bias):
    L = q.shape[1]
    outs = []
    for q0 in range(0, L, Q_BLOCK):
        kend = key_end(q0)
        s = jnp.einsum('bqhd,bkhd->bhqk', q[:, q0:q0 + Q_BLOCK], k[:, :kend]).astype(jnp.float32) * scale
        s = mask_and_bias(s, q0, kend)
        p = jax.nn.softmax(s, axis=-1).astype(v.dtype)
        outs.append(jnp.einsum('bhqk,bkhd->bqhd', p, v[:, :kend]))
    return jnp.concatenate(outs, axis=1)

def _layer(x, norm_pre, norm_post, w_in, b_f, q_norm, w_uq, kv_norm, w_ukv, w_out, cos, sin):
    B, L, _ = x.shape
    h = _rmsnorm(x, norm_pre)
    proj = h @ w_in
    (fq, fk, fv, f_logit, f_gate, c_q, c_kv, k_r, m_gate) = jnp.split(
        proj, np.cumsum(IN_SPLITS)[:-1].tolist(), axis=-1)

    fq = fq.reshape(B, L, FOX_HEADS, FOX_HEAD_DIM)
    fk = fk.reshape(B, L, FOX_HEADS, FOX_HEAD_DIM)
    fv = fv.reshape(B, L, FOX_HEADS, FOX_HEAD_DIM)
    log_f = jax.nn.log_sigmoid((f_logit + b_f).astype(jnp.float32))
    cum = jnp.cumsum(log_f, axis=1).transpose(0, 2, 1)

    def fox_mask_bias(s, q0, kend):
        qpos = q0 + jnp.arange(Q_BLOCK)
        kpos = jnp.arange(kend)
        decay = cum[:, :, q0:q0 + Q_BLOCK, None] - cum[:, :, None, :kend]
        return jnp.where(kpos[None, :] <= qpos[:, None], s + decay, NEG_INF)

    fox = _block_sweep(fq, fk, fv, FOX_HEAD_DIM ** -0.5,
                       lambda q0: q0 + Q_BLOCK, fox_mask_bias)
    fox = fox.reshape(B, L, FOX_WIDTH) * jax.nn.silu(f_gate)

    q = (_rmsnorm(c_q, q_norm) @ w_uq).reshape(B, L, MLA_HEADS, MLA_QK_DIM)
    q = jnp.concatenate([q[..., :MLA_NOPE_DIM], _rope(q[..., MLA_NOPE_DIM:], cos, sin)], axis=-1)
    kv = (_rmsnorm(c_kv, kv_norm) @ w_ukv).reshape(B, L, MLA_HEADS, MLA_NOPE_DIM + MLA_V_DIM)
    k_nope, mv = kv[..., :MLA_NOPE_DIM], kv[..., MLA_NOPE_DIM:]
    k_rope = _rope(k_r[:, :, None, :], cos, sin)
    k = jnp.concatenate([k_nope, jnp.broadcast_to(k_rope, (B, L, MLA_HEADS, MLA_ROPE_DIM))], axis=-1)

    def mla_mask(s, q0, kend):
        cq = _chunk_id(q0 + jnp.arange(Q_BLOCK))
        ck = _chunk_id(jnp.arange(kend))
        return jnp.where(ck[None, :] <= cq[:, None], s, NEG_INF)

    mla = _block_sweep(q, k, mv, MLA_QK_DIM ** -0.5,
                       lambda q0: min(L, _chunk_end(q0 + Q_BLOCK - 1)), mla_mask)
    mla = mla.reshape(B, L, MLA_WIDTH) * jax.nn.silu(m_gate)

    y = jnp.concatenate([fox, mla], axis=-1) @ w_out
    return x + _rmsnorm(y, norm_post)

def first_inputs(seed: int = 0) -> dict:
    key = jax.random.key(seed)
    ks = jax.random.split(key, 14)
    n = jax.random.normal
    f32 = jnp.float32
    return {
        "x": n(ks[0], (BATCH, SEQ, D_MODEL), f32),
        "meta": n(ks[1], (N_META, D_MODEL), f32),
        "norm_pre": 1.0 + 0.05 * n(ks[2], (DEPTH, D_MODEL), f32),
        "norm_post": 1.0 + 0.05 * n(ks[3], (DEPTH, D_MODEL), f32),
        "w_in": n(ks[4], (DEPTH, D_MODEL, D_IN), f32) * D_MODEL ** -0.5,
        "b_f": 2.0 + 0.5 * n(ks[5], (DEPTH, FOX_HEADS), f32),
        "q_norm": 1.0 + 0.05 * n(ks[6], (DEPTH, MLA_Q_RANK), f32),
        "w_uq": n(ks[7], (DEPTH, MLA_Q_RANK, MLA_HEADS * MLA_QK_DIM), f32) * MLA_Q_RANK ** -0.5,
        "kv_norm": 1.0 + 0.05 * n(ks[8], (DEPTH, MLA_KV_RANK), f32),
        "w_ukv": n(ks[9], (DEPTH, MLA_KV_RANK, MLA_HEADS * (MLA_NOPE_DIM + MLA_V_DIM)), f32) * MLA_KV_RANK ** -0.5,
        "w_out": n(ks[10], (DEPTH, D_MIX, D_MODEL), f32) * D_MIX ** -0.5,
    }

def first_block(x, meta, norm_pre, norm_post, w_in, b_f, q_norm, w_uq, kv_norm, w_ukv, w_out):
    B, S, D = x.shape
    L = S + N_META
    Lp = ((L + Q_BLOCK - 1) // Q_BLOCK) * Q_BLOCK
    h = jnp.concatenate([
        jnp.broadcast_to(meta.astype(x.dtype)[None], (B, N_META, D)),
        x,
        jnp.zeros((B, Lp - L, D), x.dtype)], axis=1)

    pos = jnp.arange(Lp, dtype=jnp.float32)
    inv_freq = ROPE_BASE ** (-jnp.arange(0, MLA_ROPE_DIM, 2, dtype=jnp.float32) / MLA_ROPE_DIM)
    ang = pos[:, None] * inv_freq[None, :]
    cos, sin = jnp.cos(ang).astype(x.dtype), jnp.sin(ang).astype(x.dtype)

    for l in range(DEPTH):
        h = _layer(h, norm_pre[l], norm_post[l], w_in[l], b_f[l], q_norm[l], w_uq[l],
                   kv_norm[l], w_ukv[l], w_out[l], cos, sin)
    return h[:, N_META:N_META + S]


CTX_LEN = 256
GRID_W = 64
D_MIX_2 = D_MODEL
HEAD_DIM = 64
ATT_HEADS = 8
ATT_KV_HEADS = 2
GQA_GROUP = ATT_HEADS // ATT_KV_HEADS
D_ATT = ATT_HEADS * HEAD_DIM
D_ATT_KV = ATT_KV_HEADS * HEAD_DIM
ATT_SCALE = HEAD_DIM ** -0.5
ROPE_THETA = 10000.0
ROPE_PAIRS = HEAD_DIM // 4
RWKV_HEADS = 8
RWKV_HEAD = 64
D_RWKV = RWKV_HEADS * RWKV_HEAD
D_DECAY_LORA = 64
D_AAA_LORA = 64
D_GATE_LORA = 128
D_RWKV_IN = 3 * D_RWKV + D_DECAY_LORA + D_AAA_LORA + D_GATE_LORA
D_IN_2 = D_ATT + 2 * D_ATT_KV + D_RWKV_IN
ATT_CUTS = (D_ATT, D_ATT + D_ATT_KV, D_ATT + 2 * D_ATT_KV)
RWKV_CUTS = (D_RWKV, 2 * D_RWKV, 3 * D_RWKV, 3 * D_RWKV + D_DECAY_LORA,
             3 * D_RWKV + D_DECAY_LORA + D_AAA_LORA)
N_EXPERTS = 16
CAPACITY_FACTOR = 2
D_EXPERT = D_MODEL
N_MOD = 6
LN_EPS = 1e-5
RMS_EPS = 1e-6
GN_EPS = 64e-5
L2_EPS = 1e-12
ALPHA = (2.0 * DEPTH) ** 0.25
BETA = (8.0 * DEPTH) ** -0.25


def layer_norm(x):
    xf = x.astype(jnp.float32)
    mu = jnp.mean(xf, -1, keepdims=True)
    var = jnp.mean(jnp.square(xf - mu), -1, keepdims=True)
    return ((xf - mu) * lax.rsqrt(var + LN_EPS)).astype(x.dtype)

def layer_norm_affine(x, g, b):
    return layer_norm(x) * g + b

def modulate(h, shift, scale):
    return h * (1.0 + scale) + shift

def to_heads(t, n):
    return t.reshape(t.shape[:-1] + (n, t.shape[-1] // n))

def head_rms_norm(t, gain):
    tf = t.astype(jnp.float32)
    return (tf * lax.rsqrt(jnp.mean(tf * tf, -1, keepdims=True) + RMS_EPS) * gain).astype(t.dtype)

def axial_rope_tables(n_tokens):
    rows = n_tokens // GRID_W
    row = jnp.repeat(jnp.arange(rows), GRID_W)
    col = jnp.tile(jnp.arange(GRID_W), rows)
    inv = ROPE_THETA ** (-jnp.arange(ROPE_PAIRS, dtype=jnp.float32) / ROPE_PAIRS)
    ang = jnp.stack([row, col], -1).astype(jnp.float32)[:, :, None] * inv
    return jnp.cos(ang), jnp.sin(ang)

def apply_axial_rope(t, cos, sin):
    B, L, H, _ = t.shape
    tf = t.astype(jnp.float32).reshape(B, L, H, 2, 2, ROPE_PAIRS)
    t1, t2 = tf[..., 0, :], tf[..., 1, :]
    cs, sn = cos[None, :, None], sin[None, :, None]
    out = jnp.stack([t1 * cs - t2 * sn, t2 * cs + t1 * sn], axis=-2)
    return out.reshape(B, L, H, HEAD_DIM).astype(t.dtype)

def gqa_attend(q, k, v):
    B, Tq = q.shape[:2]
    qg = q.reshape(B, Tq, ATT_KV_HEADS, GQA_GROUP, HEAD_DIM)
    s = jnp.einsum('bqkgd,bskd->bkgqs', qg, k).astype(jnp.float32) * ATT_SCALE
    p = jax.nn.softmax(s, axis=-1).astype(v.dtype)
    o = jnp.einsum('bkgqs,bskd->bqkgd', p, v)
    return o.reshape(B, Tq, D_ATT)

def token_shift(p, mu):
    pad = jnp.pad(p, ((0, 0), (1, 1), (0, 0)))
    return p + (0.5 * (pad[:, :-2] + pad[:, 2:]) - p) * mu

def rwkv_inputs(rw, decay_w0, decay_up, iclr_a0, iclr_up, gate_up, k_k, k_a):
    f32 = jnp.float32
    r, k, v, wl, al, gl = jnp.split(rw, RWKV_CUTS, axis=-1)
    g = jax.nn.sigmoid(gl) @ gate_up
    kk = to_heads(k * k_k, RWKV_HEADS).astype(f32)
    kk = kk / jnp.maximum(jnp.sqrt(jnp.sum(kk * kk, -1, keepdims=True)), L2_EPS)
    wt = jnp.tanh(wl)
    dirs = []
    for d in range(2):
        w = -jax.nn.softplus(-(decay_w0[d] + wt @ decay_up[d])) - 0.5
        decay = jnp.exp(-jnp.exp(to_heads(w, RWKV_HEADS).astype(f32)))
        a = jax.nn.sigmoid(iclr_a0[d] + al @ iclr_up[d])
        kd = to_heads(k * (1.0 + (a - 1.0) * k_a), RWKV_HEADS).astype(f32)
        a_h = to_heads(a, RWKV_HEADS).astype(f32)
        dirs.append((decay, kd, -kk, kk * a_h))
    r_h = to_heads(r, RWKV_HEADS).astype(f32)
    k_h = to_heads(k, RWKV_HEADS).astype(f32)
    v_h = to_heads(v, RWKV_HEADS).astype(f32)
    return r_h, k_h, v_h, g, dirs

def wkv7_scan(r, decay, k, v, a, b, s0, reverse, return_y):
    xs = tuple(jnp.moveaxis(t, 1, 0) for t in (r, decay, k, v, a, b))

    def step(s, inp):
        rt, wt, kt, vt, at, bt = inp
        sa = jnp.einsum('bhvk,bhk->bhv', s, at)
        s = s * wt[:, :, None, :] + sa[..., None] * bt[:, :, None, :] + vt[..., None] * kt[:, :, None, :]
        y = jnp.einsum('bhvk,bhk->bhv', s, rt) if return_y else None
        return s, y

    s_fin, ys = lax.scan(step, s0, xs, reverse=reverse)
    return s_fin, (jnp.moveaxis(ys, 0, 1) if return_y else None)

def rwkv_output(y, r, k, v, g, r_k, lnx_g, lnx_b):
    B, T = y.shape[:2]
    mu = jnp.mean(y, -1, keepdims=True)
    var = jnp.mean(jnp.square(y - mu), -1, keepdims=True)
    yn = ((y - mu) * lax.rsqrt(var + GN_EPS)).reshape(B, T, D_RWKV) * lnx_g + lnx_b
    bonus = (jnp.sum(r * k * r_k, -1, keepdims=True) * v).reshape(B, T, D_RWKV)
    return (yn + bonus) * g

def token_mixer(h_lat, h_ctx, w_in, q_gain, k_gain, tshift_mu, decay_w0, decay_up, iclr_a0, iclr_up,
                gate_up, k_k, k_a, r_k, lnx_g, lnx_b, w_out, with_ctx_out):
    B, L, _ = h_lat.shape
    q_l, k_l, v_l, rw_l = jnp.split(h_lat @ w_in, ATT_CUTS, axis=-1)
    q_c, k_c, v_c, rw_c = jnp.split(h_ctx @ w_in, ATT_CUTS, axis=-1)

    cos, sin = axial_rope_tables(L)
    q_l = apply_axial_rope(head_rms_norm(to_heads(q_l, ATT_HEADS), q_gain), cos, sin)
    k_l = apply_axial_rope(head_rms_norm(to_heads(k_l, ATT_KV_HEADS), k_gain), cos, sin)
    k_c = head_rms_norm(to_heads(k_c, ATT_KV_HEADS), k_gain)
    v_l = to_heads(v_l, ATT_KV_HEADS)
    v_c = to_heads(v_c, ATT_KV_HEADS)
    k_all = jnp.concatenate([k_l, k_c], axis=1)
    v_all = jnp.concatenate([v_l, v_c], axis=1)
    n_blk = L // Q_BLOCK
    q_blocks = jnp.moveaxis(q_l.reshape(B, n_blk, Q_BLOCK, ATT_HEADS, HEAD_DIM), 1, 0)
    att_l = lax.map(lambda qb: gqa_attend(qb, k_all, v_all), q_blocks)
    att_l = jnp.moveaxis(att_l, 0, 1).reshape(B, L, D_ATT)

    rwkv_p = (decay_w0, decay_up, iclr_a0, iclr_up, gate_up, k_k, k_a)
    r_c, kb_c, vr_c, g_c, dirs_c = rwkv_inputs(token_shift(rw_c, tshift_mu), *rwkv_p)
    r_l, kb_l, vr_l, g_l, dirs_l = rwkv_inputs(token_shift(rw_l, tshift_mu), *rwkv_p)
    s0 = jnp.zeros((h_ctx.shape[0], RWKV_HEADS, RWKV_HEAD, RWKV_HEAD), jnp.float32)
    y_l, y_c = None, None
    for d, reverse in enumerate((False, True)):
        dc, kc, ac, bc = dirs_c[d]
        s_c, yc = wkv7_scan(r_c, dc, kc, vr_c, ac, bc, s0, reverse, with_ctx_out)
        dl, kl, al, bl = dirs_l[d]
        _, yl = wkv7_scan(r_l, dl, kl, vr_l, al, bl, s_c, reverse, True)
        y_l = yl if y_l is None else y_l + yl
        if with_ctx_out:
            y_c = yc if y_c is None else y_c + yc
    rw_out_l = rwkv_output(y_l, r_l, kb_l, vr_l, g_l, r_k, lnx_g, lnx_b).astype(h_lat.dtype)
    out_l = jnp.concatenate([att_l, rw_out_l], axis=-1) @ w_out
    if not with_ctx_out:
        return out_l, None
    q_c = head_rms_norm(to_heads(q_c, ATT_HEADS), q_gain)
    att_c = gqa_attend(q_c, k_c, v_c)
    rw_out_c = rwkv_output(y_c, r_c, kb_c, vr_c, g_c, r_k, lnx_g, lnx_b).astype(h_ctx.dtype)
    out_c = jnp.concatenate([att_c, rw_out_c], axis=-1) @ w_out
    return out_l, out_c

def expert_choice_ffn(h, router_w, w_gate, w_up, w_down):
    B, T, D = h.shape
    cap = CAPACITY_FACTOR * T // N_EXPERTS
    logits = jnp.einsum('btd,de->bte', h, router_w).astype(jnp.float32)
    aff = jax.nn.softmax(logits, axis=-1)
    gate, idx = lax.top_k(jnp.swapaxes(aff, 1, 2), cap)
    xin = jax.vmap(lambda hb, ib: hb[ib])(h, idx)
    hid = jax.nn.silu(jnp.einsum('becd,edf->becf', xin, w_gate)) * jnp.einsum('becd,edf->becf', xin, w_up)
    y = jnp.einsum('becf,efd->becd', hid, w_down) * gate[..., None].astype(h.dtype)
    return jax.vmap(lambda ib, yb: jnp.zeros((T, D), h.dtype).at[ib.reshape(-1)].add(yb.reshape(-1, D)))(idx, y)

def second_inputs(seed: int = 0) -> dict:
    key = jax.random.key(seed)
    ks = jax.random.split(key, 32)
    f32 = jnp.float32
    nl = DEPTH

    def nrm(k, shape, s):
        return jax.random.normal(k, shape, f32) * s

    return {
        'x': nrm(ks[0], (BATCH, SEQ, D_MODEL), 1.0),
        'c': nrm(ks[1], (BATCH, D_MODEL), 1.0),
        'ctx': nrm(ks[2], (BATCH, CTX_LEN, D_MODEL), 1.0),
        'c_ctx': nrm(ks[3], (D_MODEL,), 1.0),
        'w_ada': nrm(ks[4], (nl, D_MODEL, N_MOD * D_MODEL), 0.02),
        'b_ada': nrm(ks[5], (nl, N_MOD * D_MODEL), 0.02),
        'w_in': nrm(ks[6], (nl, D_MODEL, D_IN_2), D_MODEL ** -0.5),
        'q_gain': 1.0 + nrm(ks[7], (nl, HEAD_DIM), 0.1),
        'k_gain': 1.0 + nrm(ks[8], (nl, HEAD_DIM), 0.1),
        'tshift_mu': jax.random.uniform(ks[9], (nl, D_RWKV_IN), f32),
        'decay_w0': jax.random.uniform(ks[10], (nl, 2, D_RWKV), f32, -6.0, -1.0),
        'decay_up': nrm(ks[11], (nl, 2, D_DECAY_LORA, D_RWKV), 0.1 * D_DECAY_LORA ** -0.5),
        'iclr_a0': nrm(ks[12], (nl, 2, D_RWKV), 0.5),
        'iclr_up': nrm(ks[13], (nl, 2, D_AAA_LORA, D_RWKV), D_AAA_LORA ** -0.5),
        'gate_up': nrm(ks[14], (nl, D_GATE_LORA, D_RWKV), D_GATE_LORA ** -0.5),
        'k_k': 0.85 + nrm(ks[15], (nl, D_RWKV), 0.1),
        'k_a': 1.0 + nrm(ks[16], (nl, D_RWKV), 0.1),
        'r_k': nrm(ks[17], (nl, RWKV_HEADS, RWKV_HEAD), 0.1),
        'lnx_g': 1.0 + nrm(ks[18], (nl, D_RWKV), 0.1),
        'lnx_b': nrm(ks[19], (nl, D_RWKV), 0.02),
        'w_out': nrm(ks[20], (nl, D_MIX_2, D_MODEL), BETA * D_MIX_2 ** -0.5),
        'ln1_g': 1.0 + nrm(ks[21], (nl, D_MODEL), 0.1),
        'ln1_b': nrm(ks[22], (nl, D_MODEL), 0.02),
        'router_w': nrm(ks[23], (nl, D_MODEL, N_EXPERTS), D_MODEL ** -0.5),
        'exp_w_gate': nrm(ks[24], (nl, N_EXPERTS, D_MODEL, D_EXPERT), D_MODEL ** -0.5),
        'exp_w_up': nrm(ks[25], (nl, N_EXPERTS, D_MODEL, D_EXPERT), D_MODEL ** -0.5),
        'exp_w_down': nrm(ks[26], (nl, N_EXPERTS, D_EXPERT, D_MODEL), BETA * D_EXPERT ** -0.5),
        'ln2_g': 1.0 + nrm(ks[27], (nl, D_MODEL), 0.1),
        'ln2_b': nrm(ks[28], (nl, D_MODEL), 0.02),
    }

def second_block(x, c, ctx, c_ctx, w_ada, b_ada, w_in, q_gain, k_gain, tshift_mu, decay_w0, decay_up,
              iclr_a0, iclr_up, gate_up, k_k, k_a, r_k, lnx_g, lnx_b, w_out, ln1_g, ln1_b,
              router_w, exp_w_gate, exp_w_up, exp_w_down, ln2_g, ln2_b):
    for li in range(DEPTH):
        last = li == DEPTH - 1
        mod = jax.nn.silu(c) @ w_ada[li] + b_ada[li]
        sh1, sc1, gt1, sh2, sc2, gt2 = jnp.split(mod[:, None, :], N_MOD, axis=-1)
        mc = jnp.split(jax.nn.silu(c_ctx) @ w_ada[li] + b_ada[li], N_MOD, axis=-1)
        h_lat = modulate(layer_norm(x), sh1, sc1)
        h_ctx = modulate(layer_norm(ctx), mc[0], mc[1])
        mix_l, mix_c = token_mixer(h_lat, h_ctx, w_in[li], q_gain[li], k_gain[li], tshift_mu[li],
                                   decay_w0[li], decay_up[li], iclr_a0[li], iclr_up[li], gate_up[li],
                                   k_k[li], k_a[li], r_k[li], lnx_g[li], lnx_b[li], w_out[li],
                                   not last)
        x = layer_norm_affine(ALPHA * x + gt1 * mix_l, ln1_g[li], ln1_b[li])
        h2 = modulate(layer_norm(x), sh2, sc2)
        ffn_l = expert_choice_ffn(h2, router_w[li], exp_w_gate[li], exp_w_up[li], exp_w_down[li])
        x = layer_norm_affine(ALPHA * x + gt2 * ffn_l, ln2_g[li], ln2_b[li])
        if not last:
            ctx = layer_norm_affine(ALPHA * ctx + mc[2] * mix_c, ln1_g[li], ln1_b[li])
            h2c = modulate(layer_norm(ctx), mc[3], mc[4])
            ffn_c = expert_choice_ffn(h2c, router_w[li], exp_w_gate[li], exp_w_up[li], exp_w_down[li])
            ctx = layer_norm_affine(ALPHA * ctx + mc[5] * ffn_c, ln2_g[li], ln2_b[li])
    return x


def setup_inputs(seed=0):
    out = dict(first_inputs(seed))
    for name, value in second_inputs(seed + 1).items():
        if name != "x":
            out[name + "_2"] = value
    return out


def reference(
    x, meta, norm_pre, norm_post, w_in, b_f, q_norm, w_uq, kv_norm, w_ukv, w_out, c_2, ctx_2,
    c_ctx_2, w_ada_2, b_ada_2, w_in_2, q_gain_2, k_gain_2, tshift_mu_2, decay_w0_2, decay_up_2,
    iclr_a0_2, iclr_up_2, gate_up_2, k_k_2, k_a_2, r_k_2, lnx_g_2, lnx_b_2, w_out_2, ln1_g_2,
    ln1_b_2, router_w_2, exp_w_gate_2, exp_w_up_2, exp_w_down_2, ln2_g_2, ln2_b_2,
):
    x = first_block(
        x, meta, norm_pre, norm_post, w_in, b_f, q_norm, w_uq, kv_norm, w_ukv, w_out,
    )
    return second_block(
        x, c_2, ctx_2, c_ctx_2, w_ada_2, b_ada_2, w_in_2, q_gain_2, k_gain_2, tshift_mu_2,
        decay_w0_2, decay_up_2, iclr_a0_2, iclr_up_2, gate_up_2, k_k_2, k_a_2, r_k_2, lnx_g_2,
        lnx_b_2, w_out_2, ln1_g_2, ln1_b_2, router_w_2, exp_w_gate_2, exp_w_up_2, exp_w_down_2,
        ln2_g_2, ln2_b_2,
    )


_drawn_inputs = setup_inputs


def setup_inputs(seed=0):
    import zlib

    import numpy as np

    out = dict(_drawn_inputs(seed))
    spreads = {}
    factors = {'q_norm': 4.3,
     'kv_norm': 2.828,
     'ctx_2': 4.161,
     'c_ctx_2': 3.316,
     'b_ada_2': 7.604,
     'q_gain_2': 8.0,
     'k_gain_2': 8.0,
     'decay_up_2': 8.0,
     'iclr_a0_2': 5.594,
     'iclr_up_2': 3.306,
     'k_k_2': 3.521,
     'k_a_2': 3.224,
     'lnx_g_2': 8.0,
     'lnx_b_2': 54.134,
     'ln1_b_2': 2.947,
     'ln2_b_2': 2.918}
    for name, (base, spread) in spreads.items():
        noise = np.random.default_rng([zlib.crc32(name.encode()), seed]).standard_normal(out[name].shape)
        drawn = base * np.exp(spread * noise) if base else spread * noise
        out[name] = __import__('jax').numpy.asarray(drawn.astype(out[name].dtype))
    for name, factor in factors.items():
        out[name] = (out[name] * factor).astype(out[name].dtype)
    return out
```

```python
from contextlib import ExitStack

import concourse.bass as bass
from concourse import mybir

F32 = mybir.dt.float32
ALU = mybir.AluOpType
ACT = mybir.ActivationFunctionType
AX = mybir.AxisListType.X

P = 128
D = 1024
KT = D // P
SEQ, META, CTX = 512, 16, 256
QT = SEQ // P
TOK2 = CTX + SEQ
H = 8
HD = 64
CH = 64
NOPE, ROPE, QK = 64, 32, 96
EXP, CAP = 16, 64
RING = 4
SLOT = KT * 512
BANK = 512
EPS1, LN_EPS, GN_EPS, L2_EPS = 1e-6, 1e-5, 64e-5, 1e-12
ALPHA = 2.0 ** 0.25
FOX_SCALE, MLA_SCALE, GQA_SCALE = HD ** -0.5, QK ** -0.5, HD ** -0.5
DECAY = 0.6065306597126334
NEG = -1e30

CONST = {}
_at = 0
for _name, _w in (("ident", 128), ("causal", 128), ("chunkmask", 128), ("negsel", 8 * 128), ("mcos", 80),
                  ("msin", 80), ("acos", 128), ("asin", 128), ("strict", 128), ("incl", 128),
                  ("pair0", 128), ("level", 6 * 128), ("ident2", 64), ("seg", 512), ("headsum", 32),
                  ("headspread", 512), ("slot", 64), ("blockones", 128)):
    CONST[_name] = (_at, _w)
    _at += _w
NCONST = _at
VEC = {}
_at = 0
for _name, _w in (("norm_pre", 8), ("q_norm", 2), ("kv_norm", 1), ("b_f", 1), ("cvec", 16), ("b_ada", 48),
                  ("mu", 14), ("w0", 8), ("a0", 8), ("k_k", 4), ("k_a", 4), ("r_k", 4), ("lnx_g", 4), ("lnx_b", 4)):
    VEC[_name] = (_at, _w)
    _at += _w
NVEC = _at

LOAD, PROJ1, FOX, MLAPREP, MLA, OUT1, MOD, PROJ2, GQA, RWKV, OUT2, ROUTE, GATHER, EXPERTS, FINAL = range(15)
LIVES = [
    ("const", NCONST, LOAD, FINAL), ("vec", NVEC, LOAD, FINAL), ("small", 512, LOAD, FINAL),
    ("xin", 5 * D, LOAD, LOAD), ("junk", D, LOAD, MOD), ("junk2", D, OUT2, FINAL),
    ("xT", KT * 528, LOAD, PROJ1),
    ("fqT", 4 * SEQ, PROJ1, FOX), ("fkT", 4 * 528, PROJ1, FOX), ("fv", 5 * 512, PROJ1, FOX),
    ("cum", 528, PROJ1, FOX), ("fox_cum", 528, PROJ1, PROJ1), ("fgate", 4 * 512, PROJ1, FOX), ("mgate", 4 * 512, PROJ1, MLA),
    ("cqkv", 5 * 416, PROJ1, MLAPREP), ("mixR", 4 * D, FOX, OUT1),
    ("prob", 2 * 768, FOX, GQA), ("probT", 2 * 768, FOX, GQA),
    ("cqT", 2 * 512, MLAPREP, MLAPREP), ("ckvT", 528, MLAPREP, MLAPREP), ("krT", 528, MLAPREP, MLAPREP),
    ("qrow", 4 * 768, MLAPREP, MLAPREP), ("rtmp", 2 * 512, MLAPREP, MLAPREP), ("krow", 5 * 32, MLAPREP, MLAPREP),
    ("mqT", 8 * 512, MLAPREP, MLA), ("mkT", 8 * 528, MLAPREP, MLA), ("mv", 5 * 512, MLAPREP, MLA),
    ("mixT", 8 * SEQ, OUT1, OUT1), ("xres", 4 * D, OUT1, MOD), ("norm_post", D, OUT1, OUT1),
    ("ytmp", 2 * D, OUT1, OUT1),
    ("mod", 96, MOD, FINAL), ("csil", 16, MOD, MOD), ("ctx", 2 * D, MOD, MOD), ("lnx", 6 * D, MOD, MOD),
    ("hT", KT * TOK2, MOD, PROJ2),
    ("gq", 4 * 512, PROJ2, PROJ2), ("gkv", 6 * 256, PROJ2, GQA), ("gsq", 512, PROJ2, PROJ2),
    ("gtmp", 2 * 256, PROJ2, PROJ2), ("gains", 128, PROJ2, PROJ2),
    ("gqT", 4 * 512, PROJ2, GQA), ("gkT", TOK2, PROJ2, GQA),
    ("raw", 2 * 772, PROJ2, PROJ2), ("nbr", 2 * 770, PROJ2, PROJ2),
    ("rT", 4 * SEQ, PROJ2, RWKV), ("kT", 4 * TOK2, PROJ2, RWKV), ("vT", 4 * TOK2, PROJ2, RWKV),
    ("wal", TOK2, PROJ2, RWKV), ("gl", TOK2, PROJ2, RWKV),
    ("mixG", 4 * 512, GQA, OUT2),
    ("kkT", 4 * TOK2, RWKV, RWKV), ("lora", 2 * 512, RWKV, RWKV), ("gateup", 512, RWKV, RWKV),
    
    ("yacc", 4 * 512, RWKV, RWKV), ("kkn", 2 * 768, RWKV, RWKV), ("rwT", 4 * 512, RWKV, OUT2),
] + [(f"w{i}", 512, RWKV, RWKV) for i in range(18)] + [
    ("mixT2", 4 * 512, OUT2, OUT2), ("x2", 4 * D, OUT2, FINAL), ("ln1", 2 * D, OUT2, OUT2),
    ("grow", D, OUT2, OUT2), ("ln2", 2 * D, FINAL, FINAL), ("grow2", D, ROUTE, EXPERTS),
    ("xn", 4 * D, ROUTE, GATHER), ("h2T", 8 * 512, ROUTE, ROUTE), ("router", 128, ROUTE, ROUTE),
    ("aff", 64, ROUTE, ROUTE), ("affT", 4 * 512, ROUTE, ROUTE), ("pos", 64, ROUTE, ROUTE),
    ("hot", 4 * 1024, ROUTE, GATHER), ("hotg", 1024, ROUTE, ROUTE), ("hotT", 8 * 512, ROUTE, EXPERTS),
    ("xinT", 8 * 1024, GATHER, EXPERTS),
    ("sg", 512 * 2, EXPERTS, EXPERTS), ("hid", D, EXPERTS, EXPERTS), ("hidT", 2 * 512, EXPERTS, EXPERTS),
    ("ypair", 2 * D, EXPERTS, EXPERTS),
]
MAXF = (229344 - 16512) // 4 - RING * SLOT - 64


def place():
    placed, at = [], {}
    for name, size, a, b in sorted(LIVES, key=lambda t: (-(t[3] - t[2]), -t[1])):
        off = 0
        for o, s in sorted((o, s) for o, s, pa, pb in placed if not (b < pa or pb < a)):
            if off + size <= o:
                break
            off = max(off, o + s)
        placed.append((off, size, a, b))
        at[name] = (off, size)
    top = max(o + s for o, s in at.values())
    assert top <= MAXF, (top, MAXF, sorted([(o + s, n) for n, (o, s) in at.items()])[-8:])
    return at, top


def unit_list(w):
    def cols(m, lo, n):
        return (m[:, lo:lo + n].rearrange("(k p) n -> p k n", p=P), m.shape[0] // P, n)
    w_in, w2 = w["w_in"][0], w["w_in_2"][0]
    units = [cols(w_in, lo, n) for lo, n in ((0, 512), (512, 512), (1024, 512), (1544, 512), (2056, 416),
                                             (2472, 512), (1536, 8))]
    units += [cols(w["w_uq"][0], 0, 768), cols(w["w_ukv"][0], 0, 1024)]
    units += [cols(w["w_out"][0], lo, 512) for lo in (0, 512)]
    units += [cols(w["w_ada_2"][0], lo, 512) for lo in range(0, 6 * D, 512)]
    units += [cols(w2, lo, n) for lo, n in ((0, 512), (512, 256), (768, 512), (1280, 512), (1792, 512), (2304, 256))]
    units += [cols(w["w_out_2"][0], lo, 512) for lo in (0, 512)]
    for e in range(EXP):
        for n in (0, 512):
            units += [cols(w["exp_w_gate_2"][0, e], n, 512), cols(w["exp_w_up_2"][0, e], n, 512)]
        units += [cols(w["exp_w_down_2"][0, e], n, 512) for n in (0, 512)]
    return units


JOBS = []
for _name, _n, _engines in (("fq", 4, "da"), ("fk", 4, "da"), ("fv", 5, "da"), ("fgate", 4, "a"),
                            ("cqkv", 5, "d"), ("mgate", 4, "a"), ("flog", 1, "d")):
    JOBS += [(PROJ1, _name, _i, _engines[_i % len(_engines)]) for _i in range(_n)]
JOBS += [(MLAPREP, "mq", _i, "d") for _i in range(4)]
JOBS += [(MLAPREP, "mv", _i, "a") for _i in range(5)]
JOBS += [(MLAPREP, "mk", _i, "a") for _i in range(8)]
JOBS += [(PROJ2, "gq", _i, "a") for _i in range(4)]
JOBS += [(PROJ2, "gkv", _i, "a") for _i in range(6)]
JOBS += [(PROJ2, "rw", _i, "a") for _i in range(14)]


STAGES = {
    "dve_stage": (
        "small_clear xs_var flog_ready mvar_ready cq_scaled cqT_ready ys_var hs_nmean hs_var gvar_ready "
        "kkn_ready yvar_ready yn_ready z1_nmean z1_var f_nmean f_var logits_in aff_ready rank_ready o_nmean "
        "o_var ").split(),
    "act_stage": (
        "xs_ss xs_std logf_ready mss_ready mstd_ready ys_ss ys_std c_silu hs_sum hs_ss hs_std gstd_ready "
        "kkroot ystd_ready mixT2_ready gt1_ready z1_sum z1_ss z1_std f_sum f_ss f_std gt2_ready aff_exp o_sum "
        "o_ss o_std ").split(),
    "pe_stage": (
        "cq_turned kksum_done mix2_turned gt1_rep logits_done gt2_rep aff_turned rank_turned ").split(),
}


def emptied(n):
    return JOBS[n][3], sum(j[3] == JOBS[n][3] for j in JOBS[:n + 1])


def program(nc, w, out):
    at, top = place()
    with ExitStack() as ctx:
        arena = ctx.enter_context(nc.sbuf_tensor("arena", [P, top], F32))
        ring = ctx.enter_context(nc.sbuf_tensor("ring", [P, RING, SLOT], F32))
        PS = ctx.enter_context(nc.psum_tensor("PS", [P, 8 * BANK], F32))
        x1_dram = nc.dram_tensor("x1_scratch", (P, 4 * D), F32, kind="Internal").ap()
        sems = {}

        def sem(name):
            if name not in sems:
                sems[name] = ctx.enter_context(nc.semaphore(name))
            return sems[name]

        def stage(name):
            return sem(next(k for k, v in STAGES.items() if name in v))

        def after(name):
            return stage(name), next(v.index(name) + 1 for v in STAGES.values() if name in v)

        def T(name, lo=0, n=None, p=(0, P)):
            off, size = at[name]
            assert lo + (size - lo if n is None else n) <= size, name
            return arena[p[0]:p[1], off + lo:off + (size if n is None else lo + n)]

        def C(name, lo=0, n=None, p=(0, P)):
            off, size = CONST[name]
            return T("const", off + lo, size - lo if n is None else n, p)

        def V(name, i, n=1, p=(0, P)):
            return T("vec", VEC[name][0] + i, n, p)

        small_at = [0]

        def small(n):
            small_at[0] += n
            assert small_at[0] <= 512
            return T("small", small_at[0] - n, n)

        def bank(b, lo=0, n=BANK, p=(0, P)):
            return PS[p[0]:p[1], b * BANK + lo:b * BANK + lo + n]

        def bc(ap, n):
            return ap.unsqueeze(2).broadcast_to([ap.shape[0], ap.shape[1], n])

        def rep(ap, n):
            return ap.unsqueeze(1).broadcast_to([ap.shape[0], n, ap.shape[1]])

        def unit(i):
            _, k, n = units[i]
            return ring[:, i % RING, 0:k * n].rearrange("p (k n) -> p k n", k=k)

        units = unit_list(w)
        U_IN, U_UP, U_OUT, U_ADA, U_IN2, U_OUT2, U_EXP = 0, 7, 9, 11, 23, 29, 31

        st_sum, st_nmean, st_ss, st_var, st_std, st_rstd, st_nb = (small(6) for _ in range(7))
        mx, nbias, rsum, rinv = (small(32) for _ in range(4))
        gss, gstd, grs = small(44), small(44), small(44)
        mss, mstd, mrs = small(10), small(10), small(10)
        omsc = small(32)
        wc = small(8)
        yst, yvar, ystd = small(32), small(32), small(32)
        rmx, rsm, rri = small(4), small(4), small(4)
        m8 = small(8)

        block = ctx.enter_context(nc.Block())
        phase_n = {}

        def phase_end(e):
            e.drain()
            e.sem_inc(sem("phase_left"), 1)
            phase_n[e] = phase_n.get(e, 0) + 1
            e.wait_ge(sem("phase_left"), 4 * phase_n[e])

        def chain(e, name):
            n = [0]

            def link(ins):
                n[0] += 1
                ins.then_inc(sem(name), 1)
                e.wait_ge(sem(name), n[0])
                return ins
            return link

        def unit_wait(pe, i):
            pe.wait_ge(sem(f"unit_loaded{i % RING}"), 16 * (i // RING + 1))

        @block.sync
        def _(sp):
            sp.dma_start(T("const"), w["consts"]).then_inc(sem("const_loaded"), 16)
            sp.dma_start(T("vec"), w["vecs"]).then_inc(sem("vec_loaded"), 16)
            xin = T("xin").rearrange("p (t d) -> p t d", d=D)
            sp.dma_start(xin[:, 0:4, :], w["x"][0].rearrange("(t p) d -> p t d", p=P)).then_inc(sem("x_loaded"), 16)
            sp.dma_start(xin[0:META, 4, :], w["meta"]).then_inc(sem("meta_loaded"), 16)
            for i, (src, k, n) in enumerate(units):
                if i >= RING:
                    sp.wait_ge(sem("unit_used"), i - RING + 1)
                sp.dma_start(unit(i), src).then_inc(sem(f"unit_loaded{i % RING}"), 16)

        def stats_act(act, link, tag, srcs, mean, junk, waits=None):
            for i, (src, n) in enumerate(srcs):
                if waits:
                    act.wait_ge(*waits(i))
                if mean:
                    link(act.activation(T(junk, 0, D, (0, n)), src, ACT.Identity, accum_out=st_sum[0:n, i:i + 1]))
            if mean:
                act.sem_inc(stage(f"{tag}_sum"), 1)
                act.wait_ge(*after(f"{tag}_nmean"))
            for i, (src, n) in enumerate(srcs):
                link(act.activation(T(junk, 0, D, (0, n)), src, ACT.Square,
                                    bias=st_nmean[0:n, i:i + 1] if mean else 0.0,
                                    accum_out=st_ss[0:n, i:i + 1]))
            act.sem_inc(stage(f"{tag}_ss"), 1)
            k = len(srcs)
            act.wait_ge(*after(f"{tag}_var"))
            act.activation(st_std[:, 0:k], st_var[:, 0:k], ACT.Sqrt).then_inc(stage(f"{tag}_std"), 1)

        def stats_dve(dve, link, tag, k, mean, eps):
            if mean:
                dve.wait_ge(*after(f"{tag}_sum"))
                dve.tensor_scalar(st_nmean[:, 0:k], st_sum[:, 0:k], -1.0 / D, None, ALU.mult)\
                    .then_inc(stage(f"{tag}_nmean"), 1)
            dve.wait_ge(*after(f"{tag}_ss"))
            dve.tensor_scalar(st_var[:, 0:k], st_ss[:, 0:k], 1.0 / D, eps, ALU.mult, ALU.add)\
                .then_inc(stage(f"{tag}_var"), 1)
            dve.wait_ge(*after(f"{tag}_std"))
            link(dve.reciprocal(st_rstd[:, 0:k], st_std[:, 0:k]))
            if mean:
                link(dve.tensor_tensor(st_nb[:, 0:k], st_nmean[:, 0:k], st_rstd[:, 0:k], ALU.mult))

        fqT = T("fqT").rearrange("p (m t) -> p m t", t=SEQ)
        fkT = T("fkT").rearrange("p (m t) -> p m t", t=528)
        fv = T("fv").rearrange("p (t n) -> p t n", n=512)
        mqT = T("mqT").rearrange("p (h t) -> p h t", t=SEQ)
        mkT = T("mkT").rearrange("p (h t) -> p h t", t=528)
        mv = T("mv").rearrange("p (t n) -> p t n", n=512)
        gqT = T("gqT").rearrange("p (j t) -> p j t", t=SEQ)
        gkv = T("gkv").rearrange("p (t n) -> p t n", n=256)
        mixR = T("mixR").rearrange("p (t n) -> p t n", n=D)
        mixG = T("mixG").rearrange("p (t n) -> p t n", n=512)
        prob = T("prob").rearrange("p (b n) -> p b n", b=2)
        probT = T("probT").rearrange("p (b n) -> p b n", b=2)

        def att_keys(kind, qt):
            if kind == "gqa":
                return [(b * P, P, b * P, b) for b in range(6)]
            return [(b * P, P, b * P, b) for b in range(qt + 1)] + [(SEQ, META, (qt + 1) * P, 4)]

        def att_segments(kind, qt):
            if kind == "gqa":
                return [(0, 512, 0), (512, 256, 512)]
            n = (qt + 1) * P
            return [(0, n, 0), (SEQ, META, n)]

        def att_pe(pe, kind, base):
            for i in range(32 + 2):
                if i < 32:
                    h, qt, g = i % 8, i // 8, base + i
                    q0 = qt * P
                    if g >= 2:
                        pe.wait_ge(sem("probs_ready"), g - 1)
                    score = PS[:, (g % 2) * 2 * BANK:(g % 2 + 1) * 2 * BANK]
                    for k0, n, s0 in att_segments(kind, qt):
                        o = score[:, s0:s0 + n]
                        if kind == "fox":
                            a, half = h // 2, (h % 2) * 64
                            pe.matmul(o, fqT[half:half + 64, a, q0:q0 + P], fkT[half:half + 64, a, k0:k0 + n],
                                      start=True, stop=False)
                            mm = pe.matmul(o, C("negsel", h * P, P, (0, 8)), T("cum", k0, n, (0, 8)),
                                           start=False, stop=(k0 == SEQ))
                        elif kind == "mla":
                            mm = pe.matmul(o, mqT[0:QK, h, q0:q0 + P], mkT[0:QK, h, k0:k0 + n],
                                           start=True, stop=(k0 == SEQ))
                        else:
                            half = (h // 4) * 64
                            mm = pe.matmul(o, gqT[half:half + 64, h % 4, q0:q0 + P],
                                           T("gkT", k0, n, (half, half + 64)), start=True, stop=True)
                        if kind != "gqa" and k0 == 0:
                            mm = pe.matmul(score[:, q0:q0 + P], C("ident"),
                                           C("causal" if kind == "fox" else "chunkmask"), start=False, stop=True)
                    mm.then_inc(sem("scores_ready"), 1)
                if 1 <= i < 33:
                    g = base + i - 1
                    qt = (i - 1) // 8
                    pe.wait_ge(sem("probs_ready"), g + 1)
                    if g >= 1:
                        pe.wait_ge(sem("probT_dve"), g)
                        pe.wait_ge(sem("probT_act"), g)
                    for b, (_, n, s0, _) in enumerate(att_keys(kind, qt)):
                        c = b if n == P else 4
                        mm = pe.transpose(PS[0:n, (4 * BANK) + c * P:(4 * BANK) + c * P + P],
                                          prob[:, g % 2, s0:s0 + n], C("ident"))
                    mm.then_inc(sem("probs_turned"), 1)
                if i >= 2:
                    g = base + i - 2
                    h, qt = (i - 2) % 8, (i - 2) // 8
                    pe.wait_ge(sem("probT_dve"), g + 1)
                    pe.wait_ge(sem("probT_act"), g + 1)
                    ob = 6 + (g // 8) % 2
                    if h == 0 and g >= 16:
                        pe.wait_ge(sem("heads_out"), g // 8 - 1)
                    keys = att_keys(kind, qt)
                    for b, (_, n, _, vt) in enumerate(keys):
                        c = b if n == P else 4
                        if kind == "gqa":
                            v = gkv[:, vt, 128 + (h // 4) * 64:128 + (h // 4) * 64 + 64]
                        else:
                            v = (fv if kind == "fox" else mv)[0:n, vt, h * 64:h * 64 + 64]
                        mm = pe.matmul(bank(ob, h * 64, 64), probT[0:n, g % 2, c * P:c * P + P], v,
                                       start=(b == 0), stop=(b == len(keys) - 1))
                    mm.then_inc(sem("head_done"), 1)

        def att_width(kind, qt):
            return 768 if kind == "gqa" else (qt + 1) * P + META

        def att_act(act, kind, base, scale):
            for i in range(32 + 1):
                if i < 32:
                    g, qt = base + i, i // 8
                    act.wait_ge(sem("max_ready"), g + 1)
                    if g >= 2:
                        act.wait_ge(sem("probs_turned"), g - 1)
                    n = att_width(kind, qt)
                    act.activation(prob[:, g % 2, 0:n], PS[:, (g % 2) * 1024:(g % 2) * 1024 + n], ACT.Exp,
                                   bias=nbias[:, i:i + 1], scale=scale, accum_out=rsum[:, i:i + 1])\
                        .then_inc(sem("probs_ready"), 1)
                if i >= 1:
                    g = base + i - 1
                    act.wait_ge(sem("probs_turned"), g + 1)
                    if g >= 2:
                        act.wait_ge(sem("head_done"), g - 1)
                    if kind == "gqa":
                        s, d = bank(5, 0, 256), probT[:, g % 2, 512:768]
                    else:
                        s, d = bank(5, 0, P, (0, META)), probT[0:META, g % 2, 512:512 + P]
                    act.activation(d, s, ACT.Copy).then_inc(sem("probT_act"), 1)

        def att_dve(dve, link, kind, base, scale, dest, gate):
            for i in range(32 + 2):
                if i < 32:
                    g, qt = base + i, i // 8
                    dve.wait_ge(sem("scores_ready"), g + 1)
                    link(dve.tensor_reduce(mx[:, i:i + 1],
                                           PS[:, (g % 2) * 1024:(g % 2) * 1024 + att_width(kind, qt)], AX, ALU.max))
                    dve.tensor_scalar(nbias[:, i:i + 1], mx[:, i:i + 1], -scale, None, ALU.mult)\
                        .then_inc(sem("max_ready"), 1)
                if 1 <= i < 33:
                    g, qt = base + i - 1, (i - 1) // 8
                    n = 512 if kind == "gqa" else (qt + 1) * P
                    dve.wait_ge(sem("probs_turned"), g + 1)
                    if g >= 2:
                        dve.wait_ge(sem("head_done"), g - 1)
                    dve.tensor_copy(probT[:, g % 2, 0:n], bank(4, 0, n)).then_inc(sem("probT_dve"), 1)
                if i >= 2 and (i - 2) % 8 == 7:
                    g, qt = base + i - 2, (i - 2) // 8
                    dve.wait_ge(sem("probs_ready"), g + 1)
                    link(dve.reciprocal(rinv[:, qt * 8:qt * 8 + 8], rsum[:, qt * 8:qt * 8 + 8]))
                    dve.wait_ge(sem("head_done"), g + 1)
                    o = dest[:, qt, :].rearrange("p (h n) -> p h n", n=64)
                    src = bank(6 + (g // 8) % 2).rearrange("p (h n) -> p h n", n=64)
                    ins = dve.tensor_tensor(o, src, bc(rinv[:, qt * 8:qt * 8 + 8], 64), ALU.mult)
                    ins.then_inc(sem("heads_out"), 1)
                    if gate is not None:
                        dve.wait_ge(sem("heads_out"), g // 8 + 1)
                        link(dve.tensor_tensor(dest[:, qt, :], dest[:, qt, :], gate[:, qt, :], ALU.mult))

        xT = T("xT").rearrange("p (k t) -> p k t", t=528)
        hT = T("hT").rearrange("p (k t) -> p k t", t=TOK2)
        cqT = T("cqT").rearrange("p (k t) -> p k t", t=512)
        cqkv = T("cqkv").rearrange("p (t n) -> p t n", n=416)
        UNIT_OF = {"fq": 0, "fk": 1, "fv": 2, "fgate": 3, "cqkv": 4, "mgate": 5, "flog": 6}

        def job_matmuls(pe, name, i, s):
            A, B = 2 * s, 2 * s + 1
            rows = META if i == 4 else P
            if name in ("fq", "fk", "flog"):
                u = unit(U_IN + UNIT_OF[name])
                m = 8 if name == "flog" else P
                for dst, t0, n in ((bank(A, 0, 512, (0, m)), 0, 512), (bank(B, 0, META, (0, m)), 512, META)):
                    if name == "fq" and t0:
                        continue
                    for k in range(KT):
                        mm = pe.matmul(dst, u[:, k, i * P:i * P + m], xT[:, k, t0:t0 + n],
                                       start=(k == 0), stop=(k == KT - 1))
            elif name in ("fv", "fgate", "cqkv", "mgate"):
                u = unit(U_IN + UNIT_OF[name])
                n = u.shape[2]
                for k in range(KT):
                    mm = pe.matmul(bank(A, 0, n, (0, rows)), xT[:, k, i * P:i * P + rows], u[:, k, :],
                                   start=(k == 0), stop=(k == KT - 1))
            elif name == "mq":
                u = unit(U_UP)
                for b, lo, n in ((A, 0, 512), (B, 512, 256)):
                    for k in range(2):
                        mm = pe.matmul(bank(b, 0, n), cqT[:, k, i * P:i * P + P], u[:, k, lo:lo + n],
                                       start=(k == 0), stop=(k == 1))
            elif name == "mv":
                u = unit(U_UP + 1)[:, 0, :].rearrange("p (h a n) -> p h a n", h=8, a=2)
                mm = pe.matmul(bank(A, 0, 512, (0, rows)), T("ckvT", i * P, rows), u[:, :, 1, :],
                               start=True, stop=True)
            elif name == "mk":
                u = unit(U_UP + 1)[:, 0, i * 128:i * 128 + 64]
                pe.matmul(bank(A, 0, 512, (0, 64)), u, T("ckvT", 0, 512), start=True, stop=True)
                mm = pe.matmul(bank(B, 0, META, (0, 64)), u, T("ckvT", 512, META), start=True, stop=True)
            elif name == "gq":
                for k in range(KT):
                    mm = pe.matmul(bank(A), hT[:, k, CTX + i * P:CTX + i * P + P], unit(U_IN2)[:, k, :],
                                   start=(k == 0), stop=(k == KT - 1))
            elif name == "gkv":
                for k in range(KT):
                    mm = pe.matmul(bank(A, 0, 256), hT[:, k, i * P:i * P + P], unit(U_IN2 + 1)[:, k, :],
                                   start=(k == 0), stop=(k == KT - 1))
            else:
                u = unit(U_IN2 + 2 + i // 4)
                for b, t0, n in ((A, CTX, SEQ), (B, 0, CTX)):
                    if (i < 4 or i == 13) and b == B:
                        continue
                    for k in range(KT):
                        mm = pe.matmul(bank(b, 0, n), u[:, k, (i % 4) * P:(i % 4) * P + P], hT[:, k, t0:t0 + n],
                                       start=(k == 0), stop=(k == KT - 1))
            return mm

        LAST_OF_UNIT = {("fq", 3), ("fk", 3), ("fv", 4), ("fgate", 3), ("cqkv", 4), ("mgate", 3), ("flog", 0),
                        ("mq", 3), ("mk", 7), ("gq", 3), ("gkv", 5), ("rw", 3), ("rw", 7), ("rw", 11), ("rw", 13)}
        FIRST_OF_UNIT = {("fq", 0): 0, ("fk", 0): 1, ("fv", 0): 2, ("fgate", 0): 3, ("cqkv", 0): 4, ("mgate", 0): 5,
                         ("flog", 0): 6, ("mq", 0): 7, ("mv", 0): 8, ("gq", 0): 23, ("gkv", 0): 24, ("rw", 0): 25,
                         ("rw", 4): 26, ("rw", 8): 27, ("rw", 12): 28}

        def used(pe, n):
            pe.wait_ge(sem("job_done"), n)
            pe.sem_inc(sem("unit_used"), 1)

        def jobs_pe(pe, phase, before=None):
            for n, (ph, name, i, _) in enumerate(JOBS):
                if ph != phase:
                    continue
                if (name, i) in FIRST_OF_UNIT:
                    unit_wait(pe, FIRST_OF_UNIT[(name, i)])
                if n >= 4:
                    e, c = emptied(n - 4)
                    pe.wait_ge(sem("slot_dve" if e == "d" else "slot_act"), c)
                if before:
                    before(name, i)
                job_matmuls(pe, name, i, n % 4).then_inc(sem("job_done"), 1)
                if (name, i) in LAST_OF_UNIT:
                    used(pe, n + 1)

        fgate = T("fgate").rearrange("p (t n) -> p t n", n=512)
        mgate = T("mgate").rearrange("p (t n) -> p t n", n=512)
        qrow = T("qrow").rearrange("p (t n) -> p t n", n=768)
        gq = T("gq").rearrange("p (t n) -> p t n", n=512)
        raw = T("raw").rearrange("p (b n) -> p b n", b=2)
        nbr = T("nbr").rearrange("p (b n) -> p b n", b=2)
        rT = T("rT").rearrange("p (j t) -> p j t", t=SEQ)
        kT = T("kT").rearrange("p (j t) -> p j t", t=TOK2)
        vT = T("vT").rearrange("p (j t) -> p j t", t=TOK2)
        wal, gl = T("wal"), T("gl")

        def job_empty(e, is_act, name, i, s):
            A, B = 2 * s, 2 * s + 1
            rows = META if i == 4 else P

            def copy(dst, src):
                return e.activation(dst, src, ACT.Copy) if is_act else e.tensor_copy(dst, src)
            if name == "fq":
                return copy(fqT[:, i, :], bank(A))
            if name == "fk":
                copy(fkT[:, i, 0:512], bank(A))
                return copy(fkT[:, i, 512:528], bank(B, 0, META))
            if name == "fv":
                return copy(fv[0:rows, i, :], bank(A, 0, 512, (0, rows)))
            if name in ("fgate", "mgate"):
                return e.activation((fgate if name == "fgate" else mgate)[:, i, :], bank(A), ACT.Silu)
            if name == "cqkv":
                return copy(cqkv[0:rows, i, :], bank(A, 0, 416, (0, rows)))
            if name == "flog":
                copy(T("cum", META, 512, (0, 8)), bank(A, 0, 512, (0, 8)))
                return copy(T("cum", 0, META, (0, 8)), bank(B, 0, META, (0, 8)))
            if name == "mq":
                return copy(qrow[:, i, :], PS[:, A * BANK:A * BANK + 768])
            if name == "mv":
                return copy(mv[0:rows, i, :], bank(A, 0, 512, (0, rows)))
            if name == "mk":
                copy(mkT[0:64, i, 0:512], bank(A, 0, 512, (0, 64)))
                return copy(mkT[0:64, i, 512:528], bank(B, 0, META, (0, 64)))
            if name == "gq":
                return copy(gq[:, i, :], bank(A))
            if name == "gkv":
                return copy(gkv[:, i, :], bank(A, 0, 256))
            if i >= 2:
                e.wait_ge(sem("shifted"), i - 1)
            e.wait_ge(sem("raw_clear"), 1)
            if not (i < 4 or i == 13):
                copy(raw[:, i % 2, 1:257], bank(B, 0, 256))
            return copy(raw[:, i % 2, 259:771], bank(A))

        def jobs_empty(e, which, phase, after=None):
            for n, (ph, name, i, eng) in enumerate(JOBS):
                if ph != phase or eng != which:
                    continue
                e.wait_ge(sem("job_done"), n + 1)
                job_empty(e, which == "a", name, i, n % 4).then_inc(sem("slot_dve" if which == "d" else "slot_act"), 1)
                if name == "rw":
                    e.wait_ge(sem("slot_act"), emptied(n)[1])
                    e.sem_inc(sem("raw_ready"), 1)
                if after:
                    after(name, i)

        ident = C("ident")
        xin = T("xin").rearrange("p (t d) -> p t d", d=D)
        mixT = T("mixT").rearrange("p (k t) -> p k t", t=SEQ)
        xres = T("xres").rearrange("p (t d) -> p t d", d=D)
        ytmp = T("ytmp").rearrange("p (t d) -> p t d", d=D)
        mod = T("mod").rearrange("p (c v) -> p c v", v=2)
        csil = T("csil").rearrange("p (k v) -> p k v", v=2)
        ctxr = T("ctx").rearrange("p (t d) -> p t d", d=D)
        lnx = T("lnx").rearrange("p (t d) -> p t d", d=D)
        qn = T("gsq")
        mixT2 = T("mixT2").rearrange("p (k t) -> p k t", t=SEQ)
        rwT = T("rwT").rearrange("p (k t) -> p k t", t=SEQ)
        x2 = T("x2").rearrange("p (t d) -> p t d", d=D)
        xn = T("xn").rearrange("p (t d) -> p t d", d=D)
        h2T = T("h2T").rearrange("p (k t) -> p k t", t=SEQ)
        router = T("router").rearrange("p (k e) -> p k e", e=EXP)
        aff = T("aff").rearrange("p (t e) -> p t e", e=EXP)
        pos = T("pos").rearrange("p (t e) -> p t e", e=EXP)
        hot = T("hot").rearrange("p (t c) -> p t c", c=EXP * CAP)
        hotT = T("hotT").rearrange("p (e t) -> p e t", t=SEQ)
        xinT = T("xinT").rearrange("p (k c) -> p k c", c=EXP * CAP)
        kkT = T("kkT").rearrange("p (j t) -> p j t", t=TOK2)
        kkn = T("kkn").rearrange("p (b t) -> p b t", b=2)
        yacc = T("yacc").rearrange("p (j c n) -> p j c n", j=4, n=64)
        lora = T("lora").rearrange("p (d n) -> p d n", d=2)

        W = {n: T(f"w{i}") for i, n in enumerate(
            ("sg", "a", "P", "Ei", "Ev", "Ee", "kd", "al", "bt", "kt", "rt", "X", "XT", "AT", "AakT", "ArbT",
             "ArkT", "S"))}
        W.update(M=W["P"], Z=W["Ee"], bN=W["kd"], kN=W["sg"], vN=W["Ei"], R1=W["Ev"], U=W["a"])

        def halves(name, s, q):
            return W[name][q * 64:q * 64 + 64, s * 64:s * 64 + 64]

        def step_tok(g, d):
            return 64 * (g if d == 0 else (3 - g if g < 4 else 15 - g))

        def kk_sq(j):
            off = at["w0"][0]
            assert all(at[f"w{i}"][0] == off + 512 * i for i in range(18))
            return arena[:, off + j * TOK2:off + (j + 1) * TOK2]

        def rep2(ap, n):
            return ap.unsqueeze(1).broadcast_to([ap.shape[0], n, ap.shape[1], ap.shape[2]])

        def affine_norm(dve, link, tag, gb, ready=None):
            stats_dve(dve, link, tag, 4, True, LN_EPS)
            dve.wait_ge(sem(f"{gb}_loaded"), 16)
            for t in range(4):
                link(dve.tensor_scalar(x2[:, t, :], x2[:, t, :], st_rstd[:, t:t + 1], st_nb[:, t:t + 1], ALU.mult,
                                       ALU.add))
                link(dve.tensor_tensor(x2[:, t, :], x2[:, t, :], T(gb, 0, D), ALU.mult))
                ins = dve.tensor_tensor(x2[:, t, :], x2[:, t, :], T(gb, D, D), ALU.add)
                if ready:
                    ins.then_inc(sem(ready), 1)
                else:
                    link(ins)

        def kk_sq_all(n):
            off = at["w0"][0]
            return arena[:, off:off + n]

        def rwkv_pe(pe):
            pe.wait_ge(sem("kksq_ready"), 4)
            for b, t0, n in ((0, 0, 512), (1, 512, 256)):
                for j in range(4):
                    mm = pe.matmul(bank(b, 0, n, (0, 8)), C("headsum", j * 8, 8), kk_sq(j)[:, t0:t0 + n],
                                   start=(j == 0), stop=(j == 3))
            mm.then_inc(stage("kksum_done"), 1)
            pe.wait_ge(*after("kkn_ready"))
            for j in range(4):
                if j >= 2:
                    pe.wait_ge(sem("kk_ready"), j - 1)
                for b, t0, n in ((0, 0, 512), (1, 512, 256)):
                    mm = pe.matmul(bank(2 + 2 * (j % 2) + b, 0, n), C("headspread", j * P, P, (0, 8)),
                                   kkn[0:8, 1, t0:t0 + n], start=True, stop=True)
                mm.then_inc(sem("kk_spread"), 1)
            pe.wait_ge(sem("lora_loaded"), 32)
            for g in range(12):
                lat = g >= 4
                if g == 0:
                    pe.wait_ge(sem("kk_ready"), 4)
                for d in range(2):
                    tok = step_tok(g, d)
                    for j in range(4):
                        s = d * 4 + j
                        pe.matmul(bank(0, s * 64, 64), lora[0:64, d, j * P:j * P + P], wal[0:64, tok:tok + 64],
                                  start=True, stop=True)
                        mm = pe.matmul(bank(1, s * 64, 64), lora[64:128, d, j * P:j * P + P],
                                       wal[64:128, tok:tok + 64], start=True, stop=True)
                mm.then_inc(sem("lora_done"), 1)

                def product(b, lhs, rhs):
                    for s in range(8):
                        for q in range(2):
                            mm = pe.matmul(bank(b, s * 64, 64, (q * 64, q * 64 + 64)), lhs(s, q), rhs(s, q),
                                           start=True, stop=True)
                    return mm

                def of(name):
                    return lambda s, q: halves(name, s, q)

                eye = lambda s, q: C("ident2", 0, 64, (q * 64, q * 64 + 64))
                pe.wait_ge(sem("bt_ready"), g + 1)
                pe.wait_ge(sem("s_ready"), g + 1)
                product(3, of("bt"), of("al")).then_inc(sem("ab_done"), 1)
                product(7, of("al"), of("bt")).then_inc(sem("an_done"), 1)
                pe.wait_ge(sem("kt_ready"), g + 1)
                product(4, of("kt"), of("al")).then_inc(sem("ak_done"), 1)
                if lat:
                    pe.wait_ge(sem("rt_ready"), g - 3)
                    product(5, of("bt"), of("rt")).then_inc(sem("rb_done"), 1)
                    product(6, of("kt"), of("rt")).then_inc(sem("rk_done"), 1)
                pe.wait_ge(sem("x_ready"), 6 * g + 1)
                for lv in range(1, 6):
                    pe.wait_ge(sem("m_ready"), 5 * g + lv)
                    product(0, of("M"), of("X")).then_inc(sem("z_done"), 1)
                    pe.wait_ge(sem("z_ready"), 5 * g + lv)
                    if lv < 5:
                        product(1, of("XT"), of("Z"))
                    product(2, of("Z"), of("XT")).then_inc(sem("dx_done"), 1)
                    pe.wait_ge(sem("x_ready"), 6 * g + 1 + lv)
                product(7, of("bt"), eye)
                product(0, of("kt"), eye)
                for s in range(8):
                    tok = step_tok(g, s // 4)
                    for q in range(2):
                        mm = pe.matmul(bank(1, s * 64, 64, (q * 64, q * 64 + 64)),
                                       vT[q * 64:q * 64 + 64, s % 4, tok:tok + 64],
                                       C("ident2", 0, 64, (q * 64, q * 64 + 64)), start=True, stop=True)
                mm.then_inc(sem("rows_done"), 1)
                pe.wait_ge(sem("rows_ready"), g + 1)
                pe.wait_ge(sem("akT_ready"), g + 1)

                def sums(b, pairs):
                    for s in range(8):
                        for q in range(2):
                            for n, (lhs, rhs) in enumerate(pairs):
                                mm = pe.matmul(bank(b, s * 64, 64, (q * 64, q * 64 + 64)), halves(lhs, s, q),
                                               halves(rhs, s, q), start=(n == 0), stop=(n == len(pairs) - 1))
                    return mm

                sums(2, (("al", "S"), ("AakT", "vN"))).then_inc(sem("r1_done"), 1)
                pe.wait_ge(sem("r1_ready"), g + 1)
                product(3, of("XT"), of("R1")).then_inc(sem("u_done"), 1)
                pe.wait_ge(sem("u_ready"), g + 1)
                if lat:
                    pe.wait_ge(sem("arT_ready"), g - 3)
                    sums(4, (("rt", "S"), ("ArbT", "U"), ("ArkT", "vN"))).then_inc(sem("yc_done"), 1)
                sums(5, (("bN", "U"), ("kN", "vN"))).then_inc(sem("ds_done"), 1)

            pe.wait_ge(*after("yn_ready"))
            pe.wait_ge(sem("gate_loaded"), 16)
            for j in range(4):
                if j >= 2:
                    pe.wait_ge(sem("rw_out"), j - 1)
                A = 3 * (j % 2)
                for c in range(8):
                    for q in range(2):
                        pe.matmul(bank(A, c * 64, 64, (q * 64, q * 64 + 64)),
                                  yacc[q * 64:q * 64 + 64, j, c, :], C("ident2", 0, 64, (q * 64, q * 64 + 64)),
                                  start=True, stop=True)
                pe.wait_ge(sem("rk_prod"), j + 1)
                pe.matmul(bank(A + 1), C("blockones"), W["kd" if j % 2 else "sg"], start=True, stop=True)
                pe.matmul(bank(A + 2), T("gateup", j * P, P), gl[:, 0:512], start=True, stop=True)\
                    .then_inc(sem("rw_cols"), 1)

        def experts_pe(pe):
            for e in range(EXP):
                u0 = U_EXP + 6 * e
                for n in range(2):
                    b = 2 * (e % 2) + n
                    if e >= 2:
                        pe.wait_ge(sem("hid_ready"), 2 * (e - 2) + n + 1)
                    unit_wait(pe, u0 + 2 * n)
                    unit_wait(pe, u0 + 2 * n + 1)
                    for k in range(KT):
                        x = xinT[:, k, e * CAP:(e + 1) * CAP]
                        pe.matmul(bank(b, 0, 512, (0, 64)), x, unit(u0 + 2 * n)[:, k, :],
                                  start=(k == 0), stop=(k == KT - 1))
                        mm = pe.matmul(bank(b, 0, 512, (64, 128)), x, unit(u0 + 2 * n + 1)[:, k, :],
                                       start=(k == 0), stop=(k == KT - 1))
                    mm.then_inc(sem("gu_done"), 1)
                    pe.wait_ge(sem("gu_done"), 2 * e + n + 1)
                    pe.sem_inc(sem("unit_used"), 2)
                if e >= 1:
                    pe.wait_ge(sem("hidT_ready"), e)
                hid = T("hid", 0, D, (64, 128))
                for f in range(8):
                    if f % 4 == 0:
                        pe.wait_ge(sem("hid_ready"), 2 * e + f // 4 + 1)
                    mm = pe.matmul(bank(4, f * 64, 64), hid[:, f * P:f * P + P], C("ident2", 0, 64, (64, 128)),
                                   start=True, stop=True)
                mm.then_inc(sem("hid_turned"), 1)
                pe.wait_ge(sem("hidT_ready"), e + 1)
                if e >= 1:
                    pe.wait_ge(sem("y_left"), e)
                unit_wait(pe, u0 + 4)
                unit_wait(pe, u0 + 5)
                hidT = T("hidT", (e % 2) * 512, 512).rearrange("p (f c) -> p f c", c=64)
                for f in range(8):
                    pe.matmul(bank(5, 0, 512, (0, 64)), hidT[:, f, :], unit(u0 + 4)[:, f, :],
                              start=(f == 0), stop=(f == 7))
                    mm = pe.matmul(bank(5, 0, 512, (64, 128)), hidT[:, f, :], unit(u0 + 5)[:, f, :],
                                   start=(f == 0), stop=(f == 7))
                mm.then_inc(sem("down_done"), 1)
                pe.wait_ge(sem("down_done"), e + 1)
                pe.sem_inc(sem("unit_used"), 2)
                if e % 2:
                    p2 = e // 2
                    pe.wait_ge(sem("y_left"), e + 1)
                    yp = T("ypair", (p2 % 2) * D, D)
                    for t in range(4):
                        for n in range(2):
                            i = p2 * 8 + t * 2 + n
                            if i >= 2:
                                pe.wait_ge(sem("added"), i - 1)
                            pe.matmul(bank(6 + i % 2), hotT[:, p2, t * P:t * P + P], yp[:, n * 512:n * 512 + 512],
                                      start=True, stop=True).then_inc(sem("scattered"), 1)

        def rwkv_dve(dve, link):
            kk_k = VEC["k_k"][0]
            for j in range(4):
                link(dve.tensor_scalar(kkT[:, j, :], kT[:, j, :], T("vec", kk_k + j, 1), None, ALU.mult))
                dve.tensor_tensor(kk_sq(j), kkT[:, j, :], kkT[:, j, :], ALU.mult).then_inc(sem("kksq_ready"), 1)
            dve.wait_ge(*after("kkroot"))
            link(dve.tensor_scalar(kkn[0:8, 0, :], kkn[0:8, 0, :], L2_EPS, None, ALU.max))
            dve.reciprocal(kkn[0:8, 1, :], kkn[0:8, 0, :]).then_inc(stage("kkn_ready"), 1)
            for j in range(4):
                dve.wait_ge(sem("kk_spread"), j + 1)
                A = (2 + 2 * (j % 2)) * BANK
                dve.tensor_tensor(kkT[:, j, :], kkT[:, j, :], PS[:, A:A + 768], ALU.mult).then_inc(sem("kk_ready"), 1)
            dve.wait_ge(sem("kk_ready"), 4)
            dve.memset(T("yacc"), 0.0)
            dve.memset(W["S"], 0.0).then_inc(sem("s_ready"), 1)

            def by(ap, d):
                return ap[:, d * 256:d * 256 + 256].rearrange("p (j n) -> p j n", n=64)

            def mask(name, d, i=0):
                return rep(C(name, i * 128 + d * 64, 64), 4)

            for g in range(12):
                lat = g >= 4
                dve.wait_ge(sem("lora_done"), g + 1)
                dve.tensor_tensor(W["sg"].rearrange("p (s n) -> p s n", n=64),
                                  bank(0).rearrange("p (s n) -> p s n", n=64), bc(T("vec", VEC["w0"][0], 8), 64),
                                  ALU.add)
                dve.tensor_tensor(W["a"].rearrange("p (s n) -> p s n", n=64),
                                  bank(1).rearrange("p (s n) -> p s n", n=64), bc(T("vec", VEC["a0"][0], 8), 64),
                                  ALU.add).then_inc(sem("z_in"), 1)
                dve.wait_ge(sem("tanh_done"), g + 1)
                link(dve.tensor_scalar(W["sg"], W["sg"], 0.5, 0.5, ALU.mult, ALU.add))
                dve.tensor_scalar(W["a"], W["a"], 0.5, 0.5, ALU.mult, ALU.add).then_inc(sem("a_ready"), 1)
                dve.tensor_tensor_scan(W["P"][:, 0:256], C("seg", 0, 256), W["sg"][:, 0:256], 0.0, ALU.mult, ALU.add)
                dve.tensor_tensor_scan(W["P"][:, 256:512][:, ::-1], C("seg", 256, 256)[:, ::-1],
                                       W["sg"][:, 256:512][:, ::-1], 0.0, ALU.mult, ALU.add)\
                    .then_inc(sem("p_ready"), 1)
                dve.wait_ge(sem("p_ready"), g + 1)
                dve.tensor_tensor(W["Ee"], W["P"], W["sg"], ALU.subtract).then_inc(sem("ex_ready"), 1)
                dve.wait_ge(sem("e_ready"), g + 1)
                for d in range(2):
                    tok = step_tok(g, d)
                    dve.scalar_tensor_tensor(out=by(W["al"], d), in0=kkT[:, :, tok:tok + 64], scalar=-1.0,
                                             in1=by(W["Ee"], d), op0=ALU.mult, op1=ALU.mult)
                dve.wait_ge(sem("b_ready"), g + 1)
                dve.tensor_tensor(W["bt"], W["bt"], W["Ev"], ALU.mult).then_inc(sem("bt_ready"), 1)
                dve.wait_ge(sem("kd_ready"), g + 1)
                dve.tensor_tensor(W["kt"], W["kd"], W["Ev"], ALU.mult).then_inc(sem("kt_ready"), 1)
                for d in range(2):
                    ins = dve.tensor_copy(wc[:, 4 * d:4 * d + 4], by(W["Ei"], d)[:, :, 63 if d == 0 else 0])
                ins.then_inc(sem("wc_ready"), 1)
                if lat:
                    for d in range(2):
                        tok = step_tok(g, d) - CTX
                        ins = dve.tensor_tensor(by(W["rt"], d), rT[:, :, tok:tok + 64], by(W["Ei"], d), ALU.mult)
                    ins.then_inc(sem("rt_ready"), 1)
                dve.wait_ge(sem("at_ready"), g + 1)
                dve.wait_ge(sem("an_done"), g + 1)
                for d in range(2):
                    dve.tensor_tensor(by(W["XT"], d), by(W["AT"], d), mask("level", d), ALU.mult)
                    ins = dve.tensor_tensor(by(W["X"], d), by(bank(7), d), mask("pair0", d), ALU.mult)
                link(ins)
                eye = rep(C("ident2"), 8)
                dve.tensor_tensor(W["XT"].rearrange("p (s n) -> p s n", n=64),
                                  W["XT"].rearrange("p (s n) -> p s n", n=64), eye, ALU.add)
                dve.tensor_tensor(W["X"].rearrange("p (s n) -> p s n", n=64),
                                  W["X"].rearrange("p (s n) -> p s n", n=64), eye, ALU.add).then_inc(sem("x_ready"), 1)
                dve.wait_ge(sem("ak_done"), g + 1)
                for d in range(2):
                    ins = dve.tensor_tensor(by(W["AakT"], d), by(bank(4), d), mask("strict", d), ALU.mult)
                ins.then_inc(sem("akT_ready"), 1)
                if lat:
                    dve.wait_ge(sem("rk_done"), g - 3)
                    for d in range(2):
                        dve.tensor_tensor(by(W["ArbT"], d), by(bank(5), d), mask("incl", d), ALU.mult)
                        ins = dve.tensor_tensor(by(W["ArkT"], d), by(bank(6), d), mask("incl", d), ALU.mult)
                    ins.then_inc(sem("arT_ready"), 1)
                for lv in range(1, 6):
                    dve.wait_ge(sem("dx_done"), 5 * g + lv)
                    dve.wait_ge(sem("x_ready"), 6 * g + lv)
                    if lv < 5:
                        dve.tensor_tensor(W["X"], W["X"], bank(1), ALU.add)
                    dve.tensor_tensor(W["XT"], W["XT"], bank(2), ALU.add).then_inc(sem("x_ready"), 1)
                if lat:
                    dve.wait_ge(sem("yc_done"), g - 3)
                    for d in range(2):
                        c = (step_tok(g, d) - CTX) // 64
                        ins = dve.tensor_tensor(yacc[:, :, c, :], yacc[:, :, c, :], by(bank(4), d), ALU.add)
                        link(ins)
                dve.wait_ge(sem("ds_done"), g + 1)
                link(dve.tensor_tensor(W["S"], W["S"], bank(5), ALU.add))
                s3 = W["S"].rearrange("p (s n) -> p s n", n=64)
                dve.tensor_tensor(s3, s3, bc(wc, 64), ALU.mult).then_inc(sem("s_ready"), 1)
                dve.wait_ge(sem("s_ready"), g + 2)
            y3 = T("yacc").rearrange("p (s n) -> p s n", n=64)
            link(dve.tensor_reduce(yst, y3, AX, ALU.add))
            link(dve.tensor_scalar(yst, yst, -1.0 / 64, None, ALU.mult))
            link(dve.tensor_tensor(y3, y3, bc(yst, 64), ALU.add))
            sq = kk_sq_all(2048)
            link(dve.tensor_tensor(sq, T("yacc"), T("yacc"), ALU.mult))
            link(dve.tensor_reduce(yvar, sq.rearrange("p (s n) -> p s n", n=64), AX, ALU.add))
            dve.tensor_scalar(yvar, yvar, 1.0 / 64, GN_EPS, ALU.mult, ALU.add).then_inc(stage("yvar_ready"), 1)
            dve.wait_ge(*after("ystd_ready"))
            link(dve.reciprocal(yst, ystd))
            dve.tensor_tensor(y3, y3, bc(yst, 64), ALU.mult).then_inc(stage("yn_ready"), 1)
            for j in range(4):
                buf = W["kd" if j % 2 else "sg"]
                if j >= 2:
                    dve.wait_ge(sem("rw_cols"), j - 1)
                dve.scalar_tensor_tensor(out=buf, in0=rT[:, j, :], scalar=T("vec", VEC["r_k"][0] + j, 1),
                                         in1=kT[:, j, CTX:TOK2], op0=ALU.mult, op1=ALU.mult)\
                    .then_inc(sem("rk_prod"), 1)
                A = 3 * (j % 2)
                dve.wait_ge(sem("rw_cols"), j + 1)
                link(dve.tensor_tensor(W["al"], vT[:, j, CTX:TOK2], bank(A + 1), ALU.mult))
                dve.wait_ge(sem("yn_affine"), j + 1)
                link(dve.tensor_tensor(rwT[:, j, :], rwT[:, j, :], W["al"], ALU.add))
                dve.tensor_tensor(rwT[:, j, :], rwT[:, j, :], bank(A + 2), ALU.mult).then_inc(sem("rw_out"), 1)


        @block.tensor
        def _(pe):
            pe.wait_ge(sem("const_loaded"), 16)
            for t in range(5):
                pe.wait_ge(sem("x_scaled"), t + 1)
            for k in range(KT):
                if k >= 4:
                    pe.wait_ge(sem("xT_dve" if k % 2 == 0 else "xT_act"), (k - 4) // 2 + 1)
                A = 2 * (k % 4)
                for t in range(4):
                    pe.transpose(bank(A, t * P, P), xin[:, t, k * P:k * P + P], ident)
                pe.transpose(bank(A + 1, 0, META), xin[0:META, 4, k * P:k * P + P], ident[0:META, 0:META])\
                    .then_inc(sem("x_turned"), 1)
            phase_end(pe)
            jobs_pe(pe, PROJ1)
            phase_end(pe)
            att_pe(pe, "fox", 0)
            phase_end(pe)

            pe.wait_ge(*after("cq_scaled"))
            for k in range(2):
                for t in range(4):
                    pe.transpose(bank(k, t * P, P), cqkv[:, t, k * P:k * P + P], ident)
            krow = T("krow").rearrange("p (t n) -> p t n", n=32)
            for t in range(5):
                n = META if t == 4 else P
                b, c = (1, 0) if t == 4 else (0, t * P)
                pe.transpose(bank(2 + b, c, n), cqkv[0:n, t, 256:384], ident[0:n, 0:n])
                mm = pe.transpose(bank(4 + b, c, n, (0, 32)), krow[0:n, t, :], ident[0:n, 0:n])
            mm.then_inc(stage("cq_turned"), 1)
            pe.wait_ge(*after("cqT_ready"))
            jobs_pe(pe, MLAPREP)
            n0 = [n for n, j in enumerate(JOBS) if j[0] == MLAPREP]
            for n in n0[-4:]:
                e, c = emptied(n)
                pe.wait_ge(sem("slot_dve" if e == "d" else "slot_act"), c)
            pe.wait_ge(sem("q_roped"), 4)
            for h in range(H):
                for t in range(4):
                    mm = pe.transpose(bank(h, t * P, P, (0, QK)), qrow[:, t, h * QK:h * QK + QK], ident)
                mm.then_inc(sem("q_turned"), 1)
            phase_end(pe)
            att_pe(pe, "mla", 32)
            phase_end(pe)

            for k in range(8):
                for t in range(4):
                    mm = pe.transpose(bank(k, t * P, P), mixR[:, t, k * P:k * P + P], ident)
                mm.then_inc(sem("mix_turned"), 1)
            pe.wait_ge(sem("mixT_dve"), 4)
            pe.wait_ge(sem("mixT_act"), 4)
            for n in range(2):
                unit_wait(pe, U_OUT + n)
                for t in range(4):
                    for k in range(KT):
                        mm = pe.matmul(bank(2 * t + n), mixT[:, k, t * P:t * P + P], unit(U_OUT + n)[:, k, :],
                                       start=(k == 0), stop=(k == KT - 1))
                mm.then_inc(sem("y_done"), 1)
                pe.wait_ge(sem("y_done"), n + 1)
                pe.sem_inc(sem("unit_used"), 1)
            phase_end(pe)

            pe.wait_ge(*after("c_silu"))
            for i in range(12):
                unit_wait(pe, U_ADA + i)
                for m in range(4):
                    c = 4 * i + m
                    for k in range(KT):
                        mm = pe.matmul(bank(7, 2 * c, 2), unit(U_ADA + i)[:, k, m * P:m * P + P], csil[:, k, :],
                                       start=(k == 0), stop=(k == KT - 1))
                mm.then_inc(sem("ada_done"), 1)
                pe.wait_ge(sem("ada_done"), i + 1)
                pe.sem_inc(sem("unit_used"), 1)
            pe.wait_ge(sem("h_normed"), 6)
            for k in range(KT):
                A = 2 * (k % 3)
                if k >= 3:
                    pe.wait_ge(sem("hT_ready"), k - 2)
                for t in range(6):
                    dst = bank(A, t * P, P) if t < 2 else bank(A + 1, (t - 2) * P, P)
                    mm = pe.transpose(dst, lnx[:, t, k * P:k * P + P], ident)
                mm.then_inc(sem("h_turned"), 1)
            phase_end(pe)

            jobs_pe(pe, PROJ2)
            for n in range(len(JOBS) - 4, len(JOBS)):
                pe.wait_ge(sem("slot_act"), emptied(n)[1])
            for t in range(6):
                pe.wait_ge(sem("qk_roped"), t + 1)
                if t >= 2:
                    pe.wait_ge(sem("qkT_ready"), t - 1)
                b = t % 2
                mm = pe.transpose(bank(b, 0, P), gkv[:, t, 0:P], ident)
                if t >= 2:
                    for j in range(4):
                        mm = pe.transpose(bank(2 + b, j * P, P), qn[:, j * P:j * P + P], ident)
                mm.then_inc(sem("qk_turned"), 1)
            phase_end(pe)
            att_pe(pe, "gqa", 64)
            phase_end(pe)

            rwkv_pe(pe)
            phase_end(pe)

            for k in range(4):
                for t in range(4):
                    mm = pe.transpose(bank(k, t * P, P), mixG[:, t, k * P:k * P + P], ident)
            mm.then_inc(stage("mix2_turned"), 1)
            pe.wait_ge(*after("mixT2_ready"))
            for c in range(8):
                mm = pe.matmul(bank(c // 4, (c % 4) * P, P), mod[:, 16 + c, 0:1].broadcast_to([P, P]), ident,
                               start=True, stop=True)
            mm.then_inc(stage("gt1_rep"), 1)
            pe.wait_ge(*after("gt1_ready"))
            for n in range(2):
                unit_wait(pe, U_OUT2 + n)
                for t in range(4):
                    for k in range(KT):
                        lhs = mixT2[:, k, t * P:t * P + P] if k < 4 else rwT[:, k - 4, t * P:t * P + P]
                        mm = pe.matmul(bank(2 * t + n), lhs, unit(U_OUT2 + n)[:, k, :],
                                       start=(k == 0), stop=(k == KT - 1))
                mm.then_inc(sem("y2_done"), 1)
                pe.wait_ge(sem("y2_done"), n + 1)
                pe.sem_inc(sem("unit_used"), 1)
            phase_end(pe)

            pe.wait_ge(sem("xn_ready"), 4)
            for k in range(KT):
                if k >= 6:
                    pe.wait_ge(sem("h2T_ready"), k - 5)
                for t in range(4):
                    mm = pe.transpose(bank(k % 6, t * P, P), xn[:, t, k * P:k * P + P], ident)
                mm.then_inc(sem("h2_turned"), 1)
            pe.wait_ge(sem("h2T_ready"), 8)
            pe.wait_ge(sem("router_loaded"), 16)
            for t in range(4):
                for k in range(KT):
                    mm = pe.matmul(bank(7, t * EXP, EXP), h2T[:, k, t * P:t * P + P], router[:, k, :],
                                   start=(k == 0), stop=(k == KT - 1))
            mm.then_inc(stage("logits_done"), 1)
            for c in range(8):
                mm = pe.matmul(bank(4 + c // 4, (c % 4) * P, P), mod[:, 40 + c, 0:1].broadcast_to([P, P]), ident,
                               start=True, stop=True)
            mm.then_inc(stage("gt2_rep"), 1)
            pe.wait_ge(*after("aff_ready"))
            for t in range(4):
                mm = pe.transpose(bank(0, t * P, P, (0, EXP)), aff[:, t, :], ident)
            mm.then_inc(stage("aff_turned"), 1)
            pe.wait_ge(*after("rank_ready"))
            for t in range(4):
                mm = pe.transpose(bank(1, t * EXP, EXP), T("affT", 0, 2048, (0, EXP))[:, 512 + t * P:512 + t * P + P],
                                  ident[0:EXP, 0:EXP])
            mm.then_inc(stage("rank_turned"), 1)
            for t in range(4):
                pe.wait_ge(sem("hotg_ready"), t + 1)
                if t >= 1:
                    pe.wait_ge(sem("hotT_ready"), t)
                for e in range(8):
                    mm = pe.transpose(bank(2 + e // 4, (e % 4) * P, P), T("hotg", e * P, P), ident)
                mm.then_inc(sem("hot_turned"), 1)
            phase_end(pe)
            for k in range(KT):
                for eh in range(2):
                    n = 2 * k + eh
                    if n >= 8:
                        pe.wait_ge(sem("gather_dve" if n % 2 == 0 else "gather_act"), (n - 8) // 2 + 1)
                    for t in range(4):
                        mm = pe.matmul(bank(n % 8), xn[:, t, k * P:k * P + P], hot[:, t, eh * 512:eh * 512 + 512],
                                       start=(t == 0), stop=(t == 3))
                    mm.then_inc(sem("gathered"), 1)
            phase_end(pe)
            experts_pe(pe)
            phase_end(pe)


        @block.scalar
        def _(act):
            link = chain(act, "act_chain")
            act.wait_ge(sem("x_loaded"), 16)
            act.wait_ge(sem("meta_loaded"), 16)
            act.wait_ge(*after("small_clear"))
            stats_act(act, link, "xs", [(xin[:, t, :], P) for t in range(4)] + [(xin[0:META, 4, :], META)],
                      False, "junk")
            act.wait_ge(sem("vec_loaded"), 16)
            g = T("vec", VEC["norm_pre"][0], 8)
            for k in range(1, KT, 2):
                act.wait_ge(sem("x_turned"), k + 1)
                A = 2 * (k % 4)
                act.activation(xT[:, k, 0:512], bank(A), ACT.Copy, scale=g[:, k:k + 1])
                act.activation(xT[:, k, 512:528], bank(A + 1, 0, META), ACT.Copy, scale=g[:, k:k + 1])\
                    .then_inc(sem("xT_act"), 1)
            phase_end(act)
            jobs_empty(act, "a", PROJ1)
            act.wait_ge(*after("flog_ready"))
            z = T("cum", 0, 528, (0, 8))
            lz = T("junk", 0, 528, (0, 8))
            link(act.activation(lz, z, ACT.Abs))
            link(act.activation(lz, lz, ACT.Exp, scale=-1.0))
            act.activation(lz, lz, ACT.Ln, bias=1.0).then_inc(stage("logf_ready"), 1)
            phase_end(act)
            att_act(act, "fox", 0, FOX_SCALE)
            phase_end(act)
            for t in range(4):
                link(act.activation(T("junk", 0, 256), cqkv[:, t, 0:256], ACT.Square, accum_out=mss[:, t:t + 1]))
            for t in range(5):
                n = META if t == 4 else P
                link(act.activation(T("junk", 0, 128, (0, n)), cqkv[0:n, t, 256:384], ACT.Square,
                                    accum_out=mss[0:n, 5 + t:6 + t]))
            act.sem_inc(stage("mss_ready"), 1)
            act.wait_ge(*after("mvar_ready"))
            act.activation(mstd, mss, ACT.Sqrt).then_inc(stage("mstd_ready"), 1)
            jobs_empty(act, "a", MLAPREP)
            act.wait_ge(sem("slot_act"), sum(j[3] == "a" for j in JOBS if j[0] <= MLAPREP))
            for h in range(H):
                act.wait_ge(sem("q_turned"), h + 1)
                act.activation(mqT[0:QK, h, :], bank(h, 0, 512, (0, QK)), ACT.Copy)
            phase_end(act)
            att_act(act, "mla", 32, MLA_SCALE)
            phase_end(act)

            for k in range(1, 8, 2):
                act.wait_ge(sem("mix_turned"), k + 1)
                act.activation(mixT[:, k, :], bank(k), ACT.Copy).then_inc(sem("mixT_act"), 1)
            act.wait_ge(sem("y_done"), 2)
            stats_act(act, link, "ys", [(PS[:, t * 1024:t * 1024 + 1024], P) for t in range(4)], False, "junk")
            for t in range(4):
                act.wait_ge(sem("x1_ready"), t + 1)
            act.dma_start(x1_dram, T("xres")).then_inc(sem("x1_saved"), 16)
            phase_end(act)

            cv = T("vec", VEC["cvec"][0], 16)
            act.activation(T("csil"), cv, ACT.Silu).then_inc(stage("c_silu"), 1)
            act.wait_ge(sem("ctx_loaded"), 16)
            stats_act(act, link, "hs", [(ctxr[:, t, :], P) for t in range(2)] + [(xres[:, t, :], P) for t in range(4)],
                      True, "junk")
            act.wait_ge(sem("x1_saved"), 16)
            phase_end(act)
            jobs_empty(act, "a", PROJ2)
            act.wait_ge(sem("shifted"), 14)
            act.activation(wal[0:64, :], wal[0:64, :], ACT.Tanh).then_inc(sem("wal_ready"), 1)
            act.activation(gl[:, 0:512], gl[:, 0:512], ACT.Sigmoid).then_inc(sem("wal_ready"), 1)
            act.wait_ge(*after("gvar_ready"))
            act.activation(gstd, gss, ACT.Sqrt).then_inc(stage("gstd_ready"), 1)
            for t in range(6):
                act.wait_ge(sem("qk_turned"), t + 1)
                b = t % 2
                ins = act.activation(T("gkT", t * P, P), bank(b, 0, P), ACT.Copy)
                if t >= 2:
                    ins = act.activation(gqT[:, :, (t - 2) * P:(t - 1) * P],
                                         bank(2 + b).rearrange("p (j t) -> p j t", j=4), ACT.Copy)
                ins.then_inc(sem("qkT_ready"), 1)
            phase_end(act)
            att_act(act, "gqa", 64, GQA_SCALE)
            phase_end(act)

            act.wait_ge(*after("kksum_done"))
            act.activation(kkn[0:8, 0, :], PS[0:8, 0:768], ACT.Sqrt).then_inc(stage("kkroot"), 1)
            for g in range(12):
                act.wait_ge(sem("z_in"), g + 1)
                link(act.activation(W["sg"], W["sg"], ACT.Tanh, scale=0.5))
                act.activation(W["a"], W["a"], ACT.Tanh, scale=0.5).then_inc(sem("tanh_done"), 1)
                act.wait_ge(sem("p_ready"), g + 1)
                act.activation(W["Ei"], W["P"], ACT.Exp, scale=-DECAY)
                act.activation(W["Ev"], W["P"], ACT.Exp, scale=DECAY)
                act.wait_ge(sem("ex_ready"), g + 1)
                act.activation(W["Ee"], W["Ee"], ACT.Exp, scale=-DECAY).then_inc(sem("e_ready"), 1)
                act.wait_ge(sem("ab_done"), g + 1)
                act.activation(W["AT"], bank(3), ACT.Copy).then_inc(sem("at_ready"), 1)
                for lv in range(1, 6):
                    act.wait_ge(sem("z_done"), 5 * g + lv)
                    act.activation(W["Z"], bank(0), ACT.Copy).then_inc(sem("z_ready"), 1)
                act.wait_ge(sem("rows_done"), g + 1)
                act.wait_ge(sem("wc_ready"), g + 1)
                act.activation(W["bN"], bank(7), ACT.Copy)
                act.activation(W["kN"], bank(0), ACT.Copy)
                act.activation(W["vN"], bank(1), ACT.Copy).then_inc(sem("rows_ready"), 1)
                act.wait_ge(sem("r1_done"), g + 1)
                act.activation(W["R1"], bank(2), ACT.Copy).then_inc(sem("r1_ready"), 1)
                act.wait_ge(sem("u_done"), g + 1)
                act.activation(W["U"], bank(3), ACT.Copy).then_inc(sem("u_ready"), 1)
            act.wait_ge(*after("yvar_ready"))
            act.activation(ystd, yvar, ACT.Sqrt).then_inc(stage("ystd_ready"), 1)
            for j in range(4):
                act.wait_ge(sem("rw_cols"), j + 1)
                act.activation(rwT[:, j, :], bank(3 * (j % 2)), ACT.Identity, scale=T("vec", VEC["lnx_g"][0] + j, 1),
                               bias=T("vec", VEC["lnx_b"][0] + j, 1)).then_inc(sem("yn_affine"), 1)
            phase_end(act)

            act.dma_start(T("x2"), x1_dram).then_inc(sem("x1_back"), 16)
            act.dma_start(T("ln1"), w["ln1"].broadcast_to([P, 2 * D])).then_inc(sem("ln1_loaded"), 16)
            act.wait_ge(*after("mix2_turned"))
            act.activation(T("mixT2"), PS[:, 0:2048], ACT.Copy).then_inc(stage("mixT2_ready"), 1)
            act.wait_ge(*after("gt1_rep"))
            act.activation(T("grow"), PS[:, 0:1024], ACT.Copy).then_inc(stage("gt1_ready"), 1)
            stats_act(act, link, "z1", [(x2[:, t, :], P) for t in range(4)], True, "junk2",
                      lambda t: (sem("z1_ready"), t + 1))
            phase_end(act)

            act.dma_start(T("router"), w["router_w_2"][0].rearrange("(k p) e -> p k e", p=P))\
                .then_inc(sem("router_loaded"), 16)
            stats_act(act, link, "f", [(x2[:, t, :], P) for t in range(4)], True, "junk2")
            act.wait_ge(*after("gt2_rep"))
            act.activation(T("grow2"), PS[:, 4 * BANK:6 * BANK], ACT.Copy).then_inc(stage("gt2_ready"), 1)
            act.wait_ge(*after("logits_in"))
            act.activation(T("aff"), T("aff"), ACT.Exp).then_inc(stage("aff_exp"), 1)
            phase_end(act)
            for k in range(KT):
                act.wait_ge(sem("gathered"), 2 * k + 2)
                act.activation(xinT[:, k, 512:1024], bank((2 * k + 1) % 8), ACT.Identity,
                               scale=omsc[:, 16 + k:17 + k], bias=mod[:, 24 + k, 0:1]).then_inc(sem("gather_act"), 1)
            phase_end(act)
            for e in range(EXP):
                for n in range(2):
                    act.wait_ge(sem("gu_done"), 2 * e + n + 1)
                    if e >= 1:
                        act.wait_ge(sem("hid_ready"), 2 * (e - 1) + n + 1)
                    act.activation(T("sg", n * 512, 512, (64, 128)), bank(2 * (e % 2) + n, 0, 512, (0, 64)), ACT.Silu)\
                        .then_inc(sem("silu_done"), 1)
                act.wait_ge(sem("hid_turned"), e + 1)
                act.activation(T("hidT", (e % 2) * 512, 512), bank(4), ACT.Copy).then_inc(sem("hidT_ready"), 1)
            phase_end(act)
            act.dma_start(T("ln2"), w["ln2"].broadcast_to([P, 2 * D])).then_inc(sem("ln2_loaded"), 16)
            stats_act(act, link, "o", [(x2[:, t, :], P) for t in range(4)], True, "junk2")
            for t in range(4):
                act.wait_ge(sem("out_ready"), t + 1)
                act.dma_start(out[0, t * P:(t + 1) * P, :], x2[:, t, :]).then_inc(sem("out_stored"), 16)
            act.wait_ge(sem("out_stored"), 64)

        @block.vector
        def _(dve):
            link = chain(dve, "dve_chain")
            dve.memset(T("small"), 1.0).then_inc(stage("small_clear"), 1)
            stats_dve(dve, link, "xs", 5, False, EPS1)
            for t in range(5):
                n = META if t == 4 else P
                dve.tensor_scalar(xin[0:n, t, :], xin[0:n, t, :], st_rstd[0:n, t:t + 1], None, ALU.mult)\
                    .then_inc(sem("x_scaled"), 1)
            dve.wait_ge(sem("vec_loaded"), 16)
            g = T("vec", VEC["norm_pre"][0], 8)
            for k in range(0, KT, 2):
                dve.wait_ge(sem("x_turned"), k + 1)
                A = 2 * (k % 4)
                dve.tensor_scalar(xT[:, k, 0:512], bank(A), g[:, k:k + 1], None, ALU.mult)
                dve.tensor_scalar(xT[:, k, 512:528], bank(A + 1, 0, META), g[:, k:k + 1], None, ALU.mult)\
                    .then_inc(sem("xT_dve"), 1)
            phase_end(dve)
            jobs_empty(dve, "d", PROJ1)
            z = T("cum", 0, 528, (0, 8))
            dve.wait_ge(sem("slot_dve"), sum(j[3] == "d" for j in JOBS if j[0] <= PROJ1))
            dve.tensor_scalar(z, z, T("vec", VEC["b_f"][0], 1, (0, 8)), None, ALU.add).then_inc(stage("flog_ready"), 1)
            dve.wait_ge(*after("logf_ready"))
            logf = T("junk", 0, 528, (0, 8))
            link(dve.scalar_tensor_tensor(out=logf, in0=z, scalar=0.0, in1=logf, op0=ALU.min, op1=ALU.subtract))
            zero = T("junk", 528, 496, (0, 8))
            link(dve.memset(T("junk", 528, 496, (0, 8)), 0.0))
            cumt = T("fox_cum", 0, 528, (0, 8))
            link(dve.tensor_tensor_scan(cumt[:, 0:264], logf[:, 0:264], zero[:, 0:264], 0.0, ALU.add, ALU.add))
            link(dve.tensor_tensor_scan(cumt[:, 264:528], logf[:, 264:528], zero[:, 0:264], cumt[:, 263:264],
                                        ALU.add, ALU.add))
            dve.tensor_copy(T("cum", 0, 512, (0, 8)), cumt[:, META:528])
            dve.tensor_copy(T("cum", 512, META, (0, 8)), cumt[:, 0:META])
            phase_end(dve)
            att_dve(dve, link, "fox", 0, FOX_SCALE, mixR[:, :, 0:512], fgate)
            phase_end(dve)

            dve.wait_ge(*after("mss_ready"))
            dve.tensor_scalar(mss[:, 0:5], mss[:, 0:5], 1.0 / 256, EPS1, ALU.mult, ALU.add)
            dve.tensor_scalar(mss[:, 5:10], mss[:, 5:10], 1.0 / 128, EPS1, ALU.mult, ALU.add)\
                .then_inc(stage("mvar_ready"), 1)
            mcos = C("mcos").rearrange("p (t n) -> p t n", n=16)
            msin = C("msin").rearrange("p (t n) -> p t n", n=16)
            krow = T("krow").rearrange("p (t n) -> p t n", n=32)
            tmp = T("rtmp")

            def rope(x1, x2, c, s, o1, o2, shape):
                n = 1
                for a in shape:
                    n *= a
                t = []
                for i in range(4):
                    v = tmp_rope[0][:, i * n:(i + 1) * n]
                    if len(shape) == 2:
                        v = v.rearrange("p (a b) -> p a b", a=shape[0])
                    if len(shape) == 3:
                        v = v.rearrange("p (a b c) -> p a b c", a=shape[0], b=shape[1])
                    t.append(v[0:x1.shape[0]])
                dve.tensor_tensor(t[0], x1, c, ALU.mult)
                dve.tensor_tensor(t[1], x2, s, ALU.mult)
                dve.tensor_tensor(t[2], x1, s, ALU.mult)
                link(dve.tensor_tensor(t[3], x2, c, ALU.mult))
                dve.tensor_tensor(o1, t[0], t[1], ALU.subtract)
                return dve.tensor_tensor(o2, t[2], t[3], ALU.add)

            tmp_rope = [tmp]
            for lo, hi, n in ((0, 4, P), (4, 5, META)):
                kr = cqkv[0:n, lo:hi, 384:416]
                link(rope(kr[:, :, 0:16], kr[:, :, 16:32], mcos[0:n, lo:hi, :], msin[0:n, lo:hi, :],
                          krow[0:n, lo:hi, 0:16], krow[0:n, lo:hi, 16:32], (hi - lo, 16)))
            dve.wait_ge(*after("mstd_ready"))
            link(dve.reciprocal(mrs, mstd))
            for t in range(5):
                n = META if t == 4 else P
                if t < 4:
                    dve.tensor_scalar(cqkv[:, t, 0:256], cqkv[:, t, 0:256], mrs[:, t:t + 1], None, ALU.mult)
                ins = dve.tensor_scalar(cqkv[0:n, t, 256:384], cqkv[0:n, t, 256:384], mrs[0:n, 5 + t:6 + t], None,
                                        ALU.mult)
            ins.then_inc(stage("cq_scaled"), 1)
            dve.wait_ge(*after("cq_turned"))
            qg, kg = T("vec", VEC["q_norm"][0], 2), T("vec", VEC["kv_norm"][0], 1)
            for k in range(2):
                dve.tensor_scalar(cqT[:, k, :], bank(k), qg[:, k:k + 1], None, ALU.mult)
            dve.tensor_scalar(T("ckvT", 0, 512), bank(2), kg, None, ALU.mult)
            dve.tensor_scalar(T("ckvT", 512, META), bank(3, 0, META), kg, None, ALU.mult)
            dve.tensor_copy(T("krT", 0, 512, (0, 32)), bank(4, 0, 512, (0, 32)))
            dve.tensor_copy(T("krT", 512, META, (0, 32)), bank(5, 0, META, (0, 32))).then_inc(stage("cqT_ready"), 1)

            def rope_q(name, i):
                dve.wait_ge(sem("slot_dve"), emptied([n for n, j in enumerate(JOBS) if j[1:3] == (name, i)][0])[1])
                q = qrow[:, i, :].rearrange("p (h n) -> p h n", n=QK)
                c, s = rep(mcos[:, i, :], 8), rep(msin[:, i, :], 8)
                rope(q[:, :, 64:80], q[:, :, 80:96], c, s, q[:, :, 64:80], q[:, :, 80:96], (8, 16))\
                    .then_inc(sem("q_roped"), 1)
                dve.wait_ge(sem("q_roped"), i + 1)
            jobs_empty(dve, "d", MLAPREP, rope_q)
            dve.wait_ge(*after("cqT_ready"))
            for h in range(H):
                dve.tensor_copy(mkT[64:96, h, :], T("krT", 0, 528, (0, 32)))
            phase_end(dve)
            att_dve(dve, link, "mla", 32, MLA_SCALE, mixR[:, :, 512:1024], mgate)
            phase_end(dve)

            for k in range(0, 8, 2):
                dve.wait_ge(sem("mix_turned"), k + 1)
                dve.tensor_copy(mixT[:, k, :], bank(k)).then_inc(sem("mixT_dve"), 1)
            stats_dve(dve, link, "ys", 4, False, EPS1)
            dve.wait_ge(sem("xres_loaded"), 16)
            dve.wait_ge(sem("npost_loaded"), 16)
            for t in range(4):
                link(dve.scalar_tensor_tensor(out=ytmp[:, t % 2, :], in0=PS[:, t * 1024:t * 1024 + 1024],
                                              scalar=st_rstd[:, t:t + 1], in1=T("norm_post"), op0=ALU.mult,
                                              op1=ALU.mult))
                dve.tensor_tensor(xres[:, t, :], xres[:, t, :], ytmp[:, t % 2, :], ALU.add)\
                    .then_inc(sem("x1_ready"), 1)
            phase_end(dve)

            stats_dve(dve, link, "hs", 6, True, LN_EPS)
            for t in range(6):
                src = ctxr[:, t, :] if t < 2 else xres[:, t - 2, :]
                dve.tensor_scalar(lnx[:, t, :], src, st_rstd[:, t:t + 1], st_nb[:, t:t + 1], ALU.mult, ALU.add)\
                    .then_inc(sem("h_normed"), 1)
            dve.wait_ge(sem("ada_done"), 12)
            bada = bc(T("vec", VEC["b_ada"][0], 48), 2)
            link(dve.tensor_tensor(mod, bank(7, 0, 96).rearrange("p (c v) -> p c v", v=2), bada, ALU.add))
            dve.tensor_scalar(omsc[:, 0:8], mod[:, 8:16, 0], 1.0, None, ALU.add)
            dve.tensor_scalar(omsc[:, 8:16], mod[:, 8:16, 1], 1.0, None, ALU.add)
            link(dve.tensor_scalar(omsc[:, 16:24], mod[:, 32:40, 0], 1.0, None, ALU.add))
            for k in range(KT):
                dve.wait_ge(sem("h_turned"), k + 1)
                A = 2 * (k % 3)
                dve.tensor_scalar(hT[:, k, 0:CTX], bank(A, 0, CTX), omsc[:, 8 + k:9 + k], mod[:, k, 1:2],
                                  ALU.mult, ALU.add)
                dve.tensor_scalar(hT[:, k, CTX:TOK2], bank(A + 1), omsc[:, k:k + 1], mod[:, k, 0:1],
                                  ALU.mult, ALU.add).then_inc(sem("hT_ready"), 1)
            phase_end(dve)

            for i in range(14):
                latent_only = i < 4 or i == 13
                lo = 258 if latent_only else 0
                dve.wait_ge(sem("raw_ready"), i + 1)
                dve.wait_ge(sem("nbr_ready"), i + 1)
                r, nb = raw[:, i % 2, :], nbr[:, i % 2, :]
                link(dve.scalar_tensor_tensor(out=nb[:, lo:770], in0=nb[:, lo:770], scalar=0.5,
                                              in1=r[:, lo + 1:771], op0=ALU.mult, op1=ALU.subtract))
                mu = T("vec", VEC["mu"][0] + i, 1)
                if i < 4:
                    dl, dc = rT[:, i, :], None
                elif i == 13:
                    dl, dc = gl[:, 0:512], None
                else:
                    dst = kT[:, i - 4, :] if i < 8 else vT[:, i - 8, :] if i < 12 else wal
                    dl, dc = dst[:, CTX:TOK2], dst[:, 0:CTX]
                if dc is not None:
                    dve.scalar_tensor_tensor(out=dc, in0=nb[:, 0:256], scalar=mu, in1=r[:, 1:257], op0=ALU.mult,
                                             op1=ALU.add)
                dve.scalar_tensor_tensor(out=dl, in0=nb[:, 258:770], scalar=mu, in1=r[:, 259:771], op0=ALU.mult,
                                         op1=ALU.add).then_inc(sem("shifted"), 1)
            for t in range(4):
                link(dve.tensor_tensor(T("gsq"), gq[:, t, :], gq[:, t, :], ALU.mult))
                link(dve.tensor_reduce(gss[:, 8 * t:8 * t + 8], T("gsq").rearrange("p (h n) -> p h n", n=64), AX,
                                       ALU.add))
            sq = T("gsq", 0, 128)
            for t in range(6):
                link(dve.tensor_tensor(sq, gkv[:, t, 0:128], gkv[:, t, 0:128], ALU.mult))
                link(dve.tensor_reduce(gss[:, 32 + 2 * t:34 + 2 * t], sq.rearrange("p (h n) -> p h n", n=64), AX,
                                       ALU.add))
            dve.tensor_scalar(gss, gss, 1.0 / 64, EPS1, ALU.mult, ALU.add).then_inc(stage("gvar_ready"), 1)
            dve.wait_ge(*after("gstd_ready"))
            link(dve.reciprocal(grs, gstd))
            dve.wait_ge(sem("gains_loaded"), 16)
            acos = C("acos").rearrange("p (t a n) -> p t a n", t=4, a=2)
            asin = C("asin").rearrange("p (t a n) -> p t a n", t=4, a=2)
            tmp_rope[0] = T("gtmp")
            for t in range(6):
                k = gkv[:, t, 0:128].rearrange("p (h n) -> p h n", n=64)
                link(dve.tensor_tensor(k, k, bc(grs[:, 32 + 2 * t:34 + 2 * t], 64), ALU.mult))
                ins = dve.tensor_tensor(k, k, rep(T("gains", 64, 64), 2), ALU.mult)
                if t < 2:
                    ins.then_inc(sem("qk_roped"), 1)
                    continue
                link(ins)
                kh = gkv[:, t, 0:128].rearrange("p (h a b n) -> p h a b n", h=2, a=2, b=2)
                c, s = rep2(acos[:, t - 2], 2), rep2(asin[:, t - 2], 2)
                link(rope(kh[:, :, :, 0, :], kh[:, :, :, 1, :], c, s, kh[:, :, :, 0, :], kh[:, :, :, 1, :],
                          (2, 2, 16)))
                q = gq[:, t - 2, :].rearrange("p (h n) -> p h n", n=64)
                link(dve.tensor_tensor(q, q, bc(grs[:, 8 * (t - 2):8 * (t - 2) + 8], 64), ALU.mult))
                link(dve.tensor_tensor(q, q, rep(T("gains", 0, 64), 8), ALU.mult))
                if t >= 3:
                    dve.wait_ge(sem("qk_turned"), t)
                for gg in range(2):
                    qh = gq[:, t - 2, gg * 256:gg * 256 + 256].rearrange("p (h a b n) -> p h a b n", h=4, a=2, b=2)
                    o = qn.rearrange("p (j g a b n) -> p j g a b n", j=4, g=2, a=2, b=2)[:, :, gg]
                    c, s = rep2(acos[:, t - 2], 4), rep2(asin[:, t - 2], 4)
                    ins = rope(qh[:, :, :, 0, :], qh[:, :, :, 1, :], c, s, o[:, :, :, 0, :], o[:, :, :, 1, :],
                               (4, 2, 16))
                    if gg == 0:
                        link(ins)
                ins.then_inc(sem("qk_roped"), 1)
                dve.wait_ge(sem("qk_roped"), t + 1)
            phase_end(dve)
            att_dve(dve, link, "gqa", 64, GQA_SCALE, mixG, None)
            phase_end(dve)
            rwkv_dve(dve, link)
            phase_end(dve)

            dve.wait_ge(sem("x1_back"), 16)
            dve.wait_ge(sem("y2_done"), 2)
            dve.wait_ge(*after("gt1_ready"))
            for t in range(4):
                y = PS[:, t * 1024:t * 1024 + 1024]
                link(dve.tensor_tensor(T("junk2"), y, T("grow"), ALU.mult))
                dve.scalar_tensor_tensor(out=x2[:, t, :], in0=x2[:, t, :], scalar=ALPHA, in1=T("junk2"),
                                         op0=ALU.mult, op1=ALU.add).then_inc(sem("z1_made"), 1)
                dve.wait_ge(sem("z1_made"), t + 1)
            dve.sem_inc(sem("z1_ready"), 4)
            affine_norm(dve, link, "z1", "ln1")
            phase_end(dve)

            stats_dve(dve, link, "f", 4, True, LN_EPS)
            for t in range(4):
                dve.tensor_scalar(xn[:, t, :], x2[:, t, :], st_rstd[:, t:t + 1], st_nb[:, t:t + 1], ALU.mult,
                                  ALU.add).then_inc(sem("xn_ready"), 1)
            for k in range(KT):
                dve.wait_ge(sem("h2_turned"), k + 1)
                dve.tensor_scalar(h2T[:, k, :], bank(k % 6), omsc[:, 16 + k:17 + k], mod[:, 24 + k, 0:1], ALU.mult,
                                  ALU.add).then_inc(sem("h2T_ready"), 1)
            for t in range(4):
                dve.wait_ge(sem("xn_ready"), 4)
                dve.tensor_scalar(x2[:, t, :], x2[:, t, :], ALPHA, None, ALU.mult)
            dve.wait_ge(*after("logits_done"))
            lg = bank(7, 0, 64).rearrange("p (t e) -> p t e", e=EXP)
            link(dve.tensor_reduce(rmx, lg, AX, ALU.max))
            dve.tensor_tensor(aff, lg, bc(rmx, EXP), ALU.subtract).then_inc(stage("logits_in"), 1)
            dve.wait_ge(*after("aff_exp"))
            link(dve.tensor_reduce(rsm, aff, AX, ALU.add))
            link(dve.reciprocal(rri, rsm))
            dve.tensor_tensor(aff, aff, bc(rri, EXP), ALU.mult).then_inc(stage("aff_ready"), 1)
            dve.wait_ge(*after("aff_turned"))
            work = [T("affT", b * 512, 512, (0, EXP)) for b in range(4)]
            link(dve.tensor_copy(work[0], bank(0, 0, 512, (0, EXP))))
            for r in range(CAP // 8):
                a, b = work[r % 2], work[(r + 1) % 2]
                link(dve.max(m8[0:EXP, :], a))
                link(dve.match_replace(out=b, in_to_replace=m8[0:EXP, :], in_values=a, imm_value=-1.0))
            taken, count = work[2], work[3]
            link(dve.tensor_scalar(taken, work[0], 0.0, None, ALU.is_lt))
            link(dve.memset(work[1], 0.0))
            link(dve.tensor_tensor_scan(count, taken, work[1], 0.0, ALU.add, ALU.add))
            dve.tensor_tensor(work[1], count, taken, ALU.mult).then_inc(stage("rank_ready"), 1)
            dve.wait_ge(*after("rank_turned"))
            link(dve.tensor_copy(T("pos"), bank(1, 0, 64)))
            for t in range(4):
                h = hot[:, t, :].rearrange("p (e c) -> p e c", c=CAP)
                link(dve.tensor_tensor(h, bc(pos[:, t, :], CAP), rep(C("slot"), EXP), ALU.is_equal))
                if t >= 1:
                    dve.wait_ge(sem("hot_turned"), t)
                dve.tensor_tensor(T("hotg").rearrange("p (e c) -> p e c", c=CAP), h, bc(aff[:, t, :], CAP), ALU.mult)\
                    .then_inc(sem("hotg_ready"), 1)
                dve.wait_ge(sem("hot_turned"), t + 1)
                dve.tensor_copy(hotT[:, :, t * P:t * P + P],
                                PS[:, 2 * BANK:4 * BANK].rearrange("p (e t) -> p e t", t=P))\
                    .then_inc(sem("hotT_ready"), 1)
            phase_end(dve)
            for k in range(KT):
                dve.wait_ge(sem("gathered"), 2 * k + 1)
                dve.tensor_scalar(xinT[:, k, 0:512], bank(2 * k % 8), omsc[:, 16 + k:17 + k], mod[:, 24 + k, 0:1],
                                  ALU.mult, ALU.add).then_inc(sem("gather_dve"), 1)
            phase_end(dve)

            def scatter_add(p2):
                for t in range(4):
                    for n in range(2):
                        i = p2 * 8 + t * 2 + n
                        dve.wait_ge(sem("scattered"), i + 1)
                        if i >= 8:
                            dve.wait_ge(sem("added"), i - 7)
                        dst = x2[:, t, n * 512:n * 512 + 512]
                        dve.tensor_tensor(dst, dst, bank(6 + i % 2), ALU.add).then_inc(sem("added"), 1)

            for e in range(EXP):
                for n in range(2):
                    dve.wait_ge(sem("silu_done"), 2 * e + n + 1)
                    if e >= 1:
                        dve.wait_ge(sem("hid_turned"), e)
                    dve.tensor_tensor(T("hid", n * 512, 512, (64, 128)), T("sg", n * 512, 512, (64, 128)),
                                      bank(2 * (e % 2) + n, 0, 512, (64, 128)), ALU.mult)\
                        .then_inc(sem("hid_ready"), 1)
                dve.wait_ge(sem("down_done"), e + 1)
                lo = (e % 2) * 64
                y = T("ypair", (e // 2 % 2) * D, D, (lo, lo + 64))
                if e >= 4:
                    dve.wait_ge(sem("scattered"), 8 * (e // 2 - 1))
                for n in range(2):
                    g2 = T("grow2", n * 512, 512, (lo, lo + 64))
                    ins = dve.tensor_tensor(y[:, n * 512:n * 512 + 512], bank(5, 0, 512, (n * 64, n * 64 + 64)), g2,
                                            ALU.mult)
                ins.then_inc(sem("y_left"), 1)
                if e % 2:
                    scatter_add(e // 2)
            phase_end(dve)
            affine_norm(dve, link, "o", "ln2", "out_ready")

        @block.gpsimd
        def _(pool):
            phase_end(pool)
            phase_end(pool)
            phase_end(pool)
            phase_end(pool)
            phase_end(pool)
            pool.dma_start(T("xres").rearrange("p (t d) -> p t d", d=D), w["x"][0].rearrange("(t p) d -> p t d", p=P))\
                .then_inc(sem("xres_loaded"), 16)
            pool.dma_start(T("norm_post"), w["norm_post"].broadcast_to([P, D])).then_inc(sem("npost_loaded"), 16)
            pool.wait_ge(sem("xres_loaded"), 16)
            pool.wait_ge(sem("npost_loaded"), 16)
            phase_end(pool)
            pool.dma_start(ctxr, w["ctx_2"][0].rearrange("(t p) d -> p t d", p=P)).then_inc(sem("ctx_loaded"), 16)
            pool.wait_ge(sem("ctx_loaded"), 16)
            phase_end(pool)
            pool.dma_start(T("gains"), w["gains"].broadcast_to([P, 128])).then_inc(sem("gains_loaded"), 16)
            pool.memset(T("raw"), 0.0).then_inc(sem("raw_clear"), 1)
            for i in range(14):
                lo = 258 if (i < 4 or i == 13) else 0
                pool.wait_ge(sem("raw_ready"), i + 1)
                if i >= 2:
                    pool.wait_ge(sem("shifted"), i - 1)
                r = raw[:, i % 2, :]
                pool.tensor_tensor(nbr[:, i % 2, lo:770], r[:, lo:770], r[:, lo + 2:772], ALU.add)\
                    .then_inc(sem("nbr_ready"), 1)
            pool.wait_ge(sem("gains_loaded"), 16)
            phase_end(pool)
            phase_end(pool)
            pool.dma_start(lora[0:64], w["decay_up_2"][0].rearrange("d k n -> k d n")).then_inc(sem("lora_loaded"), 16)
            pool.dma_start(lora[64:128], w["iclr_up_2"][0].rearrange("d k n -> k d n")).then_inc(sem("lora_loaded"), 16)
            pool.dma_start(T("gateup"), w["gate_up_2"][0]).then_inc(sem("gate_loaded"), 16)
            ka = T("vec", VEC["k_a"][0], 4)
            for g in range(12):
                if g:
                    pool.wait_ge(sem("ds_done"), g)
                pool.wait_ge(sem("a_ready"), g + 1)
                for d in range(2):
                    tok = step_tok(g, d)
                    a = W["a"][:, d * 256:d * 256 + 256].rearrange("p (j n) -> p j n", n=64)
                    b = W["bt"][:, d * 256:d * 256 + 256].rearrange("p (j n) -> p j n", n=64)
                    ins = pool.tensor_tensor(b, kkT[:, :, tok:tok + 64], a, ALU.mult)
                ins.then_inc(sem("b_ready"), 1)
                pool.tensor_scalar(W["kd"], W["a"], 1.0, None, ALU.subtract).then_inc(sem("pool_chain"), 1)
                pool.wait_ge(sem("pool_chain"), 4 * g + 1)
                for d in range(2):
                    kd = W["kd"][:, d * 256:d * 256 + 256].rearrange("p (j n) -> p j n", n=64)
                    ins = pool.tensor_tensor(kd, kd, bc(ka, 64), ALU.mult)
                ins.then_inc(sem("pool_chain"), 1)
                pool.wait_ge(sem("pool_chain"), 4 * g + 2)
                pool.tensor_scalar(W["kd"], W["kd"], 1.0, None, ALU.add).then_inc(sem("pool_chain"), 1)
                pool.wait_ge(sem("pool_chain"), 4 * g + 3)
                for d in range(2):
                    tok = step_tok(g, d)
                    kd = W["kd"][:, d * 256:d * 256 + 256].rearrange("p (j n) -> p j n", n=64)
                    ins = pool.tensor_tensor(kd, kd, kT[:, :, tok:tok + 64], ALU.mult)
                ins.then_inc(sem("kd_ready"), 1)
                pool.sem_inc(sem("pool_chain"), 1)
                pool.wait_ge(sem("at_ready"), g + 1)
                for lv in range(1, 6):
                    if lv > 1:
                        pool.wait_ge(sem("z_done"), 5 * g + lv - 1)
                    for d in range(2):
                        sl = slice(d * 256, d * 256 + 256)
                        ins = pool.tensor_tensor(W["M"][:, sl].rearrange("p (j n) -> p j n", n=64),
                                                 W["AT"][:, sl].rearrange("p (j n) -> p j n", n=64),
                                                 rep(C("level", lv * 128 + d * 64, 64), 4), ALU.mult)
                    ins.then_inc(sem("m_ready"), 1)
            pool.wait_ge(sem("lora_loaded"), 32)
            pool.wait_ge(sem("gate_loaded"), 16)
            phase_end(pool)
            phase_end(pool)
            phase_end(pool)
            phase_end(pool)
            phase_end(pool)


def constants():
    import numpy as np
    c = {n: np.zeros((P, wd), np.float32) for n, (_, wd) in CONST.items()}
    p = np.arange(P)[:, None]
    n128, n64 = np.arange(P)[None, :], np.arange(64)[None, :]
    c["ident"][:] = p == n128
    c["causal"][:] = np.where(n128 > p, NEG, 0)
    c["chunkmask"][:] = np.where(n128 // CH > p // CH, NEG, 0)
    for h in range(8):
        c["negsel"][h, h * P:(h + 1) * P] = -1.0 / FOX_SCALE
    inv = (np.float32(10000.0) ** (-np.arange(0, ROPE, 2, dtype=np.float32) / np.float32(ROPE))).astype(np.float32)
    for t in range(5):
        posn = (np.arange(P) + (META + t * P if t < 4 else 0)).astype(np.float32)
        ang = (posn[:, None] * inv[None, :]).astype(np.float32)
        c["mcos"][:, t * 16:t * 16 + 16] = np.cos(ang)
        c["msin"][:, t * 16:t * 16 + 16] = np.sin(ang)
    inv = (np.float32(10000.0) ** (-np.arange(16, dtype=np.float32) / np.float32(16))).astype(np.float32)
    for t in range(4):
        posn = np.arange(P) + t * P
        for a, q in enumerate((posn // 64, posn % 64)):
            ang = (q.astype(np.float32)[:, None] * inv[None, :]).astype(np.float32)
            c["acos"][:, t * 32 + a * 16:t * 32 + a * 16 + 16] = np.cos(ang)
            c["asin"][:, t * 32 + a * 16:t * 32 + a * 16 + 16] = np.sin(ang)
    s = p % 64
    for d in range(2):
        lo, o = slice(d * 64, d * 64 + 64), n64
        before = (s < o) if d == 0 else (s > o)
        c["strict"][:, lo] = before
        c["incl"][:, lo] = before | (s == o)
        c["pair0"][:, lo] = (s // 2 == o // 2) & ((s > o) if d == 0 else (s < o))
        for lv in range(6):
            b = 2 ** lv
            lvl = slice(lv * 128 + d * 64, lv * 128 + d * 64 + 64)
            c["level"][:, lvl] = (s // (2 * b) == o // (2 * b)) & (s // b != o // b) & before
        seg = np.ones((4, 64))
        seg[:, 0 if d == 0 else 63] = 0
        c["seg"][:, d * 256:d * 256 + 256] = seg.reshape(1, 256)
    c["ident2"][:] = s == n64
    for j in range(4):
        for q in range(2):
            c["headsum"][q * 64:q * 64 + 64, j * 8 + 2 * j + q] = 1
            c["headspread"][2 * j + q, j * P + q * 64:j * P + q * 64 + 64] = 1
    c["slot"][:] = n64 + 1
    c["blockones"][:] = p // 64 == n128 // 64
    return np.concatenate([c[n] for n in CONST], 1)


def vectors(a):
    import numpy as np

    def cols(x, n):
        return np.asarray(x).reshape(n, P).T
    out = np.zeros((P, NVEC), np.float32)

    def put(name, x):
        lo, n = VEC[name]
        out[0:x.shape[0], lo:lo + n] = x
    put("norm_pre", cols(a["norm_pre"][0], 8))
    put("q_norm", cols(a["q_norm"][0], 2))
    put("kv_norm", cols(a["kv_norm"][0], 1))
    put("b_f", np.asarray(a["b_f"])[0][:, None])
    put("cvec", np.stack([cols(a["c_2"][0], 8), cols(a["c_ctx_2"], 8)], 2).reshape(P, 16))
    put("b_ada", cols(a["b_ada_2"][0], 48))
    put("mu", cols(a["tshift_mu_2"][0], 14))
    put("w0", cols(a["decay_w0_2"][0], 8))
    put("a0", cols(a["iclr_a0_2"][0], 8))
    for n in ("k_k", "k_a", "r_k", "lnx_g", "lnx_b"):
        put(n, cols(a[n + "_2"][0], 4))
    return out


_WHOLE = ("x", "meta", "w_in", "w_uq", "w_ukv", "w_out", "ctx_2", "w_ada_2", "w_in_2", "decay_up_2", "iclr_up_2",
          "gate_up_2", "w_out_2", "router_w_2", "exp_w_gate_2", "exp_w_up_2", "exp_w_down_2", "norm_post")


def kernel(**inputs):
    import numpy as np
    import concourse.bacc as bacc
    from concourse.bass_utils import run_bass_kernel_spmd

    nc = bacc.Bacc("TRN2", target_bir_lowering=False, num_devices=1)
    arrays = {n: np.ascontiguousarray(inputs[n]) for n in _WHOLE}
    arrays["consts"] = constants()
    arrays["vecs"] = vectors(inputs)
    arrays["ln1"] = np.concatenate([inputs["ln1_g_2"], inputs["ln1_b_2"]], 1)
    arrays["ln2"] = np.concatenate([inputs["ln2_g_2"], inputs["ln2_b_2"]], 1)
    arrays["gains"] = np.concatenate([inputs["q_gain_2"], inputs["k_gain_2"]], 1)
    w = {n: nc.dram_tensor(n, a.shape, mybir.dt.from_np(a.dtype), kind="ExternalInput").ap()
         for n, a in arrays.items()}
    out = nc.dram_tensor("out", (1, SEQ, D), F32, kind="ExternalOutput").ap()
    program(nc, w, out)
    r = run_bass_kernel_spmd(nc, [arrays], core_ids=[0])
    return r.results[0]["out"]
```

```python
from contextlib import ExitStack

import concourse.bass as bass
from concourse import mybir

F32 = mybir.dt.float32
ALU = mybir.AluOpType
ACT = mybir.ActivationFunctionType
AX = mybir.AxisListType.X

P = 128
D = 1024
KT = D // P
SEQ, META, CTX = 512, 16, 256
QT = SEQ // P
TOK2 = CTX + SEQ
H = 8
HD = 64
CH = 64
NOPE, ROPE, QK = 64, 32, 96
EXP, CAP = 16, 64
RING = 4
SLOT = KT * 512
BANK = 512
EPS1, LN_EPS, GN_EPS, L2_EPS = 1e-6, 1e-5, 64e-5, 1e-12
ALPHA = 2.0 ** 0.25
FOX_SCALE, MLA_SCALE, GQA_SCALE = HD ** -0.5, QK ** -0.5, HD ** -0.5
DECAY = 0.6065306597126334
NEG = -1e30

CONST = {}
_at = 0
for _name, _w in (("ident", 128), ("causal", 128), ("chunkmask", 128), ("mcos", 80),
                  ("msin", 80), ("acos", 128), ("asin", 128), ("strict", 128), ("incl", 128),
                  ("pair0", 128), ("level", 128), ("levelT", 6 * 128), ("ident2", 64), ("seg", 512), ("headsum", 32),
                  ("headspread", 512), ("slot", 64), ("blockones", 128), ("groupsum", 2)):
    CONST[_name] = (_at, _w)
    _at += _w
NCONST = _at
VEC = {}
_at = 0
for _name, _w in (("norm_pre", 8), ("q_norm", 2), ("kv_norm", 1), ("b_f", 1), ("cvec", 16), ("b_ada", 48),
                  ("mu", 14), ("w0", 8), ("a0", 8), ("k_k", 4), ("k_a", 4), ("r_k", 4), ("lnx_g", 4), ("lnx_b", 4)):
    VEC[_name] = (_at, _w)
    _at += _w
NVEC = _at

LOAD, PROJ1, FOX, MLAPREP, MLA, OUT1, MOD, PROJ2, GQA, RWKV, OUT2, ROUTE, GATHER, EXPERTS, FINAL = range(15)
LIVES = [
    ("const", NCONST, LOAD, FINAL), ("vec", NVEC, LOAD, FINAL), ("small", 512, LOAD, FINAL),
    ("xin", 5 * D, LOAD, LOAD), ("junk", D, LOAD, MOD), ("junk2", D, OUT2, FINAL),
    ("xT", KT * 528, LOAD, PROJ1),
    ("fqT", 8 * SEQ, PROJ1, FOX), ("fkT", 8 * 528, PROJ1, FOX), ("fv", 5 * 512, PROJ1, FOX),
    ("cum", 528, PROJ1, FOX), ("fox_cum", 528, PROJ1, PROJ1), ("fgate", 4 * 512, PROJ1, FOX), ("mgate", 4 * 512, PROJ1, MLA),
    ("cqkv", 5 * 416, PROJ1, MLAPREP), ("mixR", 4 * D, FOX, OUT1),
    ("prob", 2 * 768, FOX, GQA), ("probT", 2 * 768, FOX, GQA),
    ("cqT", 2 * 512, MLAPREP, MLAPREP), ("ckvT", 528, MLAPREP, MLAPREP), ("krT", 528, MLAPREP, MLAPREP),
    ("qrow", 4 * 768, MLAPREP, MLAPREP), ("rtmp", 2 * 512, MLAPREP, MLAPREP), ("krow", 5 * 32, MLAPREP, MLAPREP),
    ("mqT", 8 * 512, MLAPREP, MLA), ("mkT", 8 * 528, MLAPREP, MLA), ("mv", 5 * 512, MLAPREP, MLA),
    ("mixT", 8 * SEQ, OUT1, OUT1), ("xres", 4 * D, OUT1, MOD), ("norm_post", D, OUT1, OUT1),
    ("ytmp", 2 * D, OUT1, OUT1),
    ("mod", 96, PROJ1, FINAL), ("csil", 256, LOAD, PROJ1), ("adarow", 2 * 512, PROJ1, PROJ1), ("ctx", 2 * D, OUT1, MOD), ("lnx", 6 * D, MOD, MOD),
    ("hT", KT * TOK2, MOD, PROJ2),
    ("gq", 4 * 512, PROJ2, PROJ2), ("gkv", 6 * 256, PROJ2, GQA), ("gsq", 512, PROJ2, PROJ2),
    ("gtmp", 2 * 256, PROJ2, PROJ2), ("gains", 128, PROJ2, PROJ2),
    ("gqT", 8 * 512, PROJ2, GQA), ("gkT", TOK2, PROJ2, GQA),
    ("raw", 2 * 772, PROJ2, PROJ2), ("nbr", 2 * 770, PROJ2, PROJ2),
    ("rT", 4 * SEQ, PROJ2, RWKV), ("kT", 4 * TOK2, PROJ2, RWKV), ("vT", 4 * TOK2, PROJ2, RWKV),
    ("wal", TOK2, PROJ2, RWKV), ("gl", TOK2, PROJ2, RWKV),
    ("mixG", 4 * 512, GQA, OUT2),
    ("kkT", 4 * TOK2, RWKV, RWKV), ("lora", 2 * 512, RWKV, RWKV), ("gateup", 512, RWKV, RWKV),
    
    ("yacc", 4 * 512, RWKV, RWKV), ("kkn", 2 * 768, RWKV, RWKV), ("rwT", 4 * 512, RWKV, OUT2),
] + [(f"w{i}", 512, RWKV, RWKV) for i in range(18)] + [
    ("mixT2", 4 * 512, OUT2, OUT2), ("x2", 4 * D, OUT2, FINAL), ("ln1", 2 * D, OUT2, OUT2), ("ztmp", D, OUT2, OUT2),
    ("grow", D, OUT2, OUT2), ("ln2", 2 * D, FINAL, FINAL), ("grow2", D, ROUTE, EXPERTS),
    ("xn", 4 * D, ROUTE, GATHER), ("h2T", 8 * 512, ROUTE, ROUTE), ("router", 128, ROUTE, ROUTE),
    ("aff", 64, ROUTE, GATHER), ("affT", 4 * 512, ROUTE, ROUTE), ("pos", 64, ROUTE, ROUTE),
    ("hot", 4 * 1024, ROUTE, GATHER), ("hotg", 1024, GATHER, GATHER), ("hotT", 8 * 512, GATHER, EXPERTS),
    ("xinT", 8 * 1024, GATHER, EXPERTS),
    ("sg", 512 * 2, EXPERTS, EXPERTS), ("hid", D, EXPERTS, EXPERTS), ("hidT", 2 * 512, EXPERTS, EXPERTS),
    ("ypair", 2 * D, EXPERTS, EXPERTS),
]
MAXF = (229344 - 16512) // 4 - RING * SLOT - 64


def place():
    placed, at = [], {}
    for name, size, a, b in sorted(LIVES, key=lambda t: (-(t[3] - t[2]), -t[1])):
        off = 0
        for o, s in sorted((o, s) for o, s, pa, pb in placed if not (b < pa or pb < a)):
            if off + size <= o:
                break
            off = max(off, o + s)
        placed.append((off, size, a, b))
        at[name] = (off, size)
    top = max(o + s for o, s in at.values())
    assert top <= MAXF, (top, MAXF, sorted([(o + s, n) for n, (o, s) in at.items()])[-8:])
    return at, top


JOBS = []
_ada = 0
for _name, _n, _engines in (("fq", 4, "da"), ("fk", 4, "da"), ("fv", 5, "da"), ("fgate", 4, "a"),
                            ("cqkv", 5, "d"), ("mgate", 4, "a"), ("flog", 1, "d")):
    for _i in range(_n):
        JOBS.append((PROJ1, _name, _i, _engines[_i % len(_engines)]))
        if _i % 2 and _ada < 12:
            if _ada:
                JOBS.append((PROJ1, "adac", _ada - 1, "d"))
            JOBS.append((PROJ1, "ada", _ada, "a"))
            _ada += 1
JOBS.append((PROJ1, "adac", 11, "d"))
PROJ1_UNITS = []
for _, _name, _i, _ in JOBS:
    if _name == "ada" or (_name != "adac" and _i == 0):
        PROJ1_UNITS.append((_name, _i))
JOBS += [(MLAPREP, "mq", _i, "d") for _i in range(4)]
JOBS += [(MLAPREP, "mv", _i, "a") for _i in range(5)]
JOBS += [(MLAPREP, "mk", _i, "a") for _i in range(8)]
JOBS += [(PROJ2, "gq", _i, "a") for _i in range(4)]
JOBS += [(PROJ2, "gkv", _i, "a") for _i in range(6)]
JOBS += [(PROJ2, "rw", _i, "a") for _i in range(14)]

EXP_ORDER = []
for _e in range(EXP + 1):
    EXP_ORDER += [("gu", _e, 0)] * (_e < EXP) + [("down", _e - 1, 0)] * (_e > 0) + [("gu", _e, 1)] * (_e < EXP)
EXP_READS = [(k, 2 * e + n + 1 if k == "gu" else e + 1) for k, e, n in EXP_ORDER for _ in range(2)]


def unit_list(w):
    def cols(m, lo, n):
        return (m[:, lo:lo + n].rearrange("(k p) n -> p k n", p=P), m.shape[0] // P, n)
    w_in, w2 = w["w_in"][0], w["w_in_2"][0]
    part = {"fq": (0, 512), "fk": (512, 512), "fv": (1024, 512), "fgate": (1544, 512), "cqkv": (2056, 416),
            "mgate": (2472, 512), "flog": (1536, 8)}
    units = []
    for name, i in PROJ1_UNITS:
        units.append(cols(w["w_ada_2"][0], i * 512, 512) if name == "ada" else cols(w_in, *part[name]))
    units += [cols(w["w_uq"][0], 0, 768), cols(w["w_ukv"][0], 0, 1024)]
    units += [cols(w["w_out"][0], lo, 512) for lo in (0, 512)]
    units += [cols(w2, lo, n) for lo, n in ((0, 512), (512, 256), (768, 512), (1280, 512), (1792, 512), (2304, 256))]
    units += [cols(w["w_out_2"][0], lo, 512) for lo in (0, 512)]
    for kind, e, n in EXP_ORDER:
        if kind == "gu":
            units += [cols(w["exp_w_gate_2"][0, e], n * 512, 512), cols(w["exp_w_up_2"][0, e], n * 512, 512)]
        else:
            units += [cols(w["exp_w_down_2"][0, e], n, 512) for n in (0, 512)]
    return units


STAGES = {
    "dve_stage": (
        "small_clear csil_clear xs_var flog_ready mvar_ready cq_scaled cqT_ready ys_var hs_var gvar_ready "
        "kkn_ready yvar_ready yn_ready z1_var f_var logits_in aff_ready rank_ready  "
        "o_var ").split(),
    "act_stage": (
        "xs_ss xs_std logf_ready mss_ready mstd_ready ys_ss ys_std hs_ss hs_std gstd_ready "
        "kkroot ystd_ready mixT2_ready gt1_ready z1_ss z1_std f_ss f_std gt2_ready aff_exp  "
        "o_ss o_std ").split(),
    "pe_stage": (
        "cq_turned kksum_done mix2_turned gt1_rep logits_done gt2_rep aff_turned rank_turned ").split(),
}


def emptied(n):
    return JOBS[n][3], sum(j[3] == JOBS[n][3] for j in JOBS[:n + 1])


def program(nc, w, out):
    at, top = place()
    with ExitStack() as ctx:
        arena = ctx.enter_context(nc.sbuf_tensor("arena", [P, top], F32))
        ring = ctx.enter_context(nc.sbuf_tensor("ring", [P, RING, SLOT], F32))
        PS = ctx.enter_context(nc.psum_tensor("PS", [P, 8 * BANK], F32))
        x1_dram = nc.dram_tensor("x1_scratch", (P, 4 * D), F32, kind="Internal").ap()
        sems = {}

        def sem(name):
            if name not in sems:
                sems[name] = ctx.enter_context(nc.semaphore(name))
            return sems[name]

        def stage(name):
            return sem(next(k for k, v in STAGES.items() if name in v))

        def after(name):
            return stage(name), next(v.index(name) + 1 for v in STAGES.values() if name in v)

        def T(name, lo=0, n=None, p=(0, P)):
            off, size = at[name]
            assert lo + (size - lo if n is None else n) <= size, name
            return arena[p[0]:p[1], off + lo:off + (size if n is None else lo + n)]

        def C(name, lo=0, n=None, p=(0, P)):
            off, size = CONST[name]
            return T("const", off + lo, size - lo if n is None else n, p)

        def V(name, i, n=1, p=(0, P)):
            return T("vec", VEC[name][0] + i, n, p)

        small_at = [0]

        def small(n):
            small_at[0] += n
            assert small_at[0] <= 512
            return T("small", small_at[0] - n, n)

        def bank(b, lo=0, n=BANK, p=(0, P)):
            return PS[p[0]:p[1], b * BANK + lo:b * BANK + lo + n]

        def bc(ap, n):
            return ap.unsqueeze(2).broadcast_to([ap.shape[0], ap.shape[1], n])

        def rep(ap, n):
            return ap.unsqueeze(1).broadcast_to([ap.shape[0], n, ap.shape[1]])

        def unit(i):
            _, k, n = units[i]
            return ring[:, i % RING, 0:k * n].rearrange("p (k n) -> p k n", k=k)

        units = unit_list(w)
        U_UP, U_OUT, U_IN2, U_OUT2, U_EXP = 19, 21, 23, 29, 31

        SCAN_SLOTS = (U_OUT2 + 1, U_OUT2 + 2, U_OUT2 + 3)
        assert [i % RING for i in SCAN_SLOTS] == [2, 3, 0]

        st_sum, st_nmean, st_ss, st_var, st_std, st_rstd, st_nb = (small(6) for _ in range(7))
        mx, nbias, rsum, rinv = (small(32) for _ in range(4))
        gss, gstd, grs = small(44), small(44), small(44)
        mss, mstd, mrs = small(10), small(10), small(10)
        omsc = small(32)
        wcs = (small(8), small(8))
        yst, yvar, ystd = small(32), small(32), small(32)
        rmx, rsm, rri = small(4), small(4), small(4)
        m8 = small(8)

        block = ctx.enter_context(nc.Block())
        phase_n = {}

        def phase_end(e):
            e.drain()
            e.sem_inc(sem("phase_left"), 1)
            phase_n[e] = phase_n.get(e, 0) + 1
            e.wait_ge(sem("phase_left"), 4 * phase_n[e])

        def chain(e, name):
            n = [0]

            def link(ins):
                n[0] += 1
                ins.then_inc(sem(name), 1)
                e.wait_ge(sem(name), n[0])
                return ins
            return link

        def unit_wait(pe, i):
            pe.wait_ge(sem(f"unit_loaded{i % RING}"), 16 * (i // RING + 1))

        LAST_OF_UNIT = {U_UP: ("mq", 3), U_UP + 1: ("mk", 7), U_IN2: ("gq", 3), U_IN2 + 1: ("gkv", 5),
                        U_IN2 + 2: ("rw", 3), U_IN2 + 3: ("rw", 7), U_IN2 + 4: ("rw", 11), U_IN2 + 5: ("rw", 13)}

        def last_read(i):
            if i < U_UP:
                name, j = PROJ1_UNITS[i]
                last = (name, j) if name == "ada" else (name, max(a[2] for a in JOBS if a[1] == name))
                return sem("job_done"), [n for n, a in enumerate(JOBS) if a[1:3] == last][0] + 1
            if U_OUT <= i < U_IN2:
                return sem("y_done"), i - U_OUT + 1
            if U_OUT2 <= i < U_EXP:
                return sem("y2_done"), i - U_OUT2 + 1
            if i >= U_EXP:
                return (sem("gu_done"), EXP_READS[i - U_EXP][1]) if EXP_READS[i - U_EXP][0] == "gu" else \
                    (sem("down_done"), EXP_READS[i - U_EXP][1])
            return sem("job_done"), [n for n, j in enumerate(JOBS) if j[1:3] == LAST_OF_UNIT[i]][0] + 1

        @block.sync
        def _(sp):
            sp.dma_start(T("const"), w["consts"]).then_inc(sem("const_loaded"), 16)
            sp.dma_start(T("vec"), w["vecs"]).then_inc(sem("vec_loaded"), 16)
            xin = T("xin").rearrange("p (t d) -> p t d", d=D)
            sp.dma_start(xin[:, 0:4, :], w["x"][0].rearrange("(t p) d -> p t d", p=P)).then_inc(sem("x_loaded"), 16)
            sp.dma_start(xin[0:META, 4, :], w["meta"]).then_inc(sem("meta_loaded"), 16)
            for i, (src, k, n) in enumerate(units):
                if i >= RING:
                    sp.wait_ge(*last_read(i - RING))
                if i in SCAN_SLOTS:
                    sp.wait_ge(sem("ds_done"), 24)
                sp.dma_start(unit(i), src).then_inc(sem(f"unit_loaded{i % RING}"), 16)

        NMEANS = {"hs": 0, "z1": 6, "f": 10, "o": 14}

        def stats_act(act, link, tag, srcs, mean, junk):
            for i, (src, n) in enumerate(srcs):
                if mean:
                    act.wait_ge(sem("nmean_ready"), NMEANS[tag] + i + 1)
                link(act.activation(T(junk, 0, D, (0, n)), src, ACT.Square,
                                    bias=st_nmean[0:n, i:i + 1] if mean else 0.0,
                                    accum_out=st_ss[0:n, i:i + 1]))
            act.sem_inc(stage(f"{tag}_ss"), 1)
            k = len(srcs)
            act.wait_ge(*after(f"{tag}_var"))
            act.activation(st_std[:, 0:k], st_var[:, 0:k], ACT.Sqrt).then_inc(stage(f"{tag}_std"), 1)

        def row_mean(dve, link, tag, i, src):
            link(dve.tensor_reduce(st_sum[:, i:i + 1], src, AX, ALU.add))
            dve.tensor_scalar(st_nmean[:, i:i + 1], st_sum[:, i:i + 1], -1.0 / D, None, ALU.mult)\
                .then_inc(sem("nmean_ready"), 1)

        def stats_dve(dve, link, tag, k, mean, eps):
            dve.wait_ge(*after(f"{tag}_ss"))
            dve.tensor_scalar(st_var[:, 0:k], st_ss[:, 0:k], 1.0 / D, eps, ALU.mult, ALU.add)\
                .then_inc(stage(f"{tag}_var"), 1)
            dve.wait_ge(*after(f"{tag}_std"))
            link(dve.reciprocal(st_rstd[:, 0:k], st_std[:, 0:k]))
            if mean:
                dve.wait_ge(sem("nmean_ready"), NMEANS[tag] + k)
                link(dve.tensor_tensor(st_nb[:, 0:k], st_nmean[:, 0:k], st_rstd[:, 0:k], ALU.mult))

        fqT = T("fqT").rearrange("p (m t) -> p m t", t=SEQ)
        fkT = T("fkT").rearrange("p (m t) -> p m t", t=528)
        fv = T("fv").rearrange("p (t n) -> p t n", n=512)
        mqT = T("mqT").rearrange("p (h t) -> p h t", t=SEQ)
        mkT = T("mkT").rearrange("p (h t) -> p h t", t=528)
        mv = T("mv").rearrange("p (t n) -> p t n", n=512)
        gqT = T("gqT").rearrange("p (j t) -> p j t", t=SEQ)
        gkv = T("gkv").rearrange("p (t n) -> p t n", n=256)
        mixR = T("mixR").rearrange("p (t n) -> p t n", n=D)
        mixG = T("mixG").rearrange("p (t n) -> p t n", n=512)
        prob = T("prob").rearrange("p (b n) -> p b n", b=2)
        probT = T("probT").rearrange("p (b n) -> p b n", b=2)

        def att_keys(kind, qt):
            if kind == "gqa":
                return [(b * P, P, b * P, b) for b in range(6)]
            return [(b * P, P, b * P, b) for b in range(qt + 1)] + [(SEQ, META, (qt + 1) * P, 4)]

        def att_segments(kind, qt):
            if kind == "gqa":
                return [(0, 512, 0), (512, 256, 512)]
            n = (qt + 1) * P
            return [(0, n, 0), (SEQ, META, n)]

        def att_pe(pe, kind, base):
            for i in range(32 + 3):
                if i < 32:
                    h, qt, g = i % 8, i // 8, base + i
                    q0 = qt * P
                    if g >= 2:
                        pe.wait_ge(sem("probs_ready"), g - 1)
                    score = PS[:, (g % 2) * 2 * BANK:(g % 2 + 1) * 2 * BANK]
                    for k0, n, s0 in att_segments(kind, qt):
                        o = score[:, s0:s0 + n]
                        if kind == "fox":
                            mm = pe.matmul(o, fqT[:, h, q0:q0 + P], fkT[:, h, k0:k0 + n],
                                           start=True, stop=(k0 == SEQ))
                        elif kind == "mla":
                            mm = pe.matmul(o, mqT[:, h, q0:q0 + P], mkT[:, h, k0:k0 + n],
                                           start=True, stop=(k0 == SEQ))
                        else:
                            mm = pe.matmul(o, gqT[:, h, q0:q0 + P], T("gkT", k0, n), start=True, stop=True)
                        if kind != "gqa" and k0 == 0:
                            mm = pe.matmul(score[:, q0:q0 + P], C("ident"),
                                           C("causal" if kind == "fox" else "chunkmask"), start=False, stop=True)
                    mm.then_inc(sem("scores_ready"), 1)
                if 2 <= i < 34:
                    g = base + i - 2
                    qt = (i - 2) // 8
                    if g >= 1:
                        pe.wait_ge(sem("probT_dve"), g)
                        pe.wait_ge(sem("probT_act"), g)
                    pe.wait_ge(sem("probs_ready"), g + 1)
                    for b, (_, n, s0, _) in enumerate(att_keys(kind, qt)):
                        c = b if n == P else 4
                        mm = pe.transpose(PS[0:n, (4 * BANK) + c * P:(4 * BANK) + c * P + P],
                                          prob[:, g % 2, s0:s0 + n], C("ident"))
                    mm.then_inc(sem("probs_turned"), 1)
                if i >= 3:
                    g = base + i - 3
                    h, qt = (i - 3) % 8, (i - 3) // 8
                    pe.wait_ge(sem("probT_dve"), g + 1)
                    pe.wait_ge(sem("probT_act"), g + 1)
                    ob = 6 + (g // 8) % 2
                    if h == 0 and g >= 16:
                        pe.wait_ge(sem("heads_out"), g // 8 - 1)
                    keys = att_keys(kind, qt)
                    for b, (_, n, _, vt) in enumerate(keys):
                        c = b if n == P else 4
                        if kind == "gqa":
                            v = gkv[:, vt, 128 + (h // 4) * 64:128 + (h // 4) * 64 + 64]
                        else:
                            v = (fv if kind == "fox" else mv)[0:n, vt, h * 64:h * 64 + 64]
                        mm = pe.matmul(bank(ob, h * 64, 64), probT[0:n, g % 2, c * P:c * P + P], v,
                                       start=(b == 0), stop=(b == len(keys) - 1))
                    mm.then_inc(sem("head_done"), 1)

        def att_width(kind, qt):
            return 768 if kind == "gqa" else (qt + 1) * P + META

        def att_act(act, kind, base, scale):
            for i in range(32 + 2):
                if i < 32:
                    g, qt = base + i, i // 8
                    act.wait_ge(sem("max_ready"), g + 1)
                    if g >= 2:
                        act.wait_ge(sem("probs_turned"), g - 1)
                    n = att_width(kind, qt)
                    act.activation(prob[:, g % 2, 0:n], PS[:, (g % 2) * 1024:(g % 2) * 1024 + n], ACT.Exp,
                                   bias=nbias[:, i:i + 1], scale=scale, accum_out=rsum[:, i:i + 1])\
                        .then_inc(sem("probs_ready"), 1)
                if i >= 2:
                    g = base + i - 2
                    act.wait_ge(sem("probs_turned"), g + 1)
                    if g >= 2:
                        act.wait_ge(sem("head_done"), g - 1)
                    if kind == "gqa":
                        s, d = bank(5, 0, 256), probT[:, g % 2, 512:768]
                    else:
                        s, d = bank(5, 0, P, (0, META)), probT[0:META, g % 2, 512:512 + P]
                    act.activation(d, s, ACT.Copy).then_inc(sem("probT_act"), 1)

        def att_dve(dve, link, kind, base, scale, dest, gate):
            for i in range(32 + 3):
                if i < 32:
                    g, qt = base + i, i // 8
                    dve.wait_ge(sem("scores_ready"), g + 1)
                    link(dve.tensor_reduce(mx[:, i:i + 1],
                                           PS[:, (g % 2) * 1024:(g % 2) * 1024 + att_width(kind, qt)], AX, ALU.max))
                    dve.tensor_scalar(nbias[:, i:i + 1], mx[:, i:i + 1], -scale, None, ALU.mult)\
                        .then_inc(sem("max_ready"), 1)
                if 2 <= i < 34:
                    g, qt = base + i - 2, (i - 2) // 8
                    n = 512 if kind == "gqa" else (qt + 1) * P
                    dve.wait_ge(sem("probs_turned"), g + 1)
                    if g >= 2:
                        dve.wait_ge(sem("head_done"), g - 1)
                    dve.tensor_copy(probT[:, g % 2, 0:n], bank(4, 0, n)).then_inc(sem("probT_dve"), 1)
                if i >= 3 and (i - 3) % 8 == 7:
                    g, qt = base + i - 3, (i - 3) // 8
                    dve.wait_ge(sem("probs_ready"), g + 1)
                    link(dve.reciprocal(rinv[:, qt * 8:qt * 8 + 8], rsum[:, qt * 8:qt * 8 + 8]))
                    dve.wait_ge(sem("head_done"), g + 1)
                    o = dest[:, qt, :].rearrange("p (h n) -> p h n", n=64)
                    src = bank(6 + (g // 8) % 2).rearrange("p (h n) -> p h n", n=64)
                    ins = dve.tensor_tensor(o, src, bc(rinv[:, qt * 8:qt * 8 + 8], 64), ALU.mult)
                    ins.then_inc(sem("heads_out"), 1)
                    if gate is not None:
                        dve.wait_ge(sem("heads_out"), g // 8 + 1)
                        link(dve.tensor_tensor(dest[:, qt, :], dest[:, qt, :], gate[:, qt, :], ALU.mult))

        xT = T("xT").rearrange("p (k t) -> p k t", t=528)
        hT = T("hT").rearrange("p (k t) -> p k t", t=TOK2)
        cqT = T("cqT").rearrange("p (k t) -> p k t", t=512)
        cqkv = T("cqkv").rearrange("p (t n) -> p t n", n=416)
        UNIT_OF = {n: i for i, (n, _) in enumerate(PROJ1_UNITS) if n != "ada"}
        csil = T("csil").rearrange("p (k v) -> p k v", v=32)

        def job_matmuls(pe, name, i, s):
            A, B = 2 * s, 2 * s + 1
            rows = META if i == 4 else P
            if name in ("fq", "fk", "flog"):
                u = unit(UNIT_OF[name])
                m = 8 if name == "flog" else P
                for dst, t0, n in ((bank(A, 0, 512, (0, m)), 0, 512), (bank(B, 0, META, (0, m)), 512, META)):
                    if name == "fq" and t0:
                        continue
                    for k in range(KT):
                        mm = pe.matmul(dst, u[:, k, i * P:i * P + m], xT[:, k, t0:t0 + n],
                                       start=(k == 0), stop=(k == KT - 1))
            elif name in ("fv", "fgate", "cqkv", "mgate"):
                u = unit(UNIT_OF[name])
                n = u.shape[2]
                for k in range(KT):
                    mm = pe.matmul(bank(A, 0, n, (0, rows)), xT[:, k, i * P:i * P + rows], u[:, k, :],
                                   start=(k == 0), stop=(k == KT - 1))
            elif name == "ada":
                u = unit(FIRST_OF_UNIT[(name, i)])
                for k in range(2):
                    for gp in range(4):
                        mm = pe.matmul(bank(A, 0, 512, (32 * gp, 32 * gp + 32)), csil[:, 2 * gp + k, :],
                                       u[:, 2 * gp + k, :], start=(k == 0), stop=(k == 1))
            elif name == "adac":
                pe.wait_ge(sem("ada_rows"), i + 1)
                for m in range(4):
                    mm = pe.matmul(bank(A, 2 * m, 2), T("adarow", i % 2 * 512 + m * P, P), C("groupsum"),
                                   start=True, stop=True)
            elif name == "mq":
                u = unit(U_UP)
                for b, lo, n in ((A, 0, 512), (B, 512, 256)):
                    for k in range(2):
                        mm = pe.matmul(bank(b, 0, n), cqT[:, k, i * P:i * P + P], u[:, k, lo:lo + n],
                                       start=(k == 0), stop=(k == 1))
            elif name == "mv":
                u = unit(U_UP + 1)[:, 0, :].rearrange("p (h a n) -> p h a n", h=8, a=2)
                mm = pe.matmul(bank(A, 0, 512, (0, rows)), T("ckvT", i * P, rows), u[:, :, 1, :],
                               start=True, stop=True)
            elif name == "mk":
                u = unit(U_UP + 1)[:, 0, i * 128:i * 128 + 64]
                pe.matmul(bank(A, 0, 512, (0, 64)), u, T("ckvT", 0, 512), start=True, stop=True)
                mm = pe.matmul(bank(B, 0, META, (0, 64)), u, T("ckvT", 512, META), start=True, stop=True)
            elif name == "gq":
                for k in range(KT):
                    mm = pe.matmul(bank(A), hT[:, k, CTX + i * P:CTX + i * P + P], unit(U_IN2)[:, k, :],
                                   start=(k == 0), stop=(k == KT - 1))
            elif name == "gkv":
                for k in range(KT):
                    mm = pe.matmul(bank(A, 0, 256), hT[:, k, i * P:i * P + P], unit(U_IN2 + 1)[:, k, :],
                                   start=(k == 0), stop=(k == KT - 1))
            else:
                u = unit(U_IN2 + 2 + i // 4)
                for b, t0, n in ((A, CTX, SEQ), (B, 0, CTX)):
                    if (i < 4 or i == 13) and b == B:
                        continue
                    for k in range(KT):
                        mm = pe.matmul(bank(b, 0, n), u[:, k, (i % 4) * P:(i % 4) * P + P], hT[:, k, t0:t0 + n],
                                       start=(k == 0), stop=(k == KT - 1))
            return mm

        FIRST_OF_UNIT = {**{n: i for i, n in enumerate(PROJ1_UNITS)}, ("mq", 0): 19, ("mv", 0): 20, ("gq", 0): 23, ("gkv", 0): 24, ("rw", 0): 25,
                         ("rw", 4): 26, ("rw", 8): 27, ("rw", 12): 28}

        def jobs_pe(pe, phase, before=None):
            for n, (ph, name, i, _) in enumerate(JOBS):
                if ph != phase:
                    continue
                if (name, i) in FIRST_OF_UNIT:
                    unit_wait(pe, FIRST_OF_UNIT[(name, i)])
                if n >= 4:
                    e, c = emptied(n - 4)
                    pe.wait_ge(sem("slot_dve" if e == "d" else "slot_act"), c)
                if before:
                    before(name, i)
                job_matmuls(pe, name, i, n % 4).then_inc(sem("job_done"), 1)

        fgate = T("fgate").rearrange("p (t n) -> p t n", n=512)
        mgate = T("mgate").rearrange("p (t n) -> p t n", n=512)
        qrow = T("qrow").rearrange("p (t n) -> p t n", n=768)
        gq = T("gq").rearrange("p (t n) -> p t n", n=512)
        raw = T("raw").rearrange("p (b n) -> p b n", b=2)
        nbr = T("nbr").rearrange("p (b n) -> p b n", b=2)
        rT = T("rT").rearrange("p (j t) -> p j t", t=SEQ)
        kT = T("kT").rearrange("p (j t) -> p j t", t=TOK2)
        vT = T("vT").rearrange("p (j t) -> p j t", t=TOK2)
        wal, gl = T("wal"), T("gl")

        def job_empty(e, is_act, name, i, s):
            A, B = 2 * s, 2 * s + 1
            rows = META if i == 4 else P

            def copy(dst, src):
                return e.activation(dst, src, ACT.Copy) if is_act else e.tensor_copy(dst, src)
            if name == "fq":
                copy(fqT[0:64, 2 * i, :], bank(A, 0, 512, (0, 64)))
                return copy(fqT[0:64, 2 * i + 1, :], bank(A, 0, 512, (64, 128)))
            if name == "fk":
                for q in range(2):
                    half = (q * 64, q * 64 + 64)
                    copy(fkT[0:64, 2 * i + q, 0:512], bank(A, 0, 512, half))
                    ins = copy(fkT[0:64, 2 * i + q, 512:528], bank(B, 0, META, half))
                return ins
            if name == "ada":
                if i >= 2:
                    e.wait_ge(sem("job_done"), 1 + [n for n, j in enumerate(JOBS) if j[1:3] == ("adac", i - 2)][0])
                return copy(T("adarow", i % 2 * 512, 512), bank(A))
            if name == "adac":
                return e.tensor_tensor(mod[:, 4 * i:4 * i + 4, :],
                                       bank(A, 0, 8).rearrange("p (c v) -> p c v", v=2),
                                       bc(T("vec", VEC["b_ada"][0] + 4 * i, 4), 2), ALU.add)
            if name == "fv":
                return copy(fv[0:rows, i, :], bank(A, 0, 512, (0, rows)))
            if name in ("fgate", "mgate"):
                return e.activation((fgate if name == "fgate" else mgate)[:, i, :], bank(A), ACT.Silu)
            if name == "cqkv":
                return copy(cqkv[0:rows, i, :], bank(A, 0, 416, (0, rows)))
            if name == "flog":
                copy(T("cum", META, 512, (0, 8)), bank(A, 0, 512, (0, 8)))
                return copy(T("cum", 0, META, (0, 8)), bank(B, 0, META, (0, 8)))
            if name == "mq":
                return copy(qrow[:, i, :], PS[:, A * BANK:A * BANK + 768])
            if name == "mv":
                return copy(mv[0:rows, i, :], bank(A, 0, 512, (0, rows)))
            if name == "mk":
                copy(mkT[0:64, i, 0:512], bank(A, 0, 512, (0, 64)))
                return copy(mkT[0:64, i, 512:528], bank(B, 0, META, (0, 64)))
            if name == "gq":
                return copy(gq[:, i, :], bank(A))
            if name == "gkv":
                return copy(gkv[:, i, :], bank(A, 0, 256))
            if i >= 2:
                e.wait_ge(sem("shifted"), i - 1)
            e.wait_ge(sem("raw_clear"), 1)
            if not (i < 4 or i == 13):
                copy(raw[:, i % 2, 1:257], bank(B, 0, 256))
            return copy(raw[:, i % 2, 259:771], bank(A))

        def jobs_empty(e, which, phase, after=None):
            for n, (ph, name, i, eng) in enumerate(JOBS):
                if ph != phase or eng != which:
                    continue
                e.wait_ge(sem("job_done"), n + 1)
                job_empty(e, which == "a", name, i, n % 4).then_inc(sem("slot_dve" if which == "d" else "slot_act"), 1)
                if name == "ada":
                    e.wait_ge(sem("slot_act"), emptied(n)[1])
                    e.sem_inc(sem("ada_rows"), 1)
                if name == "rw":
                    e.wait_ge(sem("slot_act"), emptied(n)[1])
                    e.sem_inc(sem("raw_ready"), 1)
                if after:
                    after(name, i)

        ident = C("ident")
        xin = T("xin").rearrange("p (t d) -> p t d", d=D)
        mixT = T("mixT").rearrange("p (k t) -> p k t", t=SEQ)
        xres = T("xres").rearrange("p (t d) -> p t d", d=D)
        ytmp = T("ytmp").rearrange("p (t d) -> p t d", d=D)
        mod = T("mod").rearrange("p (c v) -> p c v", v=2)
        ctxr = T("ctx").rearrange("p (t d) -> p t d", d=D)
        lnx = T("lnx").rearrange("p (t d) -> p t d", d=D)

        def qn(t):
            return T("prob", t * 512, 512) if t < 3 else T("gsq")

        mixT2 = T("mixT2").rearrange("p (k t) -> p k t", t=SEQ)
        rwT = T("rwT").rearrange("p (k t) -> p k t", t=SEQ)
        x2 = T("x2").rearrange("p (t d) -> p t d", d=D)
        xn = T("xn").rearrange("p (t d) -> p t d", d=D)
        h2T = T("h2T").rearrange("p (k t) -> p k t", t=SEQ)
        router = T("router").rearrange("p (k e) -> p k e", e=EXP)
        aff = T("aff").rearrange("p (t e) -> p t e", e=EXP)
        pos = T("pos").rearrange("p (t e) -> p t e", e=EXP)
        hot = T("hot").rearrange("p (t c) -> p t c", c=EXP * CAP)
        hotT = T("hotT").rearrange("p (e t) -> p e t", t=SEQ)
        xinT = T("xinT").rearrange("p (k c) -> p k c", c=EXP * CAP)
        kkT = T("kkT").rearrange("p (j t) -> p j t", t=TOK2)
        kkn = T("kkn").rearrange("p (b t) -> p b t", b=2)
        yacc = T("yacc").rearrange("p (j c n) -> p j c n", j=4, n=64)
        lora = T("lora").rearrange("p (d n) -> p d n", d=2)

        STACKED = ("sg", "a", "P", "Ei", "Ev", "Ee", "kd", "al_s", "rt_s", "bt_s", "S", "vN", "R1", "U")
        BLOCKS = ("al", "rt", "bt", "kt", "AT", "X", "XT", "AakT", "ArbT", "ArkT", "bN", "kN")
        W = {n: T(f"w{i}") for i, n in enumerate(STACKED)}
        W["Z"] = arena[:, at["w16"][0]:at["w16"][0] + 1024]
        for i, n in enumerate(BLOCKS):
            W[n] = ring[:, (0, 2, 3)[i // 4], (i % 4) * 1024:(i % 4) * 1024 + 1024]

        def hcol(d, h):
            return d * 4 * BANK + h * 256

        def hb(d, h):
            return PS[:, hcol(d, h):hcol(d, h) + 256].rearrange("p (j n) -> p j n", n=64)

        def hq(d, h, q):
            return hb(d, h)[q * 64:q * 64 + 64]

        def wide(d, b):
            return bank(4 * d + b).rearrange("p (j n) -> p j n", n=128)

        def blocks(name, d):
            return W[name][:, d * 512:d * 512 + 512].rearrange("p (j n) -> p j n", n=128)

        def diag(name, d, q):
            return blocks(name, d)[q * 64:q * 64 + 64, :, q * 64:q * 64 + 64]

        def block_all(name, q):
            return W[name].rearrange("p (s n) -> p s n", n=128)[q * 64:q * 64 + 64, :, q * 64:q * 64 + 64]

        def part(name, q):
            return W[name].rearrange("p (s n) -> p s n", n=64)[q * 64:q * 64 + 64]

        def by(name, d):
            return W[name][:, d * 256:d * 256 + 256].rearrange("p (j n) -> p j n", n=64)

        def mask(name, d, i=0):
            return rep(C(name, i * 128 + d * 64, 64), 4)

        def halves(name, s, q):
            return W[name][q * 64:q * 64 + 64, s * 64:s * 64 + 64]

        def step_tok(g, d):
            return 64 * (g if d == 0 else (3 - g if g < 4 else 15 - g))

        def kk_sq(j):
            off = at["w0"][0]
            assert all(at[f"w{i}"][0] == off + 512 * i for i in range(18))
            return arena[:, off + j * TOK2:off + (j + 1) * TOK2]

        def rep2(ap, n):
            return ap.unsqueeze(1).broadcast_to([ap.shape[0], n, ap.shape[1], ap.shape[2]])

        def affine_norm(dve, link, tag, gb, ready=None):
            stats_dve(dve, link, tag, 4, True, LN_EPS)
            dve.wait_ge(sem(f"{gb}_loaded"), 16)
            for t in range(4):
                link(dve.tensor_scalar(x2[:, t, :], x2[:, t, :], st_rstd[:, t:t + 1], st_nb[:, t:t + 1], ALU.mult,
                                       ALU.add))
                link(dve.tensor_tensor(x2[:, t, :], x2[:, t, :], T(gb, 0, D), ALU.mult))
                ins = dve.tensor_tensor(x2[:, t, :], x2[:, t, :], T(gb, D, D), ALU.add)
                if ready:
                    ins.then_inc(sem(ready), 1)
                else:
                    link(ins)

        def rk_prod(j):
            return W[STACKED[4 + j]]

        def kk_sq_all(n):
            off = at["w0"][0]
            return arena[:, off:off + n]

        def rwkv_pe(pe):
            pe.wait_ge(sem("lora_loaded"), 32)

            def product(h, d, *pairs):
                for s in range(4 * d, 4 * d + 4):
                    lo = hcol(d, h) + (s % 4) * 64
                    for n, (lhs, rhs) in enumerate(pairs):
                        r = C("ident2") if rhs == "eye" else W[rhs][:, s * 64:s * 64 + 64]
                        mm = pe.matmul(PS[:, lo:lo + 64], W[lhs][:, s * 128:s * 128 + 128], r,
                                       start=(n == 0), stop=(n == len(pairs) - 1))
                return mm

            def block_product(b, d, lhs, rhs):
                for s in range(4 * d, 4 * d + 4):
                    lo = (4 * d + b) * BANK + (s % 4) * 128
                    mm = pe.matmul(PS[:, lo:lo + 128], W[lhs][:, s * 128:s * 128 + 128],
                                   W[rhs][:, s * 128:s * 128 + 128], start=True, stop=True)
                return mm

            def two_products(b, d, lhs, both):
                off = at["w7"][0]
                assert at["w8"][0] == off + 512 and STACKED[7:9] == ("al_s", "rt_s")
                rhs = arena[:, off:off + 1024].rearrange("p (a s n) -> p a s n", a=2, n=64)
                for s in range(4 * d, 4 * d + 4):
                    lo = (4 * d + b) * BANK + (s % 4) * 128
                    n = 2 if both else 1
                    mm = pe.matmul(PS[:, lo:lo + 64 * n], W[lhs][:, s * 128:s * 128 + 128], rhs[:, 0:n, s, :],
                                   start=True, stop=True)
                return mm

            def lora_products(g):
                for d in range(2):
                    tok = step_tok(g, d)
                    for j in range(4):
                        c0, c1 = hcol(0, 6 + d) + j * 64, hcol(1, 6 + d) + j * 64
                        pe.matmul(PS[:, c0:c0 + 64], lora[0:64, d, j * P:j * P + P], wal[0:64, tok:tok + 64],
                                  start=True, stop=True)
                        mm = pe.matmul(PS[:, c1:c1 + 64], lora[64:128, d, j * P:j * P + P],
                                       wal[64:128, tok:tok + 64], start=True, stop=True)
                mm.then_inc(sem("lora_done"), 1)

            lora_products(0)
            pe.wait_ge(sem("kksq_ready"), 4)
            for b, t0, n in ((0, 0, 512), (1, 512, 256)):
                for j in range(4):
                    mm = pe.matmul(bank(b, 0, n, (0, 8)), C("headsum", j * 8, 8), kk_sq(j)[:, t0:t0 + n],
                                   start=(j == 0), stop=(j == 3))
            mm.then_inc(stage("kksum_done"), 1)
            pe.wait_ge(*after("kkn_ready"))
            for j in range(4):
                if j >= 2:
                    pe.wait_ge(sem("kk_ready"), j - 1)
                for b, t0, n in ((0, 0, 512), (1, 512, 256)):
                    mm = pe.matmul(bank(4 + b if j % 2 else b, 0, n), C("headspread", j * P, P, (0, 8)),
                                   kkn[0:8, 1, t0:t0 + n], start=True, stop=True)
                mm.then_inc(sem("kk_spread"), 1)
            pe.wait_ge(sem("kk_ready"), 4)
            for g in range(12):
                lat = g >= 4
                pe.wait_ge(sem("blocks_ready"), g + 1)
                for d in range(2):
                    two_products(0, d, "bt", lat).then_inc(sem("ab_done"), 1)
                    product(4, d, ("al", "bt_s"))
                    tok = step_tok(g, d)
                    for j in range(4):
                        for q in range(2):
                            mm = pe.matmul(PS[q * 64:q * 64 + 64, hcol(d, 5) + j * 64:hcol(d, 5) + j * 64 + 64],
                                           vT[q * 64:q * 64 + 64, j, tok:tok + 64],
                                           C("ident2", 0, 64, (q * 64, q * 64 + 64)), start=True, stop=True)
                    mm.then_inc(sem("an_done"), 1)
                    two_products(1, d, "kt", lat).then_inc(sem("ak_done"), 1)
                pe.wait_ge(sem("z_in"), g + 1)
                for d in range(2):
                    if g:
                        pe.wait_ge(sem("s_ready"), 2 * g + d - 1)
                    product(6, d, ("bt", "eye"))
                    product(7, d, ("kt", "eye")).then_inc(sem("rows_done"), 1)
                for d in range(2):
                    pe.wait_ge(sem("rows_ready"), 2 * g + d + 1)
                    pe.wait_ge(sem("ak_ready"), 2 * g + d + 1)
                    product(6, d, ("al", "S"), ("AakT", "vN")).then_inc(sem("r1_done"), 1)
                for lv in range(1, 6):
                    for d in range(2):
                        if lv == 1:
                            pe.wait_ge(sem("x_started"), 2 * g + d + 1)
                        else:
                            pe.wait_ge(sem("x_ready"), 8 * g + 2 * lv + d - 3)
                        block_product(0, d, "AT", "X").then_inc(sem("z_done"), 1)
                    if lv == 1:
                        pe.wait_ge(sem("r1_ready"), 2 * g + 2)
                        if g < 11:
                            lora_products(g + 1)
                    for d in range(2):
                        pe.wait_ge(sem("z_ready"), 10 * g + 2 * lv + d - 1)
                        if lv > 1:
                            pe.wait_ge(sem("xt_ready"), 10 * g + 2 * lv + d - 3)
                        if lv < 5:
                            block_product(1, d, "XT", "Z")
                        block_product(2, d, "Z", "XT").then_inc(sem("dx_done"), 1)
                if g < 11:
                    pe.wait_ge(sem("z_in"), g + 2)
                for d in range(2):
                    pe.wait_ge(sem("xt_ready"), 10 * g + 9 + d)
                    product(6, d, ("XT", "R1")).then_inc(sem("u_done"), 1)
                if lat:
                    pe.wait_ge(sem("rt_block_ready"), g - 3)
                for d in range(2):
                    pe.wait_ge(sem("u_ready"), 2 * g + d + 1)
                    if lat:
                        product(7, d, ("rt", "S"), ("ArkT", "vN"), ("ArbT", "U"))
                    product(6, d, ("kN", "vN"), ("bN", "U")).then_inc(sem("ds_done"), 1)

            pe.wait_ge(sem("gate_loaded"), 16)
            for j in range(4):
                if j >= 2:
                    pe.wait_ge(sem("rw_out"), j - 1)
                A = 3 * (j % 2)
                pe.wait_ge(sem("rk_prod"), j + 1)
                pe.matmul(bank(A + 1), C("blockones"), rk_prod(j), start=True, stop=True)
                pe.matmul(bank(A + 2), T("gateup", j * P, P), gl[:, 0:512], start=True, stop=True)
                pe.wait_ge(*after("yn_ready"))
                for c in range(8):
                    for q in range(2):
                        mm = pe.matmul(bank(A, c * 64, 64, (q * 64, q * 64 + 64)),
                                       yacc[q * 64:q * 64 + 64, j, c, :], C("ident2", 0, 64, (q * 64, q * 64 + 64)),
                                       start=True, stop=True)
                mm.then_inc(sem("rw_cols"), 1)

        def experts_pe(pe):
            u0 = U_EXP
            for kind, e, n in EXP_ORDER:
                if kind == "gu":
                    b = 2 * (e % 2) + n
                    if e >= 2:
                        pe.wait_ge(sem("hid_ready"), 2 * (e - 2) + n + 1)
                    unit_wait(pe, u0)
                    unit_wait(pe, u0 + 1)
                    for k in range(KT):
                        x = xinT[:, k, e * CAP:(e + 1) * CAP]
                        pe.matmul(bank(b, 0, 512, (0, 64)), x, unit(u0)[:, k, :],
                                  start=(k == 0), stop=(k == KT - 1))
                        mm = pe.matmul(bank(b, 0, 512, (64, 128)), x, unit(u0 + 1)[:, k, :],
                                       start=(k == 0), stop=(k == KT - 1))
                    mm.then_inc(sem("gu_done"), 1)
                    u0 += 2
                    continue
                if e >= 1:
                    pe.wait_ge(sem("hidT_ready"), e)
                hid = T("hid", 0, D, (64, 128))
                for f in range(8):
                    if f % 4 == 0:
                        pe.wait_ge(sem("hid_ready"), 2 * e + f // 4 + 1)
                    mm = pe.matmul(bank(4, f * 64, 64), hid[:, f * P:f * P + P], C("ident2", 0, 64, (64, 128)),
                                   start=True, stop=True)
                mm.then_inc(sem("hid_turned"), 1)
                unit_wait(pe, u0)
                unit_wait(pe, u0 + 1)
                pe.wait_ge(sem("hidT_ready"), e + 1)
                if e >= 1:
                    pe.wait_ge(sem("y_left"), e)
                hidT = T("hidT", (e % 2) * 512, 512).rearrange("p (f c) -> p f c", c=64)
                for f in range(8):
                    pe.matmul(bank(5, 0, 512, (0, 64)), hidT[:, f, :], unit(u0)[:, f, :],
                              start=(f == 0), stop=(f == 7))
                    mm = pe.matmul(bank(5, 0, 512, (64, 128)), hidT[:, f, :], unit(u0 + 1)[:, f, :],
                                   start=(f == 0), stop=(f == 7))
                mm.then_inc(sem("down_done"), 1)
                u0 += 2
                if e % 2:
                    p2 = e // 2
                    pe.wait_ge(sem("y_left"), e + 1)
                    yp = T("ypair", (p2 % 2) * D, D)
                    for t in range(4):
                        for n in range(2):
                            i = p2 * 8 + t * 2 + n
                            if i >= 2:
                                pe.wait_ge(sem("added"), i - 1)
                            pe.matmul(bank(6 + i % 2), hotT[:, p2, t * P:t * P + P], yp[:, n * 512:n * 512 + 512],
                                      start=True, stop=True).then_inc(sem("scattered"), 1)

        def rwkv_dve(dve, link):
            kk_k = VEC["k_k"][0]
            for j in range(4):
                link(dve.tensor_scalar(kkT[:, j, :], kT[:, j, :], T("vec", kk_k + j, 1), None, ALU.mult))
                dve.tensor_tensor(kk_sq(j), kkT[:, j, :], kkT[:, j, :], ALU.mult).then_inc(sem("kksq_ready"), 1)

            def add_offsets(g):
                dve.wait_ge(sem("lora_done"), g + 1)
                for d in range(2):
                    dve.tensor_tensor(by("sg", d), hb(0, 6 + d), bc(T("vec", VEC["w0"][0] + 4 * d, 4), 64), ALU.add)
                    ins = dve.tensor_tensor(by("a", d), hb(1, 6 + d), bc(T("vec", VEC["a0"][0] + 4 * d, 4), 64), ALU.add)
                ins.then_inc(sem("z_in"), 1)

            def running_sums(g):
                dve.wait_ge(sem("tanh_done"), g + 1)
                dve.tensor_scalar(W["sg"], W["sg"], 0.5, 0.5, ALU.mult, ALU.add).then_inc(sem("sg_ready"), 1)
                dve.wait_ge(sem("sg_ready"), g + 1)
                dve.tensor_tensor_scan(W["P"][:, 0:256], C("seg", 0, 256), W["sg"][:, 0:256], 0.0, ALU.mult, ALU.add)
                dve.tensor_tensor_scan(W["P"][:, 256:512][:, ::-1], C("seg", 256, 256)[:, ::-1],
                                       W["sg"][:, 256:512][:, ::-1], 0.0, ALU.mult, ALU.add)\
                    .then_inc(sem("p_ready"), 1)
                dve.wait_ge(sem("p_ready"), g + 1)
                dve.tensor_tensor(W["Ee"], W["P"], W["sg"], ALU.subtract).then_inc(sem("ex_ready"), 1)

            def decayed(g):
                dve.wait_ge(sem("e_ready"), g + 1)
                for d in range(2):
                    tok = step_tok(g, d)
                    ins = dve.scalar_tensor_tensor(out=by("al_s", d), in0=kkT[:, :, tok:tok + 64], scalar=-1.0,
                                                   in1=by("Ee", d), op0=ALU.mult, op1=ALU.mult)
                if g >= 4:
                    if g >= 5:
                        dve.wait_ge(sem("rt_block_ready"), g - 4)
                    for d in range(2):
                        tok = step_tok(g, d) - CTX
                        ins = dve.tensor_tensor(by("rt_s", d), rT[:, :, tok:tok + 64], by("Ei", d), ALU.mult)
                ins.then_inc(sem("rt_ready"), 1)

            dve.wait_ge(*after("kkroot"))
            link(dve.tensor_scalar(kkn[0:8, 0, :], kkn[0:8, 0, :], L2_EPS, None, ALU.max))
            dve.reciprocal(kkn[0:8, 1, :], kkn[0:8, 0, :]).then_inc(stage("kkn_ready"), 1)
            add_offsets(0)
            for j in range(4):
                dve.wait_ge(sem("kk_spread"), j + 1)
                A = 4 * (j % 2) * BANK
                dve.tensor_tensor(kkT[:, j, :], kkT[:, j, :], PS[:, A:A + 768], ALU.mult).then_inc(sem("kk_ready"), 1)
            running_sums(0)
            decayed(0)
            dve.wait_ge(sem("blocks_clear"), 1)
            for g in range(12):
                lat = g >= 4
                for d in range(2):
                    dve.wait_ge(sem("at_ready"), 2 * g + d + 1)
                    for q in range(2):
                        rows = slice(q * 64, q * 64 + 64)
                        dve.tensor_tensor(diag("XT", d, q), wide(d, 0)[rows, :, 0:64], mask("level", d)[rows],
                                          ALU.mult)
                        if lat:
                            dve.tensor_tensor(diag("ArbT", d, q), wide(d, 0)[rows, :, 64:128],
                                              mask("incl", d)[rows], ALU.mult)
                    dve.wait_ge(sem("an_done"), 2 * g + d + 1)
                    for q in range(2):
                        rows = slice(q * 64, q * 64 + 64)
                        ins = dve.tensor_tensor(diag("X", d, q), hq(d, 4, q), mask("pair0", d)[rows], ALU.mult)
                    ins.then_inc(sem("x0_ready"), 1)
                    dve.wait_ge(sem("ak_done"), 2 * g + d + 1)
                    for q in range(2):
                        rows = slice(q * 64, q * 64 + 64)
                        ins = dve.tensor_tensor(diag("AakT", d, q), wide(d, 1)[rows, :, 0:64],
                                                mask("strict", d)[rows], ALU.mult)
                        if lat:
                            ins = dve.tensor_tensor(diag("ArkT", d, q), wide(d, 1)[rows, :, 64:128],
                                                    mask("incl", d)[rows], ALU.mult)
                    ins.then_inc(sem("ak_ready"), 1)
                for lv in range(1, 6):
                    for d in range(2):
                        dve.wait_ge(sem("z_done"), 10 * g + 2 * lv + d - 1)
                        m = C("levelT", lv * 128 + d * 64, 64).unsqueeze(1).broadcast_to([P, 8, 64])
                        dve.tensor_tensor(W["Z"][:, d * 512:d * 512 + 512].rearrange("p (a n) -> p a n", n=64),
                                          bank(4 * d).rearrange("p (a n) -> p a n", n=64), m, ALU.mult)\
                            .then_inc(sem("z_ready"), 1)
                    if g < 11 and lv == 1:
                        add_offsets(g + 1)
                    if g < 11 and lv == 2:
                        running_sums(g + 1)
                    if g < 11 and lv == 3:
                        decayed(g + 1)
                    for d in range(2):
                        sl = slice(d * 512, d * 512 + 512)
                        dve.wait_ge(sem("dx_done"), 10 * g + 2 * lv + d - 1)
                        if lv < 5:
                            dve.tensor_tensor(W["X"][:, sl], W["X"][:, sl], bank(4 * d + 1), ALU.add)\
                                .then_inc(sem("x_ready"), 1)
                        dve.tensor_tensor(W["XT"][:, sl], W["XT"][:, sl], bank(4 * d + 2), ALU.add)\
                            .then_inc(sem("xt_ready"), 1)
                for d in range(2):
                    dve.wait_ge(sem("ds_done"), 2 * g + d + 1)
                    dve.tensor_tensor(by("S", d), by("S", d), hb(d, 6), ALU.add).then_inc(sem("s_summed"), 1)
                    if lat:
                        if g > 4 or d:
                            dve.wait_ge(sem("y_added"), 2 * (g - 4) + d)
                        y = yacc[:, :, (step_tok(g, d) - CTX) // 64, :]
                        dve.tensor_tensor(y, y, hb(d, 7), ALU.add).then_inc(sem("y_added"), 1)
                    dve.wait_ge(sem("s_summed"), 2 * g + d + 1)
                    dve.wait_ge(sem("wc_ready"), g + 1)
                    dve.tensor_tensor(by("S", d), by("S", d), bc(wcs[g % 2][:, 4 * d:4 * d + 4], 64),
                                      ALU.mult).then_inc(sem("s_ready"), 1)
            dve.wait_ge(sem("s_ready"), 24)
            for j in range(4):
                dve.scalar_tensor_tensor(out=rk_prod(j), in0=rT[:, j, :], scalar=T("vec", VEC["r_k"][0] + j, 1),
                                         in1=kT[:, j, CTX:TOK2], op0=ALU.mult, op1=ALU.mult)\
                    .then_inc(sem("rk_prod"), 1)
            y3 = T("yacc").rearrange("p (s n) -> p s n", n=64)
            link(dve.tensor_reduce(yst, y3, AX, ALU.add))
            link(dve.tensor_scalar(yst, yst, -1.0 / 64, None, ALU.mult))
            link(dve.tensor_tensor(y3, y3, bc(yst, 64), ALU.add))
            sq = kk_sq_all(2048)
            link(dve.tensor_tensor(sq, T("yacc"), T("yacc"), ALU.mult))
            link(dve.tensor_reduce(yvar, sq.rearrange("p (s n) -> p s n", n=64), AX, ALU.add))
            dve.tensor_scalar(yvar, yvar, 1.0 / 64, GN_EPS, ALU.mult, ALU.add).then_inc(stage("yvar_ready"), 1)
            dve.wait_ge(*after("ystd_ready"))
            link(dve.reciprocal(yst, ystd))
            dve.tensor_tensor(y3, y3, bc(yst, 64), ALU.mult).then_inc(stage("yn_ready"), 1)
            for j in range(4):
                A = 3 * (j % 2)
                dve.wait_ge(sem("rw_cols"), j + 1)
                link(dve.tensor_tensor(W["rt_s"], vT[:, j, CTX:TOK2], bank(A + 1), ALU.mult))
                dve.wait_ge(sem("yn_affine"), j + 1)
                link(dve.tensor_tensor(rwT[:, j, :], rwT[:, j, :], W["rt_s"], ALU.add))
                dve.tensor_tensor(rwT[:, j, :], rwT[:, j, :], bank(A + 2), ALU.mult).then_inc(sem("rw_out"), 1)


        @block.tensor
        def _(pe):
            pe.wait_ge(sem("const_loaded"), 16)
            for t in range(5):
                pe.wait_ge(sem("x_scaled"), t + 1)
            for k in range(KT):
                if k >= 4:
                    pe.wait_ge(sem("xT_dve" if k % 2 == 0 else "xT_act"), (k - 4) // 2 + 1)
                A = 2 * (k % 4)
                for t in range(4):
                    pe.transpose(bank(A, t * P, P), xin[:, t, k * P:k * P + P], ident)
                pe.transpose(bank(A + 1, 0, META), xin[0:META, 4, k * P:k * P + P], ident[0:META, 0:META])\
                    .then_inc(sem("x_turned"), 1)
            phase_end(pe)
            jobs_pe(pe, PROJ1)
            phase_end(pe)
            att_pe(pe, "fox", 0)
            phase_end(pe)

            pe.wait_ge(*after("cq_scaled"))
            for k in range(2):
                for t in range(4):
                    pe.transpose(bank(k, t * P, P), cqkv[:, t, k * P:k * P + P], ident)
            krow = T("krow").rearrange("p (t n) -> p t n", n=32)
            for t in range(5):
                n = META if t == 4 else P
                b, c = (1, 0) if t == 4 else (0, t * P)
                pe.transpose(bank(2 + b, c, n), cqkv[0:n, t, 256:384], ident[0:n, 0:n])
                mm = pe.transpose(bank(4 + b, c, n, (0, 32)), krow[0:n, t, :], ident[0:n, 0:n])
            mm.then_inc(stage("cq_turned"), 1)
            pe.wait_ge(*after("cqT_ready"))
            jobs_pe(pe, MLAPREP)
            n0 = [n for n, j in enumerate(JOBS) if j[0] == MLAPREP]
            for n in n0[-4:]:
                e, c = emptied(n)
                pe.wait_ge(sem("slot_dve" if e == "d" else "slot_act"), c)
            pe.wait_ge(sem("q_roped"), 4)
            for h in range(H):
                for t in range(4):
                    mm = pe.transpose(bank(h, t * P, P, (0, QK)), qrow[:, t, h * QK:h * QK + QK], ident)
                mm.then_inc(sem("q_turned"), 1)
            phase_end(pe)
            att_pe(pe, "mla", 32)
            phase_end(pe)

            for k in range(8):
                for t in range(4):
                    mm = pe.transpose(bank(k, t * P, P), mixR[:, t, k * P:k * P + P], ident)
                mm.then_inc(sem("mix_turned"), 1)
            pe.wait_ge(sem("mixT_dve"), 4)
            pe.wait_ge(sem("mixT_act"), 4)
            for n in range(2):
                unit_wait(pe, U_OUT + n)
                for t in range(4):
                    for k in range(KT):
                        mm = pe.matmul(bank(2 * t + n), mixT[:, k, t * P:t * P + P], unit(U_OUT + n)[:, k, :],
                                       start=(k == 0), stop=(k == KT - 1))
                mm.then_inc(sem("y_done"), 1)
            phase_end(pe)

            pe.wait_ge(sem("h_normed"), 6)
            for k in range(KT):
                A = 2 * (k % 3)
                if k >= 3:
                    pe.wait_ge(sem("hT_ready"), k - 2)
                for t in range(6):
                    dst = bank(A, t * P, P) if t < 2 else bank(A + 1, (t - 2) * P, P)
                    mm = pe.transpose(dst, lnx[:, t, k * P:k * P + P], ident)
                mm.then_inc(sem("h_turned"), 1)
            phase_end(pe)

            jobs_pe(pe, PROJ2)
            for n in range(len(JOBS) - 4, len(JOBS)):
                pe.wait_ge(sem("slot_act"), emptied(n)[1])
            for t in range(6):
                pe.wait_ge(sem("qk_roped"), t + 1)
                if t >= 2:
                    pe.wait_ge(sem("qkT_ready"), t - 1)
                b = t % 2
                mm = pe.transpose(bank(b, 0, P), gkv[:, t, 0:P], ident)
                if t >= 2:
                    for j in range(4):
                        mm = pe.transpose(bank(2 + b, j * P, P), qn(t - 2)[:, j * P:j * P + P], ident)
                mm.then_inc(sem("qk_turned"), 1)
            phase_end(pe)
            att_pe(pe, "gqa", 64)
            phase_end(pe)

            rwkv_pe(pe)
            phase_end(pe)

            for k in range(4):
                for t in range(4):
                    mm = pe.transpose(bank(k, t * P, P), mixG[:, t, k * P:k * P + P], ident)
            mm.then_inc(stage("mix2_turned"), 1)
            pe.wait_ge(*after("mixT2_ready"))
            for c in range(8):
                mm = pe.matmul(bank(c // 4, (c % 4) * P, P), mod[:, 16 + c, 0:1].broadcast_to([P, P]), ident,
                               start=True, stop=True)
            mm.then_inc(stage("gt1_rep"), 1)
            pe.wait_ge(*after("gt1_ready"))
            for n in range(2):
                unit_wait(pe, U_OUT2 + n)
                for t in range(4):
                    for k in range(KT):
                        lhs = mixT2[:, k, t * P:t * P + P] if k < 4 else rwT[:, k - 4, t * P:t * P + P]
                        mm = pe.matmul(bank(2 * t + n), lhs, unit(U_OUT2 + n)[:, k, :],
                                       start=(k == 0), stop=(k == KT - 1))
                mm.then_inc(sem("y2_done"), 1)
            phase_end(pe)

            pe.wait_ge(sem("xn_ready"), 4)
            for k in range(KT):
                if k >= 6:
                    pe.wait_ge(sem("h2T_ready"), k - 5)
                for t in range(4):
                    mm = pe.transpose(bank(k % 6, t * P, P), xn[:, t, k * P:k * P + P], ident)
                mm.then_inc(sem("h2_turned"), 1)
            pe.wait_ge(sem("h2T_ready"), 8)
            pe.wait_ge(sem("router_loaded"), 16)
            for t in range(4):
                for k in range(KT):
                    mm = pe.matmul(bank(7, t * EXP, EXP), h2T[:, k, t * P:t * P + P], router[:, k, :],
                                   start=(k == 0), stop=(k == KT - 1))
            mm.then_inc(stage("logits_done"), 1)
            for c in range(8):
                mm = pe.matmul(bank(4 + c // 4, (c % 4) * P, P), mod[:, 40 + c, 0:1].broadcast_to([P, P]), ident,
                               start=True, stop=True)
            mm.then_inc(stage("gt2_rep"), 1)
            pe.wait_ge(*after("aff_ready"))
            for t in range(4):
                mm = pe.transpose(bank(0, t * P, P, (0, EXP)), aff[:, t, :], ident)
            mm.then_inc(stage("aff_turned"), 1)
            pe.wait_ge(*after("rank_ready"))
            for t in range(4):
                mm = pe.transpose(bank(1, t * EXP, EXP), T("affT", 0, 2048, (0, EXP))[:, 512 + t * P:512 + t * P + P],
                                  ident[0:EXP, 0:EXP])
            mm.then_inc(stage("rank_turned"), 1)
            phase_end(pe)
            for k in range(KT):
                for eh in range(2):
                    n = 2 * k + eh
                    if n >= 6:
                        pe.wait_ge(sem("gather_dve" if n % 2 == 0 else "gather_act"), (n - 6) // 2 + 1)
                    for t in range(4):
                        mm = pe.matmul(bank(n % 6), xn[:, t, k * P:k * P + P], hot[:, t, eh * 512:eh * 512 + 512],
                                       start=(t == 0), stop=(t == 3))
                    mm.then_inc(sem("gathered"), 1)
                if k % 2:
                    t = k // 2
                    pe.wait_ge(sem("hotg_ready"), t + 1)
                    if t >= 1:
                        pe.wait_ge(sem("hotT_ready"), t)
                    for e in range(8):
                        mm = pe.transpose(bank(6 + e // 4, (e % 4) * P, P), T("hotg", e * P, P), ident)
                    mm.then_inc(sem("hot_turned"), 1)
            phase_end(pe)
            experts_pe(pe)
            phase_end(pe)


        @block.scalar
        def _(act):
            link = chain(act, "act_chain")
            act.wait_ge(sem("x_loaded"), 16)
            act.wait_ge(sem("meta_loaded"), 16)
            act.wait_ge(*after("small_clear"))
            stats_act(act, link, "xs", [(xin[:, t, :], P) for t in range(4)] + [(xin[0:META, 4, :], META)],
                      False, "junk")
            act.wait_ge(sem("vec_loaded"), 16)
            act.wait_ge(*after("csil_clear"))
            act.activation(csil[:, :, 0:2], T("vec", VEC["cvec"][0], 16).rearrange("p (k v) -> p k v", v=2), ACT.Silu)
            g = T("vec", VEC["norm_pre"][0], 8)
            for k in range(1, KT, 2):
                act.wait_ge(sem("x_turned"), k + 1)
                A = 2 * (k % 4)
                act.activation(xT[:, k, 0:512], bank(A), ACT.Copy, scale=g[:, k:k + 1])
                act.activation(xT[:, k, 512:528], bank(A + 1, 0, META), ACT.Copy, scale=g[:, k:k + 1])\
                    .then_inc(sem("xT_act"), 1)
            phase_end(act)
            jobs_empty(act, "a", PROJ1)
            act.wait_ge(*after("flog_ready"))
            z = T("cum", 0, 528, (0, 8))
            lz = T("junk", 0, 528, (0, 8))
            link(act.activation(lz, z, ACT.Abs))
            link(act.activation(lz, lz, ACT.Exp, scale=-1.0))
            act.activation(lz, lz, ACT.Ln, bias=1.0).then_inc(stage("logf_ready"), 1)
            phase_end(act)
            att_act(act, "fox", 0, FOX_SCALE)
            phase_end(act)
            for t in range(4):
                link(act.activation(T("junk", 0, 256), cqkv[:, t, 0:256], ACT.Square, accum_out=mss[:, t:t + 1]))
            for t in range(5):
                n = META if t == 4 else P
                link(act.activation(T("junk", 0, 128, (0, n)), cqkv[0:n, t, 256:384], ACT.Square,
                                    accum_out=mss[0:n, 5 + t:6 + t]))
            act.sem_inc(stage("mss_ready"), 1)
            act.wait_ge(*after("mvar_ready"))
            act.activation(mstd, mss, ACT.Sqrt).then_inc(stage("mstd_ready"), 1)
            jobs_empty(act, "a", MLAPREP)
            act.wait_ge(sem("slot_act"), sum(j[3] == "a" for j in JOBS if j[0] <= MLAPREP))
            for h in range(H):
                act.wait_ge(sem("q_turned"), h + 1)
                act.activation(mqT[0:QK, h, :], bank(h, 0, 512, (0, QK)), ACT.Copy)
            phase_end(act)
            att_act(act, "mla", 32, MLA_SCALE)
            phase_end(act)

            for k in range(1, 8, 2):
                act.wait_ge(sem("mix_turned"), k + 1)
                act.activation(mixT[:, k, :], bank(k), ACT.Copy).then_inc(sem("mixT_act"), 1)
            act.wait_ge(sem("y_done"), 2)
            stats_act(act, link, "ys", [(PS[:, t * 1024:t * 1024 + 1024], P) for t in range(4)], False, "junk")
            for t in range(4):
                act.wait_ge(sem("x1_ready"), t + 1)
            act.dma_start(x1_dram, T("xres")).then_inc(sem("x1_saved"), 16)
            phase_end(act)

            act.wait_ge(sem("ctx_loaded"), 16)
            stats_act(act, link, "hs", [(ctxr[:, t, :], P) for t in range(2)] + [(xres[:, t, :], P) for t in range(4)],
                      True, "junk")
            act.wait_ge(sem("x1_saved"), 16)
            phase_end(act)
            def root_of_heads(name, i):
                if (name, i) == ("rw", 0):
                    act.wait_ge(*after("gvar_ready"))
                    act.activation(gstd, gss, ACT.Sqrt).then_inc(stage("gstd_ready"), 1)
            jobs_empty(act, "a", PROJ2, root_of_heads)
            act.wait_ge(sem("shifted"), 14)
            act.activation(wal[0:64, :], wal[0:64, :], ACT.Tanh).then_inc(sem("wal_ready"), 1)
            act.activation(gl[:, 0:512], gl[:, 0:512], ACT.Sigmoid).then_inc(sem("wal_ready"), 1)
            for t in range(6):
                act.wait_ge(sem("qk_turned"), t + 1)
                b = t % 2
                ins = act.activation(T("gkT", t * P, P), bank(b, 0, P), ACT.Copy)
                if t >= 2:
                    for gg in range(2):
                        lo = gg * 64
                        ins = act.activation(gqT[lo:lo + 64, 4 * gg:4 * gg + 4, (t - 2) * P:(t - 1) * P],
                                             bank(2 + b, 0, 512, (lo, lo + 64)).rearrange("p (j t) -> p j t", j=4),
                                             ACT.Copy)
                ins.then_inc(sem("qkT_ready"), 1)
            phase_end(act)
            att_act(act, "gqa", 64, GQA_SCALE)
            phase_end(act)

            act.wait_ge(*after("kksum_done"))
            act.activation(kkn[0:8, 0, :], PS[0:8, 0:768], ACT.Sqrt).then_inc(stage("kkroot"), 1)
            def exponentials(g):
                act.wait_ge(sem("z_in"), g + 1)
                act.activation(W["a"], W["a"], ACT.Tanh, scale=0.5)
                act.activation(W["sg"], W["sg"], ACT.Tanh, scale=0.5).then_inc(sem("tanh_done"), 1)
                act.wait_ge(sem("p_ready"), g + 1)
                act.activation(W["Ei"], W["P"], ACT.Exp, scale=-DECAY)
                act.activation(W["Ev"], W["P"], ACT.Exp, scale=DECAY)
                act.wait_ge(sem("ex_ready"), g + 1)
                act.activation(W["Ee"], W["Ee"], ACT.Exp, scale=-DECAY).then_inc(sem("e_ready"), 1)

            def spread(name, src):
                for q in range(2):
                    ins = act.activation(block_all(name, q), part(src, q), ACT.Copy)
                return ins

            def spread_factors(g):
                act.wait_ge(sem("rt_ready"), g + 1)
                spread("al", "al_s")
                act.wait_ge(sem("eb_ready"), g + 1)
                spread("bt", "bt_s")
                spread("kt", "kd").then_inc(sem("blocks_ready"), 1)

            exponentials(0)
            act.wait_ge(sem("blocks_clear"), 1)
            spread_factors(0)
            for g in range(12):
                for d in range(2):
                    act.wait_ge(sem("ab_done"), 2 * g + d + 1)
                    for q in range(2):
                        ins = act.activation(diag("AT", d, q), wide(d, 0)[q * 64:q * 64 + 64, :, 0:64], ACT.Copy)
                    ins.then_inc(sem("at_ready"), 1)
                if g >= 4:
                    act.wait_ge(sem("ds_done"), 2 * g)
                    spread("rt", "rt_s").then_inc(sem("rt_block_ready"), 1)
                for d in range(2):
                    act.wait_ge(sem("rows_done"), 2 * g + d + 1)
                    for q in range(2):
                        act.activation(diag("bN", d, q), hq(d, 6, q), ACT.Copy)
                        act.activation(diag("kN", d, q), hq(d, 7, q), ACT.Copy)
                    act.wait_ge(sem("x0_ready"), 2 * g + d + 1)
                    act.activation(by("vN", d), hb(d, 5), ACT.Copy).then_inc(sem("rows_ready"), 1)
                for d in range(2):
                    act.wait_ge(sem("r1_done"), 2 * g + d + 1)
                    act.activation(by("R1", d), hb(d, 6), ACT.Copy).then_inc(sem("r1_ready"), 1)
                if g < 11:
                    exponentials(g + 1)
                    spread_factors(g + 1)
                for d in range(2):
                    act.wait_ge(sem("u_done"), 2 * g + d + 1)
                    act.activation(by("U", d), hb(d, 6), ACT.Copy).then_inc(sem("u_ready"), 1)
            act.wait_ge(*after("yvar_ready"))
            act.activation(ystd, yvar, ACT.Sqrt).then_inc(stage("ystd_ready"), 1)
            for j in range(4):
                act.wait_ge(sem("rw_cols"), j + 1)
                act.activation(rwT[:, j, :], bank(3 * (j % 2)), ACT.Identity, scale=T("vec", VEC["lnx_g"][0] + j, 1),
                               bias=T("vec", VEC["lnx_b"][0] + j, 1)).then_inc(sem("yn_affine"), 1)
            phase_end(act)

            act.dma_start(T("x2"), x1_dram).then_inc(sem("x1_back"), 16)
            act.dma_start(T("ln1"), w["ln1"].broadcast_to([P, 2 * D])).then_inc(sem("ln1_loaded"), 16)
            act.wait_ge(*after("mix2_turned"))
            act.activation(T("mixT2"), PS[:, 0:2048], ACT.Copy).then_inc(stage("mixT2_ready"), 1)
            act.wait_ge(*after("gt1_rep"))
            act.activation(T("grow"), PS[:, 0:1024], ACT.Copy).then_inc(stage("gt1_ready"), 1)
            stats_act(act, link, "z1", [(x2[:, t, :], P) for t in range(4)], True, "junk2")
            phase_end(act)

            act.dma_start(T("router"), w["router_w_2"][0].rearrange("(k p) e -> p k e", p=P))\
                .then_inc(sem("router_loaded"), 16)
            stats_act(act, link, "f", [(x2[:, t, :], P) for t in range(4)], True, "junk2")
            act.wait_ge(*after("gt2_rep"))
            act.activation(T("grow2"), PS[:, 4 * BANK:6 * BANK], ACT.Copy).then_inc(stage("gt2_ready"), 1)
            act.wait_ge(*after("logits_in"))
            act.activation(T("aff"), T("aff"), ACT.Exp).then_inc(stage("aff_exp"), 1)
            phase_end(act)
            for k in range(KT):
                act.wait_ge(sem("gathered"), 2 * k + 2)
                act.activation(xinT[:, k, 512:1024], bank((2 * k + 1) % 6), ACT.Identity,
                               scale=omsc[:, 16 + k:17 + k], bias=mod[:, 24 + k, 0:1]).then_inc(sem("gather_act"), 1)
                if k % 2:
                    t = k // 2
                    act.wait_ge(sem("hot_turned"), t + 1)
                    act.activation(hotT[:, :, t * P:t * P + P],
                                   PS[:, 6 * BANK:8 * BANK].rearrange("p (e t) -> p e t", t=P), ACT.Copy)\
                        .then_inc(sem("hotT_ready"), 1)
            phase_end(act)
            for e in range(EXP):
                for n in range(2):
                    act.wait_ge(sem("gu_done"), 2 * e + n + 1)
                    if e >= 1:
                        act.wait_ge(sem("hid_ready"), 2 * (e - 1) + n + 1)
                    act.activation(T("sg", n * 512, 512, (64, 128)), bank(2 * (e % 2) + n, 0, 512, (0, 64)), ACT.Silu)\
                        .then_inc(sem("silu_done"), 1)
                act.wait_ge(sem("hid_turned"), e + 1)
                act.activation(T("hidT", (e % 2) * 512, 512), bank(4), ACT.Copy).then_inc(sem("hidT_ready"), 1)
            phase_end(act)
            act.dma_start(T("ln2"), w["ln2"].broadcast_to([P, 2 * D])).then_inc(sem("ln2_loaded"), 16)
            stats_act(act, link, "o", [(x2[:, t, :], P) for t in range(4)], True, "junk2")
            for t in range(4):
                act.wait_ge(sem("out_ready"), t + 1)
                act.dma_start(out[0, t * P:(t + 1) * P, :], x2[:, t, :]).then_inc(sem("out_stored"), 16)
            act.wait_ge(sem("out_stored"), 64)

        @block.vector
        def _(dve):
            link = chain(dve, "dve_chain")
            dve.memset(T("small"), 1.0).then_inc(stage("small_clear"), 1)
            dve.memset(T("csil"), 0.0).then_inc(stage("csil_clear"), 1)
            stats_dve(dve, link, "xs", 5, False, EPS1)
            for t in range(5):
                n = META if t == 4 else P
                dve.tensor_scalar(xin[0:n, t, :], xin[0:n, t, :], st_rstd[0:n, t:t + 1], None, ALU.mult)\
                    .then_inc(sem("x_scaled"), 1)
            dve.wait_ge(sem("vec_loaded"), 16)
            g = T("vec", VEC["norm_pre"][0], 8)
            for k in range(0, KT, 2):
                dve.wait_ge(sem("x_turned"), k + 1)
                A = 2 * (k % 4)
                dve.tensor_scalar(xT[:, k, 0:512], bank(A), g[:, k:k + 1], None, ALU.mult)
                dve.tensor_scalar(xT[:, k, 512:528], bank(A + 1, 0, META), g[:, k:k + 1], None, ALU.mult)\
                    .then_inc(sem("xT_dve"), 1)
            phase_end(dve)
            jobs_empty(dve, "d", PROJ1)
            z = T("cum", 0, 528, (0, 8))
            dve.wait_ge(sem("slot_dve"), sum(j[3] == "d" for j in JOBS if j[0] <= PROJ1))
            dve.tensor_scalar(z, z, T("vec", VEC["b_f"][0], 1, (0, 8)), None, ALU.add).then_inc(stage("flog_ready"), 1)
            dve.wait_ge(*after("logf_ready"))
            logf = T("junk", 0, 528, (0, 8))
            link(dve.scalar_tensor_tensor(out=logf, in0=z, scalar=0.0, in1=logf, op0=ALU.min, op1=ALU.subtract))
            zero = T("junk", 528, 496, (0, 8))
            link(dve.memset(T("junk", 528, 496, (0, 8)), 0.0))
            cumt = T("fox_cum", 0, 528, (0, 8))
            link(dve.tensor_tensor_scan(cumt[:, 0:264], logf[:, 0:264], zero[:, 0:264], 0.0, ALU.add, ALU.add))
            link(dve.tensor_tensor_scan(cumt[:, 264:528], logf[:, 264:528], zero[:, 0:264], cumt[:, 263:264],
                                        ALU.add, ALU.add))
            dve.tensor_scalar(T("cum", 0, 512, (0, 8)), cumt[:, META:528], -1.0 / FOX_SCALE, None, ALU.mult)
            dve.tensor_scalar(T("cum", 512, META, (0, 8)), cumt[:, 0:META], -1.0 / FOX_SCALE, None, ALU.mult)\
                .then_inc(sem("cum_ready"), 1)
            phase_end(dve)
            att_dve(dve, link, "fox", 0, FOX_SCALE, mixR[:, :, 0:512], fgate)
            dve.tensor_scalar(omsc[:, 0:8], mod[:, 8:16, 0], 1.0, None, ALU.add)
            dve.tensor_scalar(omsc[:, 8:16], mod[:, 8:16, 1], 1.0, None, ALU.add)
            dve.tensor_scalar(omsc[:, 16:24], mod[:, 32:40, 0], 1.0, None, ALU.add)
            phase_end(dve)

            dve.wait_ge(*after("mss_ready"))
            dve.tensor_scalar(mss[:, 0:5], mss[:, 0:5], 1.0 / 256, EPS1, ALU.mult, ALU.add)
            dve.tensor_scalar(mss[:, 5:10], mss[:, 5:10], 1.0 / 128, EPS1, ALU.mult, ALU.add)\
                .then_inc(stage("mvar_ready"), 1)
            mcos = C("mcos").rearrange("p (t n) -> p t n", n=16)
            msin = C("msin").rearrange("p (t n) -> p t n", n=16)
            krow = T("krow").rearrange("p (t n) -> p t n", n=32)
            tmp = T("rtmp")

            def rope(x1, x2, c, s, o1, o2, shape):
                n = 1
                for a in shape:
                    n *= a
                t = []
                for i in range(4):
                    v = tmp_rope[0][:, i * n:(i + 1) * n]
                    if len(shape) == 2:
                        v = v.rearrange("p (a b) -> p a b", a=shape[0])
                    if len(shape) == 3:
                        v = v.rearrange("p (a b c) -> p a b c", a=shape[0], b=shape[1])
                    t.append(v[0:x1.shape[0]])
                dve.tensor_tensor(t[0], x1, c, ALU.mult)
                dve.tensor_tensor(t[1], x2, s, ALU.mult)
                dve.tensor_tensor(t[2], x1, s, ALU.mult)
                link(dve.tensor_tensor(t[3], x2, c, ALU.mult))
                dve.tensor_tensor(o1, t[0], t[1], ALU.subtract)
                return dve.tensor_tensor(o2, t[2], t[3], ALU.add)

            tmp_rope = [tmp]
            for lo, hi, n in ((0, 4, P), (4, 5, META)):
                kr = cqkv[0:n, lo:hi, 384:416]
                link(rope(kr[:, :, 0:16], kr[:, :, 16:32], mcos[0:n, lo:hi, :], msin[0:n, lo:hi, :],
                          krow[0:n, lo:hi, 0:16], krow[0:n, lo:hi, 16:32], (hi - lo, 16)))
            dve.wait_ge(*after("mstd_ready"))
            link(dve.reciprocal(mrs, mstd))
            for t in range(5):
                n = META if t == 4 else P
                if t < 4:
                    dve.tensor_scalar(cqkv[:, t, 0:256], cqkv[:, t, 0:256], mrs[:, t:t + 1], None, ALU.mult)
                ins = dve.tensor_scalar(cqkv[0:n, t, 256:384], cqkv[0:n, t, 256:384], mrs[0:n, 5 + t:6 + t], None,
                                        ALU.mult)
            ins.then_inc(stage("cq_scaled"), 1)
            dve.wait_ge(*after("cq_turned"))
            qg, kg = T("vec", VEC["q_norm"][0], 2), T("vec", VEC["kv_norm"][0], 1)
            for k in range(2):
                dve.tensor_scalar(cqT[:, k, :], bank(k), qg[:, k:k + 1], None, ALU.mult)
            dve.tensor_scalar(T("ckvT", 0, 512), bank(2), kg, None, ALU.mult)
            dve.tensor_scalar(T("ckvT", 512, META), bank(3, 0, META), kg, None, ALU.mult)
            dve.tensor_copy(T("krT", 0, 512, (0, 32)), bank(4, 0, 512, (0, 32)))
            dve.tensor_copy(T("krT", 512, META, (0, 32)), bank(5, 0, META, (0, 32))).then_inc(stage("cqT_ready"), 1)

            def rope_q(name, i):
                dve.wait_ge(sem("slot_dve"), emptied([n for n, j in enumerate(JOBS) if j[1:3] == (name, i)][0])[1])
                q = qrow[:, i, :].rearrange("p (h n) -> p h n", n=QK)
                c, s = rep(mcos[:, i, :], 8), rep(msin[:, i, :], 8)
                rope(q[:, :, 64:80], q[:, :, 80:96], c, s, q[:, :, 64:80], q[:, :, 80:96], (8, 16))\
                    .then_inc(sem("q_roped"), 1)
                dve.wait_ge(sem("q_roped"), i + 1)
            jobs_empty(dve, "d", MLAPREP, rope_q)
            dve.wait_ge(*after("cqT_ready"))
            for h in range(H):
                dve.tensor_copy(mkT[64:96, h, :], T("krT", 0, 528, (0, 32)))
            phase_end(dve)
            att_dve(dve, link, "mla", 32, MLA_SCALE, mixR[:, :, 512:1024], mgate)
            phase_end(dve)

            for k in range(0, 8, 2):
                dve.wait_ge(sem("mix_turned"), k + 1)
                dve.tensor_copy(mixT[:, k, :], bank(k)).then_inc(sem("mixT_dve"), 1)
            stats_dve(dve, link, "ys", 4, False, EPS1)
            dve.wait_ge(sem("xres_loaded"), 16)
            dve.wait_ge(sem("npost_loaded"), 16)
            for t in range(4):
                link(dve.scalar_tensor_tensor(out=ytmp[:, t % 2, :], in0=PS[:, t * 1024:t * 1024 + 1024],
                                              scalar=st_rstd[:, t:t + 1], in1=T("norm_post"), op0=ALU.mult,
                                              op1=ALU.mult))
                dve.tensor_tensor(xres[:, t, :], xres[:, t, :], ytmp[:, t % 2, :], ALU.add)\
                    .then_inc(sem("x1_ready"), 1)
            phase_end(dve)

            dve.wait_ge(sem("ctx_loaded"), 16)
            for t in range(6):
                row_mean(dve, link, "hs", t, ctxr[:, t, :] if t < 2 else xres[:, t - 2, :])
            stats_dve(dve, link, "hs", 6, True, LN_EPS)
            for t in range(6):
                src = ctxr[:, t, :] if t < 2 else xres[:, t - 2, :]
                dve.tensor_scalar(lnx[:, t, :], src, st_rstd[:, t:t + 1], st_nb[:, t:t + 1], ALU.mult, ALU.add)\
                    .then_inc(sem("h_normed"), 1)
            for k in range(KT):
                dve.wait_ge(sem("h_turned"), k + 1)
                A = 2 * (k % 3)
                dve.tensor_scalar(hT[:, k, 0:CTX], bank(A, 0, CTX), omsc[:, 8 + k:9 + k], mod[:, k, 1:2],
                                  ALU.mult, ALU.add)
                dve.tensor_scalar(hT[:, k, CTX:TOK2], bank(A + 1), omsc[:, k:k + 1], mod[:, k, 0:1],
                                  ALU.mult, ALU.add).then_inc(sem("hT_ready"), 1)
            phase_end(dve)

            dve.wait_ge(sem("slot_act"), emptied([n for n, j in enumerate(JOBS) if j[1:3] == ("gkv", 5)][0])[1])
            for t in range(4):
                link(dve.tensor_tensor(T("gsq"), gq[:, t, :], gq[:, t, :], ALU.mult))
                link(dve.tensor_reduce(gss[:, 8 * t:8 * t + 8], T("gsq").rearrange("p (h n) -> p h n", n=64), AX,
                                       ALU.add))
            sq = T("gsq", 0, 128)
            for t in range(6):
                link(dve.tensor_tensor(sq, gkv[:, t, 0:128], gkv[:, t, 0:128], ALU.mult))
                link(dve.tensor_reduce(gss[:, 32 + 2 * t:34 + 2 * t], sq.rearrange("p (h n) -> p h n", n=64), AX,
                                       ALU.add))
            dve.tensor_scalar(gss, gss, 1.0 / 64, EPS1, ALU.mult, ALU.add).then_inc(stage("gvar_ready"), 1)
            acos = C("acos").rearrange("p (t a n) -> p t a n", t=4, a=2)
            asin = C("asin").rearrange("p (t a n) -> p t a n", t=4, a=2)
            tmp_rope[0] = T("gtmp")
            def head_tile(t):
                k = gkv[:, t, 0:128].rearrange("p (h n) -> p h n", n=64)
                link(dve.tensor_tensor(k, k, bc(grs[:, 32 + 2 * t:34 + 2 * t], 64), ALU.mult))
                ins = dve.tensor_tensor(k, k, rep(T("gains", 64, 64), 2), ALU.mult)
                if t < 2:
                    ins.then_inc(sem("qk_roped"), 1)
                    return
                link(ins)
                kh = gkv[:, t, 0:128].rearrange("p (h a b n) -> p h a b n", h=2, a=2, b=2)
                c, s = rep2(acos[:, t - 2], 2), rep2(asin[:, t - 2], 2)
                link(rope(kh[:, :, :, 0, :], kh[:, :, :, 1, :], c, s, kh[:, :, :, 0, :], kh[:, :, :, 1, :],
                          (2, 2, 16)))
                q = gq[:, t - 2, :].rearrange("p (h n) -> p h n", n=64)
                link(dve.tensor_tensor(q, q, bc(grs[:, 8 * (t - 2):8 * (t - 2) + 8], 64), ALU.mult))
                link(dve.tensor_tensor(q, q, rep(T("gains", 0, 64), 8), ALU.mult))
                for gg in range(2):
                    qh = gq[:, t - 2, gg * 256:gg * 256 + 256].rearrange("p (h a b n) -> p h a b n", h=4, a=2, b=2)
                    o = qn(t - 2).rearrange("p (j g a b n) -> p j g a b n", j=4, g=2, a=2,
                                                      b=2)[:, :, gg]
                    c, s = rep2(acos[:, t - 2], 4), rep2(asin[:, t - 2], 4)
                    ins = rope(qh[:, :, :, 0, :], qh[:, :, :, 1, :], c, s, o[:, :, :, 0, :], o[:, :, :, 1, :],
                               (4, 2, 16))
                    if gg == 0:
                        link(ins)
                ins.then_inc(sem("qk_roped"), 1)
                dve.wait_ge(sem("qk_roped"), t + 1)

            for i in range(14):
                latent_only = i < 4 or i == 13
                lo = 258 if latent_only else 0
                dve.wait_ge(sem("raw_ready"), i + 1)
                dve.wait_ge(sem("nbr_ready"), i + 1)
                r, nb = raw[:, i % 2, :], nbr[:, i % 2, :]
                link(dve.scalar_tensor_tensor(out=nb[:, lo:770], in0=nb[:, lo:770], scalar=0.5,
                                              in1=r[:, lo + 1:771], op0=ALU.mult, op1=ALU.subtract))
                mu = T("vec", VEC["mu"][0] + i, 1)
                if i < 4:
                    dl, dc = rT[:, i, :], None
                elif i == 13:
                    dl, dc = gl[:, 0:512], None
                else:
                    dst = kT[:, i - 4, :] if i < 8 else vT[:, i - 8, :] if i < 12 else wal
                    dl, dc = dst[:, CTX:TOK2], dst[:, 0:CTX]
                if dc is not None:
                    dve.scalar_tensor_tensor(out=dc, in0=nb[:, 0:256], scalar=mu, in1=r[:, 1:257], op0=ALU.mult,
                                             op1=ALU.add)
                dve.scalar_tensor_tensor(out=dl, in0=nb[:, 258:770], scalar=mu, in1=r[:, 259:771], op0=ALU.mult,
                                         op1=ALU.add).then_inc(sem("shifted"), 1)
                if i == 1:
                    dve.wait_ge(*after("gstd_ready"))
                    link(dve.reciprocal(grs, gstd))
                    dve.wait_ge(sem("gains_loaded"), 16)
                if 2 <= i < 8:
                    head_tile(i - 2)
            phase_end(dve)
            att_dve(dve, link, "gqa", 64, GQA_SCALE, mixG, None)
            phase_end(dve)
            rwkv_dve(dve, link)
            phase_end(dve)

            dve.wait_ge(sem("x1_back"), 16)
            dve.wait_ge(sem("y2_done"), 2)
            dve.wait_ge(*after("gt1_ready"))
            for t in range(4):
                y = PS[:, t * 1024:t * 1024 + 1024]
                link(dve.tensor_tensor(T("ztmp"), y, T("grow"), ALU.mult))
                dve.scalar_tensor_tensor(out=x2[:, t, :], in0=x2[:, t, :], scalar=ALPHA, in1=T("ztmp"),
                                         op0=ALU.mult, op1=ALU.add).then_inc(sem("z1_made"), 1)
                dve.wait_ge(sem("z1_made"), t + 1)
                row_mean(dve, link, "z1", t, x2[:, t, :])
            affine_norm(dve, link, "z1", "ln1")
            phase_end(dve)

            for t in range(4):
                row_mean(dve, link, "f", t, x2[:, t, :])
            stats_dve(dve, link, "f", 4, True, LN_EPS)
            for t in range(4):
                dve.tensor_scalar(xn[:, t, :], x2[:, t, :], st_rstd[:, t:t + 1], st_nb[:, t:t + 1], ALU.mult,
                                  ALU.add).then_inc(sem("xn_ready"), 1)
            for k in range(KT):
                dve.wait_ge(sem("h2_turned"), k + 1)
                dve.tensor_scalar(h2T[:, k, :], bank(k % 6), omsc[:, 16 + k:17 + k], mod[:, 24 + k, 0:1], ALU.mult,
                                  ALU.add).then_inc(sem("h2T_ready"), 1)
            for t in range(4):
                dve.wait_ge(sem("xn_ready"), 4)
                dve.tensor_scalar(x2[:, t, :], x2[:, t, :], ALPHA, None, ALU.mult)
            dve.wait_ge(*after("logits_done"))
            lg = bank(7, 0, 64).rearrange("p (t e) -> p t e", e=EXP)
            link(dve.tensor_reduce(rmx, lg, AX, ALU.max))
            dve.tensor_tensor(aff, lg, bc(rmx, EXP), ALU.subtract).then_inc(stage("logits_in"), 1)
            dve.wait_ge(*after("aff_exp"))
            link(dve.tensor_reduce(rsm, aff, AX, ALU.add))
            link(dve.reciprocal(rri, rsm))
            dve.tensor_tensor(aff, aff, bc(rri, EXP), ALU.mult).then_inc(stage("aff_ready"), 1)
            dve.wait_ge(*after("aff_turned"))
            work = [T("affT", b * 512, 512, (0, EXP)) for b in range(4)]
            link(dve.tensor_copy(work[0], bank(0, 0, 512, (0, EXP))))
            for r in range(CAP // 8):
                a, b = work[r % 2], work[(r + 1) % 2]
                link(dve.max(m8[0:EXP, :], a))
                link(dve.match_replace(out=b, in_to_replace=m8[0:EXP, :], in_values=a, imm_value=-1.0))
            taken, count = work[2], work[3]
            link(dve.tensor_scalar(taken, work[0], 0.0, None, ALU.is_lt))
            link(dve.memset(work[1], 0.0))
            link(dve.tensor_tensor_scan(count, taken, work[1], 0.0, ALU.add, ALU.add))
            dve.tensor_tensor(work[1], count, taken, ALU.mult).then_inc(stage("rank_ready"), 1)
            dve.wait_ge(*after("rank_turned"))
            link(dve.tensor_copy(T("pos"), bank(1, 0, 64)))
            for t in range(4):
                h = hot[:, t, :].rearrange("p (e c) -> p e c", c=CAP)
                dve.tensor_tensor(h, bc(pos[:, t, :], CAP), rep(C("slot"), EXP), ALU.is_equal)
            phase_end(dve)
            for k in range(KT):
                if k % 2 == 0:
                    t = k // 2
                    h = hot[:, t, :].rearrange("p (e c) -> p e c", c=CAP)
                    if t >= 1:
                        dve.wait_ge(sem("hot_turned"), t)
                    dve.tensor_tensor(T("hotg").rearrange("p (e c) -> p e c", c=CAP), h, bc(aff[:, t, :], CAP),
                                      ALU.mult).then_inc(sem("hotg_ready"), 1)
                dve.wait_ge(sem("gathered"), 2 * k + 1)
                dve.tensor_scalar(xinT[:, k, 0:512], bank(2 * k % 6), omsc[:, 16 + k:17 + k], mod[:, 24 + k, 0:1],
                                  ALU.mult, ALU.add).then_inc(sem("gather_dve"), 1)
            phase_end(dve)

            def scatter_add(p2):
                for t in range(4):
                    for n in range(2):
                        i = p2 * 8 + t * 2 + n
                        dve.wait_ge(sem("scattered"), i + 1)
                        if i >= 8:
                            dve.wait_ge(sem("added"), i - 7)
                        dst = x2[:, t, n * 512:n * 512 + 512]
                        dve.tensor_tensor(dst, dst, bank(6 + i % 2), ALU.add).then_inc(sem("added"), 1)

            for e in range(EXP):
                for n in range(2):
                    dve.wait_ge(sem("silu_done"), 2 * e + n + 1)
                    if e >= 1:
                        dve.wait_ge(sem("hid_turned"), e)
                    dve.tensor_tensor(T("hid", n * 512, 512, (64, 128)), T("sg", n * 512, 512, (64, 128)),
                                      bank(2 * (e % 2) + n, 0, 512, (64, 128)), ALU.mult)\
                        .then_inc(sem("hid_ready"), 1)
                dve.wait_ge(sem("down_done"), e + 1)
                lo = (e % 2) * 64
                y = T("ypair", (e // 2 % 2) * D, D, (lo, lo + 64))
                if e >= 4:
                    dve.wait_ge(sem("scattered"), 8 * (e // 2 - 1))
                for n in range(2):
                    g2 = T("grow2", n * 512, 512, (lo, lo + 64))
                    ins = dve.tensor_tensor(y[:, n * 512:n * 512 + 512], bank(5, 0, 512, (n * 64, n * 64 + 64)), g2,
                                            ALU.mult)
                ins.then_inc(sem("y_left"), 1)
                if e % 2:
                    scatter_add(e // 2)
            phase_end(dve)
            for t in range(4):
                row_mean(dve, link, "o", t, x2[:, t, :])
            affine_norm(dve, link, "o", "ln2", "out_ready")

        @block.gpsimd
        def _(pool):
            phase_end(pool)
            pool.memset(T("fkT", 0, 8 * 528, (64, 128)), 0.0)
            pool.memset(T("fqT", 0, 8 * 512, (64, 128)), 0.0).then_inc(sem("fox_padded"), 1)
            pool.wait_ge(sem("fox_padded"), 1)
            pool.memset(T("fqT", 0, 8 * 512, (64, 65)), 1.0)
            pool.wait_ge(sem("cum_ready"), 1)
            pool.dma_start(fkT[64:65, :, :], T("cum", 0, 528, (0, 8))).then_inc(sem("cum_moved"), 16)
            pool.wait_ge(sem("cum_moved"), 16)
            phase_end(pool)
            phase_end(pool)
            pool.memset(T("mqT", 0, 8 * 512, (QK, P)), 0.0)
            pool.memset(T("mkT", 0, 8 * 528, (QK, P)), 0.0)
            phase_end(pool)
            phase_end(pool)
            pool.dma_start(T("xres").rearrange("p (t d) -> p t d", d=D), w["x"][0].rearrange("(t p) d -> p t d", p=P))\
                .then_inc(sem("xres_loaded"), 16)
            pool.dma_start(T("norm_post"), w["norm_post"].broadcast_to([P, D])).then_inc(sem("npost_loaded"), 16)
            pool.wait_ge(sem("xres_loaded"), 16)
            pool.wait_ge(sem("npost_loaded"), 16)
            pool.dma_start(ctxr, w["ctx_2"][0].rearrange("(t p) d -> p t d", p=P)).then_inc(sem("ctx_loaded"), 16)
            pool.wait_ge(sem("ctx_loaded"), 16)
            phase_end(pool)
            phase_end(pool)
            pool.dma_start(T("gains"), w["gains"].broadcast_to([P, 128])).then_inc(sem("gains_loaded"), 16)
            pool.memset(T("gqT"), 0.0)
            pool.memset(T("raw"), 0.0).then_inc(sem("raw_clear"), 1)
            for i in range(14):
                lo = 258 if (i < 4 or i == 13) else 0
                pool.wait_ge(sem("raw_ready"), i + 1)
                if i >= 2:
                    pool.wait_ge(sem("shifted"), i - 1)
                r = raw[:, i % 2, :]
                pool.tensor_tensor(nbr[:, i % 2, lo:770], r[:, lo:770], r[:, lo + 2:772], ALU.add)\
                    .then_inc(sem("nbr_ready"), 1)
            pool.wait_ge(sem("gains_loaded"), 16)
            phase_end(pool)
            phase_end(pool)
            pool.dma_start(lora[0:64], w["decay_up_2"][0].rearrange("d k n -> k d n")).then_inc(sem("lora_loaded"), 16)
            pool.dma_start(lora[64:128], w["iclr_up_2"][0].rearrange("d k n -> k d n")).then_inc(sem("lora_loaded"), 16)
            pool.dma_start(T("gateup"), w["gate_up_2"][0]).then_inc(sem("gate_loaded"), 16)
            ka = T("vec", VEC["k_a"][0], 4)

            def factors(g):
                pool.wait_ge(sem("tanh_done"), g + 1)
                pool.tensor_scalar(W["a"], W["a"], 0.5, 0.5, ALU.mult, ALU.add).then_inc(sem("pool_chain"), 1)
                pool.wait_ge(sem("pool_chain"), 4 * g + 1)
                if g:
                    pool.wait_ge(sem("an_done"), 2 * g)
                    pool.wait_ge(sem("blocks_ready"), g)
                if g == 0:
                    pool.wait_ge(sem("kk_ready"), 4)
                for d in range(2):
                    tok = step_tok(g, d)
                    pool.tensor_tensor(by("bt_s", d), kkT[:, :, tok:tok + 64], by("a", d), ALU.mult)
                pool.tensor_scalar(W["kd"], W["a"], 1.0, None, ALU.subtract).then_inc(sem("pool_chain"), 1)
                pool.wait_ge(sem("pool_chain"), 4 * g + 2)
                for d in range(2):
                    ins = pool.tensor_tensor(by("kd", d), by("kd", d), bc(ka, 64), ALU.mult)
                ins.then_inc(sem("pool_chain"), 1)
                pool.wait_ge(sem("pool_chain"), 4 * g + 3)
                pool.tensor_scalar(W["kd"], W["kd"], 1.0, None, ALU.add).then_inc(sem("pool_chain"), 1)
                pool.wait_ge(sem("pool_chain"), 4 * g + 4)
                for d in range(2):
                    tok = step_tok(g, d)
                    ins = pool.tensor_tensor(by("kd", d), by("kd", d), kT[:, :, tok:tok + 64], ALU.mult)
                ins.then_inc(sem("kd_ready"), 1)
                pool.wait_ge(sem("kd_ready"), g + 1)
                pool.wait_ge(sem("e_ready"), g + 1)
                pool.tensor_tensor(W["bt_s"], W["bt_s"], W["Ev"], ALU.mult)
                pool.tensor_tensor(W["kd"], W["kd"], W["Ev"], ALU.mult).then_inc(sem("eb_ready"), 1)
                for d in range(2):
                    ins = pool.tensor_copy(wcs[g % 2][:, 4 * d:4 * d + 4], by("Ei", d)[:, :, 63 if d == 0 else 0])
                ins.then_inc(sem("wc_ready"), 1)

            pool.memset(T("yacc"), 0.0)
            pool.memset(W["S"], 0.0)
            for i, n in enumerate(BLOCKS + ("Z",)):
                ins = pool.memset(W[n], 0.0)
            ins.then_inc(sem("blocks_clear"), 1)
            factors(0)
            for g in range(12):
                for d in range(2):
                    pool.wait_ge(sem("x0_ready"), 2 * g + d + 1)
                    pool.tensor_tensor(blocks("X", d), blocks("X", d), rep(ident, 4), ALU.add)
                    pool.tensor_tensor(blocks("XT", d), blocks("XT", d), rep(ident, 4), ALU.add)\
                        .then_inc(sem("x_started"), 1)
                if g < 11:
                    factors(g + 1)
            pool.wait_ge(sem("lora_loaded"), 32)
            pool.wait_ge(sem("gate_loaded"), 16)
            phase_end(pool)
            phase_end(pool)
            phase_end(pool)
            phase_end(pool)
            phase_end(pool)


def constants():
    import numpy as np
    c = {n: np.zeros((P, wd), np.float32) for n, (_, wd) in CONST.items()}
    p = np.arange(P)[:, None]
    n128, n64 = np.arange(P)[None, :], np.arange(64)[None, :]
    c["ident"][:] = p == n128
    c["causal"][:] = np.where(n128 > p, NEG, 0)
    c["chunkmask"][:] = np.where(n128 // CH > p // CH, NEG, 0)
    inv = (np.float32(10000.0) ** (-np.arange(0, ROPE, 2, dtype=np.float32) / np.float32(ROPE))).astype(np.float32)
    for t in range(5):
        posn = (np.arange(P) + (META + t * P if t < 4 else 0)).astype(np.float32)
        ang = (posn[:, None] * inv[None, :]).astype(np.float32)
        c["mcos"][:, t * 16:t * 16 + 16] = np.cos(ang)
        c["msin"][:, t * 16:t * 16 + 16] = np.sin(ang)
    inv = (np.float32(10000.0) ** (-np.arange(16, dtype=np.float32) / np.float32(16))).astype(np.float32)
    for t in range(4):
        posn = np.arange(P) + t * P
        for a, q in enumerate((posn // 64, posn % 64)):
            ang = (q.astype(np.float32)[:, None] * inv[None, :]).astype(np.float32)
            c["acos"][:, t * 32 + a * 16:t * 32 + a * 16 + 16] = np.cos(ang)
            c["asin"][:, t * 32 + a * 16:t * 32 + a * 16 + 16] = np.sin(ang)
    s = p % 64
    for d in range(2):
        lo, o = slice(d * 64, d * 64 + 64), n64
        before = (s < o) if d == 0 else (s > o)
        c["strict"][:, lo] = before
        c["incl"][:, lo] = before | (s == o)
        c["pair0"][:, lo] = (s // 2 == o // 2) & ((s > o) if d == 0 else (s < o))
        for lv in range(6):
            b = 2 ** lv
            lvl = slice(lv * 128 + d * 64, lv * 128 + d * 64 + 64)
            block = (s // (2 * b) == o // (2 * b)) & (s // b != o // b)
            c["levelT"][:, lvl] = block & ((s > o) if d == 0 else (s < o))
            if lv == 0:
                c["level"][:, lvl] = block & before
        seg = np.ones((4, 64))
        seg[:, 0 if d == 0 else 63] = 0
        c["seg"][:, d * 256:d * 256 + 256] = seg.reshape(1, 256)
    c["ident2"][:] = s == n64
    for j in range(4):
        for q in range(2):
            c["headsum"][q * 64:q * 64 + 64, j * 8 + 2 * j + q] = 1
            c["headspread"][2 * j + q, j * P + q * 64:j * P + q * 64 + 64] = 1
    c["slot"][:] = n64 + 1
    c["groupsum"][:] = p % 32 == np.arange(2)[None, :]
    c["blockones"][:] = p // 64 == n128 // 64
    return np.concatenate([c[n] for n in CONST], 1)


def vectors(a):
    import numpy as np

    def cols(x, n):
        return np.asarray(x).reshape(n, P).T
    out = np.zeros((P, NVEC), np.float32)

    def put(name, x):
        lo, n = VEC[name]
        out[0:x.shape[0], lo:lo + n] = x
    put("norm_pre", cols(a["norm_pre"][0], 8))
    put("q_norm", cols(a["q_norm"][0], 2))
    put("kv_norm", cols(a["kv_norm"][0], 1))
    put("b_f", np.asarray(a["b_f"])[0][:, None])
    put("cvec", np.stack([cols(a["c_2"][0], 8), cols(a["c_ctx_2"], 8)], 2).reshape(P, 16))
    put("b_ada", cols(a["b_ada_2"][0], 48))
    put("mu", cols(a["tshift_mu_2"][0], 14))
    put("w0", cols(a["decay_w0_2"][0], 8))
    put("a0", cols(a["iclr_a0_2"][0], 8))
    for n in ("k_k", "k_a", "r_k", "lnx_g", "lnx_b"):
        put(n, cols(a[n + "_2"][0], 4))
    return out


_WHOLE = ("x", "meta", "w_in", "w_uq", "w_ukv", "w_out", "ctx_2", "w_ada_2", "w_in_2", "decay_up_2", "iclr_up_2",
          "gate_up_2", "w_out_2", "router_w_2", "exp_w_gate_2", "exp_w_up_2", "exp_w_down_2", "norm_post")


def kernel(**inputs):
    import numpy as np
    import concourse.bacc as bacc
    from concourse.bass_utils import run_bass_kernel_spmd

    nc = bacc.Bacc("TRN2", target_bir_lowering=False, num_devices=1)
    arrays = {n: np.ascontiguousarray(inputs[n]) for n in _WHOLE}
    arrays["consts"] = constants()
    arrays["vecs"] = vectors(inputs)
    arrays["ln1"] = np.concatenate([inputs["ln1_g_2"], inputs["ln1_b_2"]], 1)
    arrays["ln2"] = np.concatenate([inputs["ln2_g_2"], inputs["ln2_b_2"]], 1)
    arrays["gains"] = np.concatenate([inputs["q_gain_2"], inputs["k_gain_2"]], 1)
    w = {n: nc.dram_tensor(n, a.shape, mybir.dt.from_np(a.dtype), kind="ExternalInput").ap()
         for n, a in arrays.items()}
    out = nc.dram_tensor("out", (1, SEQ, D), F32, kind="ExternalOutput").ap()
    program(nc, w, out)
    r = run_bass_kernel_spmd(nc, [arrays], core_ids=[0])
    return r.results[0]["out"]
```
